# Optimizing a Trainium2 kernel written in Bass

```python
import jax
import jax.numpy as jnp
from jax import lax
import numpy as np

D_MODEL = 1024
BATCH = 1
SEQ = 512
DEPTH = 2
DEC_BATCH = 8
DEC_SEQ = 8
PAST_LEN = 1024
PAGE_SIZE = 128

N_A_LAYERS = DEPTH // 2
N_B_LAYERS = DEPTH - N_A_LAYERS
RET_HEADS = 4
RET_DK = D_MODEL // RET_HEADS
RET_DV = 2 * D_MODEL // RET_HEADS
RET_CHUNK = 128
NSA_HEADS = 16
NSA_GROUPS = 4
HEADS_PER_GROUP = NSA_HEADS // NSA_GROUPS
HEAD_DIM = D_MODEL // NSA_HEADS
CMP_BLOCK = 32
CMP_STRIDE = 16
CMP_HIDDEN = HEAD_DIM
SEL_BLOCK = 64
N_SELECT = 16
N_LOCAL = 2
WINDOW = 512
Q_BLOCK = 64
D_FF = 2816
ROPE_THETA = 10000.0
EPS = 1e-6
NEG = -1e30
BIG = 1e9
N_ROWS = 4

kernel_name = 'yoco_retnet_nsa_macaron_step'

def rmsnorm(x, g):
    x32 = x.astype(jnp.float32)
    y = x32 * lax.rsqrt(jnp.mean(x32 * x32, axis=-1, keepdims=True) + EPS)
    return (y * g.astype(jnp.float32)).astype(x.dtype)

def rope(x, pos):
    half = x.shape[-1] // 2
    inv = ROPE_THETA ** (-jnp.arange(half, dtype=jnp.float32) / half)
    ang = pos.astype(jnp.float32)[:, None] * inv[None, :]
    cos = jnp.cos(ang)[:, None, :]
    sin = jnp.sin(ang)[:, None, :]
    x32 = x.astype(jnp.float32)
    x1, x2 = x32[..., :half], x32[..., half:]
    return jnp.concatenate([x1 * cos - x2 * sin, x1 * sin + x2 * cos], axis=-1).astype(x.dtype)

def swiglu(xn, w_in, w_out):
    a, b = jnp.split(xn @ w_in, 2, axis=-1)
    return (jax.nn.silu(a) * b) @ w_out

def retention_log_decay():
    return jnp.log(1.0 - 2.0 ** (-5.0 - jnp.arange(RET_HEADS, dtype=jnp.float32)))

def retention_chunk(q, k, v, s):
    f32 = jnp.float32
    c = q.shape[1]
    lg = retention_log_decay()
    idx = jnp.arange(c, dtype=f32)
    rel = idx[:, None] - idx[None, :]
    decay = jnp.where(rel >= 0, jnp.exp(jnp.maximum(rel, 0.0)[None] * lg[:, None, None]), 0.0)
    scores = jnp.einsum('bihd,bjhd->bhij', q, k, preferred_element_type=f32) * decay
    intra = jnp.einsum('bhij,bjhv->bihv', scores, v.astype(f32))
    q_dec = jnp.exp((idx + 1.0)[:, None] * lg[None, :])
    cross = jnp.einsum('bihd,bhdv->bihv', q.astype(f32) * q_dec[None, :, :, None], s)
    k_dec = jnp.exp((c - 1.0 - idx)[:, None] * lg[None, :])
    s_new = jnp.exp(c * lg)[None, :, None, None] * s + jnp.einsum(
        'bjhd,bjhv->bhdv', k.astype(f32) * k_dec[None, :, :, None], v.astype(f32))
    return intra + cross, s_new

def retention(xn, w_in, w_out, s0, pos):
    b, t, _ = xn.shape
    q, k, v, g = jnp.split(xn @ w_in, [D_MODEL, 2 * D_MODEL, 4 * D_MODEL], axis=-1)
    q = rope(q.reshape(b, t, RET_HEADS, RET_DK), pos)
    k = rope(k.reshape(b, t, RET_HEADS, RET_DK), pos) * (RET_DK ** -0.5)
    v = v.reshape(b, t, RET_HEADS, RET_DV)
    chunk = RET_CHUNK if t % RET_CHUNK == 0 else t
    n = t // chunk

    def to_chunks(a):
        return a.reshape(b, n, chunk, *a.shape[2:]).swapaxes(0, 1)

    def step(s, qkv):
        o, s_next = retention_chunk(qkv[0], qkv[1], qkv[2], s)
        return s_next, o

    s_fin, o = lax.scan(step, s0.astype(jnp.float32), (to_chunks(q), to_chunks(k), to_chunks(v)))
    o = o.swapaxes(0, 1).reshape(b, t, RET_HEADS, RET_DV)
    mu = jnp.mean(o, axis=-1, keepdims=True)
    var = jnp.mean(jnp.square(o - mu), axis=-1, keepdims=True)
    o = ((o - mu) * lax.rsqrt(var + EPS)).reshape(b, t, 2 * D_MODEL).astype(xn.dtype)
    return (jax.nn.silu(g) * o) @ w_out, s_fin

def shared_kv_rows(h, kv_norm, kv_w, k_norm, pos):
    b, t, _ = h.shape
    kv = (rmsnorm(h, kv_norm) @ kv_w).reshape(b, t, 6, NSA_GROUPS, HEAD_DIM)
    k_slc = rope(rmsnorm(kv[:, :, 2], k_norm[1]), pos)
    k_win = rope(rmsnorm(kv[:, :, 4], k_norm[2]), pos)
    rows = jnp.stack([kv[:, :, 0], kv[:, :, 1], k_slc, kv[:, :, 3]], axis=2)
    win = jnp.stack([k_win, kv[:, :, 5]], axis=2)
    return rows, win

def compress_blocks(tok, w1, b1, w2, pe):
    b, l = tok.shape[:2]
    nc = (l - CMP_BLOCK) // CMP_STRIDE + 1
    r = CMP_BLOCK // CMP_STRIDE
    nchunk = nc + r - 1
    chunks = tok[:, :nchunk * CMP_STRIDE].reshape(b, nchunk, CMP_STRIDE, NSA_GROUPS, HEAD_DIM)
    chunks = chunks.transpose(0, 1, 3, 2, 4).reshape(b, nchunk, NSA_GROUPS, CMP_STRIDE * HEAD_DIM)
    w1r = w1.reshape(r, CMP_STRIDE * HEAD_DIM, CMP_HIDDEN)
    h = b1 + pe.reshape(-1) @ w1
    for j in range(r):
        h = h + chunks[:, j:j + nc] @ w1r[j]
    return jax.nn.gelu(h) @ w2

def build_context(rows, k_norm, cmp_w1, cmp_b1, cmp_w2, cmp_pe):
    b, l = rows.shape[:2]
    k_c = compress_blocks(rows[:, :, 0], cmp_w1[0], cmp_b1[0], cmp_w2[0], cmp_pe[0])
    v_c = compress_blocks(rows[:, :, 1], cmp_w1[1], cmp_b1[1], cmp_w2[1], cmp_pe[1])
    nc = k_c.shape[1]
    c_end = jnp.arange(nc, dtype=jnp.int32) * CMP_STRIDE + (CMP_BLOCK - 1)
    k_c = rope(rmsnorm(k_c, k_norm[0]), c_end)
    ns = -(-l // SEL_BLOCK)
    sel = jnp.pad(rows[:, :, 2:4], ((0, 0), (0, ns * SEL_BLOCK - l), (0, 0), (0, 0), (0, 0)))
    sel = sel.reshape(b, ns, SEL_BLOCK, 2, NSA_GROUPS, HEAD_DIM).transpose(3, 0, 4, 1, 2, 5)
    ci = np.arange(nc)[:, None]
    sj = np.arange(ns)[None, :]
    overlap = (ci * CMP_STRIDE < (sj + 1) * SEL_BLOCK) & (ci * CMP_STRIDE + CMP_BLOCK > sj * SEL_BLOCK)
    return (k_c, v_c, c_end, jnp.asarray(overlap, jnp.float32), sel[0], sel[1])

def nsa_attend(q, gates, qpos, ctx, k_w, v_w, kpos_w):
    k_c, v_c, c_end, overlap, k_blk, v_blk = ctx
    f32 = jnp.float32
    b, nq = q.shape[:2]
    scale = HEAD_DIM ** -0.5
    qg = q.reshape(b, nq, NSA_GROUPS, HEADS_PER_GROUP, HEAD_DIM)
    s_c = jnp.einsum('bqghd,bcgd->bqghc', qg, k_c, preferred_element_type=f32) * scale
    valid_c = (c_end[None, :] <= qpos[:, None])[None, :, None, None, :]
    p_c = jax.nn.softmax(jnp.where(valid_c, s_c, NEG), axis=-1) * valid_c
    o_c = jnp.einsum('bqghc,bcgd->bqghd', p_c, v_c.astype(f32))
    ns = k_blk.shape[2]
    imp = jnp.einsum('bqghc,cs->bqgs', p_c, overlap)
    q_blk = (qpos // SEL_BLOCK)[:, None]
    s_idx = jnp.arange(ns)[None, :]
    valid_s = s_idx <= q_blk
    forced = (s_idx == 0) | (valid_s & (q_blk - s_idx < N_LOCAL))
    score = jnp.where(forced[None, :, None, :], BIG, jnp.where(valid_s[None, :, None, :], imp, NEG))
    _, idx = lax.top_k(score, min(N_SELECT, ns))
    idx = idx.transpose(0, 2, 1, 3)
    nsel = idx.shape[-1]
    take = jax.vmap(jax.vmap(lambda blocks, ii: blocks[ii]))
    k_s = take(k_blk, idx)
    v_s = take(v_blk, idx)
    kpos_s = idx[..., None] * SEL_BLOCK + jnp.arange(SEL_BLOCK)
    valid_k = (kpos_s <= qpos[None, None, :, None, None]).transpose(0, 2, 1, 3, 4)
    valid_k = valid_k.reshape(b, nq, NSA_GROUPS, 1, nsel * SEL_BLOCK)
    s_s = jnp.einsum('bqghd,bgqskd->bqghsk', qg, k_s, preferred_element_type=f32)
    s_s = s_s.reshape(b, nq, NSA_GROUPS, HEADS_PER_GROUP, nsel * SEL_BLOCK) * scale
    p_s = jax.nn.softmax(jnp.where(valid_k, s_s, NEG), axis=-1)
    o_s = jnp.einsum('bqghn,bgqnd->bqghd', p_s,
                     v_s.reshape(b, NSA_GROUPS, nq, nsel * SEL_BLOCK, HEAD_DIM).astype(f32))
    s_w = jnp.einsum('bqghd,bkgd->bqghk', qg, k_w, preferred_element_type=f32) * scale
    valid_w = ((kpos_w[None, :] <= qpos[:, None]) & (kpos_w[None, :] > qpos[:, None] - WINDOW)
               & (kpos_w[None, :] >= 0))[None, :, None, None, :]
    p_w = jax.nn.softmax(jnp.where(valid_w, s_w, NEG), axis=-1)
    o_w = jnp.einsum('bqghk,bkgd->bqghd', p_w, v_w.astype(f32))
    g = gates.reshape(b, nq, NSA_GROUPS, HEADS_PER_GROUP, 3)
    o = g[..., 0:1] * o_c + g[..., 1:2] * o_s + g[..., 2:3] * o_w
    return o.reshape(b, nq, NSA_HEADS * HEAD_DIM)

def nsa_mixer(xn, w_in, q_gain, w_out, pos, ctx, win_kv, win_pos, banded):
    b, t, _ = xn.shape
    proj = xn @ w_in
    q = rope(rmsnorm(proj[..., :NSA_HEADS * HEAD_DIM].reshape(b, t, NSA_HEADS, HEAD_DIM), q_gain), pos)
    gates = jax.nn.sigmoid(proj[..., NSA_HEADS * HEAD_DIM:].astype(jnp.float32))
    if banded:
        span = WINDOW + Q_BLOCK

        def block(i):
            start = i * Q_BLOCK
            kv = lax.dynamic_slice_in_dim(win_kv, start, span, axis=1)
            return nsa_attend(lax.dynamic_slice_in_dim(q, start, Q_BLOCK, axis=1),
                              lax.dynamic_slice_in_dim(gates, start, Q_BLOCK, axis=1),
                              start + jnp.arange(Q_BLOCK, dtype=jnp.int32), ctx,
                              kv[:, :, 0], kv[:, :, 1],
                              start - WINDOW + jnp.arange(span, dtype=jnp.int32))

        o = lax.map(block, jnp.arange(t // Q_BLOCK, dtype=jnp.int32))
        o = o.swapaxes(0, 1).reshape(b, t, NSA_HEADS * HEAD_DIM)
    else:
        o = nsa_attend(q, gates, pos, ctx, win_kv[:, :, 0], win_kv[:, :, 1], win_pos)
    return o.astype(xn.dtype) @ w_out

def trunk(x, pos, ret_s0, past_rows, past_win, w):
    (ffn_norm, ffn_w_in, ffn_w_out, ret_norm, ret_w_in, ret_w_out, kv_norm, kv_w, k_norm,
     cmp_w1, cmp_b1, cmp_w2, cmp_pe, nsa_norm, nsa_w_in, q_norm, nsa_w_out) = w
    t = x.shape[1]
    prompt = past_rows is None
    ret_states = []
    rows = win = ctx = win_kv = win_pos = None
    for layer in range(DEPTH):
        if layer == N_A_LAYERS:
            rows, win = shared_kv_rows(x, kv_norm, kv_w, k_norm, pos)
            if prompt:
                all_rows = rows
                win_kv = jnp.pad(win, ((0, 0), (WINDOW, 0), (0, 0), (0, 0), (0, 0)))
            else:
                all_rows = jnp.concatenate([past_rows.astype(rows.dtype), rows], axis=1)
                win_kv = jnp.concatenate([past_win.astype(win.dtype), win], axis=1)
                win_pos = pos[0] - past_win.shape[1] + jnp.arange(win_kv.shape[1], dtype=jnp.int32)
            ctx = build_context(all_rows, k_norm, cmp_w1, cmp_b1, cmp_w2, cmp_pe)
        x = x + 0.5 * swiglu(rmsnorm(x, ffn_norm[layer, 0]), ffn_w_in[layer, 0], ffn_w_out[layer, 0])
        if layer < N_A_LAYERS:
            mix, s = retention(rmsnorm(x, ret_norm[layer]), ret_w_in[layer], ret_w_out[layer], ret_s0[layer], pos)
            ret_states.append(s)
        else:
            j = layer - N_A_LAYERS
            mix = nsa_mixer(rmsnorm(x, nsa_norm[j]), nsa_w_in[j], q_norm[j], nsa_w_out[j],
                            pos, ctx, win_kv, win_pos, prompt)
        x = x + mix
        x = x + 0.5 * swiglu(rmsnorm(x, ffn_norm[layer, 1]), ffn_w_in[layer, 1], ffn_w_out[layer, 1])
    new_win = win[:, -min(WINDOW, t):] if prompt else win_kv[:, -past_win.shape[1]:]
    return x, jnp.stack(ret_states), rows, new_win

def setup_inputs(seed: int = 0) -> dict:
    key = jax.random.key(seed)
    ks = jax.random.split(key, 24)
    f32 = jnp.float32
    n_pages = PAST_LEN // PAGE_SIZE
    n_phys = (DEC_BATCH * n_pages * 5) // 4
    win_buf = min(WINDOW, PAST_LEN)

    def dense(k, shape, fan_in):
        return jax.random.normal(k, shape, f32) * fan_in ** -0.5

    def gain(k, shape):
        return 1.0 + 0.02 * jax.random.normal(k, shape, f32)

    page_table = jax.random.permutation(ks[5], n_phys)[:DEC_BATCH * n_pages]
    page_table = page_table.reshape(DEC_BATCH, n_pages).astype(jnp.int32)
    return {
        'x_prompt': jax.random.normal(ks[0], (BATCH, SEQ, D_MODEL), f32),
        'x_sample': jax.random.normal(ks[1], (DEC_BATCH, DEC_SEQ, D_MODEL), f32),
        'state_ret': jax.random.normal(ks[2], (N_A_LAYERS, DEC_BATCH, RET_HEADS, RET_DK, RET_DV), f32),
        'cache_kv': jax.random.normal(ks[3], (n_phys, PAGE_SIZE, N_ROWS, NSA_GROUPS, HEAD_DIM), f32),
        'cache_win': jax.random.normal(ks[4], (DEC_BATCH, win_buf, 2, NSA_GROUPS, HEAD_DIM), f32),
        'page_table': page_table,
        'ffn_norm': gain(ks[6], (DEPTH, 2, D_MODEL)),
        'ffn_w_in': dense(ks[7], (DEPTH, 2, D_MODEL, 2 * D_FF), D_MODEL),
        'ffn_w_out': dense(ks[8], (DEPTH, 2, D_FF, D_MODEL), D_FF),
        'ret_norm': gain(ks[9], (N_A_LAYERS, D_MODEL)),
        'ret_w_in': dense(ks[10], (N_A_LAYERS, D_MODEL, 6 * D_MODEL), D_MODEL),
        'ret_w_out': dense(ks[11], (N_A_LAYERS, 2 * D_MODEL, D_MODEL), 2 * D_MODEL),
        'kv_norm': gain(ks[12], (D_MODEL,)),
        'kv_w': dense(ks[13], (D_MODEL, 6 * NSA_GROUPS * HEAD_DIM), D_MODEL),
        'k_norm': gain(ks[14], (3, HEAD_DIM)),
        'cmp_w1': dense(ks[15], (2, CMP_BLOCK * HEAD_DIM, CMP_HIDDEN), CMP_BLOCK * HEAD_DIM),
        'cmp_b1': 0.02 * jax.random.normal(ks[16], (2, CMP_HIDDEN), f32),
        'cmp_w2': dense(ks[17], (2, CMP_HIDDEN, HEAD_DIM), CMP_HIDDEN),
        'cmp_pe': 0.1 * jax.random.normal(ks[18], (2, CMP_BLOCK, HEAD_DIM), f32),
        'nsa_norm': gain(ks[19], (N_B_LAYERS, D_MODEL)),
        'nsa_w_in': dense(ks[20], (N_B_LAYERS, D_MODEL, NSA_HEADS * HEAD_DIM + 3 * NSA_HEADS), D_MODEL),
        'q_norm': gain(ks[21], (N_B_LAYERS, HEAD_DIM)),
        'nsa_w_out': dense(ks[22], (N_B_LAYERS, NSA_HEADS * HEAD_DIM, D_MODEL), NSA_HEADS * HEAD_DIM),
    }

def reference(x_prompt, x_sample, state_ret, cache_kv, cache_win, page_table,
              ffn_norm, ffn_w_in, ffn_w_out, ret_norm, ret_w_in, ret_w_out,
              kv_norm, kv_w, k_norm, cmp_w1, cmp_b1, cmp_w2, cmp_pe,
              nsa_norm, nsa_w_in, q_norm, nsa_w_out):
    w = (ffn_norm, ffn_w_in, ffn_w_out, ret_norm, ret_w_in, ret_w_out, kv_norm, kv_w, k_norm,
         cmp_w1, cmp_b1, cmp_w2, cmp_pe, nsa_norm, nsa_w_in, q_norm, nsa_w_out)
    b, t, _ = x_prompt.shape
    db, dq, _ = x_sample.shape
    past_len = page_table.shape[1] * cache_kv.shape[1]
    pos_p = jnp.arange(t, dtype=jnp.int32)
    pos_s = past_len + jnp.arange(dq, dtype=jnp.int32)
    s0_p = jnp.zeros((N_A_LAYERS, b, RET_HEADS, RET_DK, RET_DV), jnp.float32)
    y_prompt, ret_p, rows_p, win_p = trunk(x_prompt, pos_p, s0_p, None, None, w)
    past_rows = cache_kv[page_table].reshape(db, past_len, *cache_kv.shape[2:])
    y_sample, ret_s, rows_s, win_s = trunk(x_sample, pos_s, state_ret, past_rows, cache_win, w)
    return (y_prompt, y_sample, ret_p.astype(state_ret.dtype), ret_s.astype(state_ret.dtype),
            rows_p, rows_s, win_p, win_s)


_drawn_inputs = setup_inputs


def setup_inputs(seed=0):
    import zlib

    import numpy as np

    out = dict(_drawn_inputs(seed))
    spreads = {}
    factors = {'ffn_norm': 3.332,
     'kv_norm': 2.875,
     'k_norm': 4.274,
     'cmp_b1': 8.0,
     'nsa_norm': 8.0,
     'q_norm': 8.0}
    for name, (base, spread) in spreads.items():
        noise = np.random.default_rng([zlib.crc32(name.encode()), seed]).standard_normal(out[name].shape)
        drawn = base * np.exp(spread * noise) if base else spread * noise
        out[name] = jnp.asarray(drawn.astype(out[name].dtype))
    for name, factor in factors.items():
        out[name] = (out[name] * factor).astype(out[name].dtype)
    return out
```

```python
from contextlib import ExitStack

import numpy as np

import concourse.bass as bass
from concourse import mybir

ALU = mybir.AluOpType
ACT = mybir.ActivationFunctionType
AX_X = mybir.AxisListType.X
F32 = mybir.dt.float32
F32R = mybir.dt.float32r
I32 = mybir.dt.int32
ds = bass.ds

P = 128
D = 1024
KT = D // P
PT, SB, SQ = 512, 8, 8
ST = SB * SQ
NT = PT + ST
HALF = NT // 2
FF = 2816
FT = FF // P
FH = FT // 2
RH, DK, DV = 4, 256, 512
CH = 128
NCH = PT // CH
DH, G, HG = 64, 4, 4
PAST, PAGE, NPHYS = 1024, 128, 80
NPG = PAST // PAGE
SEL = 64
NSEL = PAST // SEL
NC_P, NC_S = 31, 63
WIN = 512
EPS = 1e-6
NEG = -1e30
SCALE = DH ** -0.5

UA = KT * P
UB = FH * P

FFN_UNITS, FFN_USES = 2 * (2 * FH + KT), 2 * (FH + KT // 2)
RU, RU0, RU1 = 16, 9, 8
STAGES = ["ffn0", "ret", "ffn1", "kv", "ffn2", "nsa", "ffn3"]
UNITS = {"ret": RH * RU, "kv": 12, "nsa": 18}
USES = {"ret": (RH * RU0, RH * RU1), "kv": (5, 4), "nsa": (8, 8)}


def running(count):
    at, out = 0, {}
    for s in STAGES:
        out[s] = at
        at += count(s)
    return out, at


U0, _ = running(lambda s: UNITS.get(s, FFN_UNITS))
F0, F0_END = running(lambda s: USES.get(s, (FFN_USES,) * 2)[0])
F1, F1_END = running(lambda s: USES.get(s, (FFN_USES,) * 2)[1])

G_FFN, G_RET, G_KV, G_NSA, G_K, G_Q, G_B1, N_GAIN = 0, 32, 40, 48, 56, 59, 60, 62


class Chain:

    def __init__(self, eng, sem):
        self.eng, self.sem, self.base, self.n = eng, sem, 0, 0

    def step(self, ins):
        ins.then_inc(self.sem, 1)
        self.n += 1

    def wait(self):
        self.eng.wait_ge(self.sem, self.base + self.n)

    def link(self, ins):
        self.step(ins)
        self.wait()

    def loop(self, count, per, body):
        outer_base, outer_n = self.base, self.n
        with self.eng.Fori(0, count) as i:
            self.base, self.n = outer_base + outer_n + i * per, 0
            body(i)
            assert self.n == per, f"a turn of this loop takes {self.n} steps, not {per}"
        self.base, self.n = outer_base, outer_n + count * per


def trunk_program(nc, a, o):
    with ExitStack() as ctx:
        def sb(stack, name, shape, dt=F32):
            return stack.enter_context(nc.sbuf_tensor(name, shape, dt))

        def sem(name):
            return ctx.enter_context(nc.semaphore(name))

        x = sb(ctx, "x", [P, KT, NT])
        wf = sb(ctx, "w_staged", [P, 2, UB])
        wh = sb(ctx, "w_high", [P, 2, UB], F32R)
        wl = sb(ctx, "w_low", [P, 2, UB], F32R)
        gain = sb(ctx, "gain", [P, N_GAIN])
        mats = sb(ctx, "mats", [P, 4, P])
        ones_v, rot, ident, same = (mats[:, i, :] for i in range(4))
        mcol = sb(ctx, "mean_columns", [P, 4])
        causal = sb(ctx, "causal", [P, P])
        sq = sb(ctx, "squares", [P, 2, NT])
        r = sb(ctx, "rstd", [P, NT])
        xf = sb(ctx, "x_normed", [P, 2, NT])
        st = sb(ctx, "token_stats", [P, 5, 2])
        pgt = sb(ctx, "page_table", [1, SB * NPG], I32)
        rb = sb(ctx, "stats_broadcast", [P, 5, P])

        with ExitStack() as s:
            xh_r, xl_r = sb(s, "xh_r", [P, KT, NT], F32R), sb(s, "xl_r", [P, KT, NT], F32R)
            oh_r, ol_r = sb(s, "oh_r", [P, 4, NT], F32R), sb(s, "ol_r", [P, 4, NT], F32R)
            rtab = sb(s, "ret_cos_sin", [P, 2, NT])
            rq, rk = sb(s, "ret_q", [P, 2, NT]), sb(s, "ret_k", [P, 2, NT])
            rqd = sb(s, "ret_q_decayed", [P, 2, NT])
            rv = sb(s, "ret_v", [P, 5, DV])
            ro = sb(s, "ret_o", [P, 4, NT])
            pm = sb(s, "rope_parts", [P, 2, NT])
            sg_r = sb(s, "silu_gate_r", [P, 2, NT])
            ssb = sb(s, "ret_scores_T", [P, 2, P])
            ktk = sb(s, "k_by_token", [P, 2, DK])
            km = sb(s, "k_of_batch", [ST, 2, DK])
            state = sb(s, "state", [P, 2, DV])
            sst = sb(s, "sample_state", [P, 4, 2, DV])
            rdec = sb(s, "ret_decay_T", [P, RH, P])
            rqdec = sb(s, "ret_q_decay", [P, RH, P])
            rsdec = sb(s, "ret_sample_decay_T", [ST, RH, ST])
            rcol = sb(s, "ret_columns", [P, 4, RH])
            rbm = sb(s, "batch_mask", [ST, SB])
        kvp = ExitStack()
        with kvp:
            k_t = sb(kvp, "k_T", [P, 4, NT])
            v_tok = sb(kvp, "v_tok", [P, 5, 512])
            kc_p = sb(kvp, "kc_prompt_T", [P, 2, NC_P])
            vc_p = sb(kvp, "vc_prompt", [NC_P, 256])
            kc_s = sb(kvp, "kc_sample_T", [P, SB, 2, NC_S])
            vc_s = sb(kvp, "vc_sample", [NC_S, SB, 256])
            atab = sb(kvp, "att_cos_sin", [P, 2, NT])
            ctab = sb(kvp, "cmp_cos_sin", [P, 2, NC_S])
            with ExitStack() as s:
                xh_f, xl_f = sb(s, "xh_f", [P, KT, NT], F32R), sb(s, "xl_f", [P, KT, NT], F32R)
                hh, hl = sb(s, "hh", [P, FH, NT], F32R), sb(s, "hl", [P, FH, NT], F32R)
                sg = sb(s, "silu_gate", [P, NT])
                hf = sb(s, "h_full", [P, NT])
            with ExitStack() as s:
                kraw = sb(s, "kv_raw", [P, 8, NT])
                parts_k = sb(s, "head_parts_k", [P, 3, NT])
                with ExitStack() as s2:
                    xh_k = sb(s2, "xh_k", [P, KT, NT], F32R)
                    xl_k = sb(s2, "xl_k", [P, KT, NT], F32R)
                pgs = sb(s, "cmp_pages", [P, 2, NPG, 512])
                xp = sb(s, "cmp_prompt", [P, 2, G, 8, 32])
                w1 = sb(s, "cmp_w1", [P, 2, 8, P])
                w2 = sb(s, "cmp_w2", [DH, 2, DH])
                pe_t = sb(s, "cmp_pe", [P, 2, 8, 2])
                cb = sb(s, "cmp_bias", [DH, 2, 2])
                p1 = sb(s, "cmp_next", [DH, 2, 256])
                hid = sb(s, "cmp_hidden", [DH, 2, 4, NC_S])
                hge = sb(s, "cmp_gelu", [DH, 2, 4, NC_S])
                ck = sb(s, "kc_raw", [P, 2 * NC_S])
            with ExitStack() as s:
                q = sb(s, "q_T", [P, KT, NT])
                gt = sb(s, "gates", [P, 5, 48])
                gs = sb(s, "sample_gates", [P, SB, 3])
                with ExitStack() as s2:
                    xh_n = sb(s2, "xh_n", [P, KT, NT], F32R)
                    xl_n = sb(s2, "xl_n", [P, KT, NT], F32R)
                    parts_n = sb(s2, "head_parts_n", [P, 3, NT])
                    sel_e = sb(s2, "gate_rows", [ST, SB, P])
                    sel_m = sb(s2, "gate_mask", [P, 48])
                    gw = sb(s2, "gates_by_row", [P, SB, 48])
                ah, al = sb(s, "ah", [P, KT, NT], F32R), sb(s, "al", [P, KT, NT], F32R)
                with ExitStack() as s2:
                    qst = sb(s2, "q_pair", [P, 2, PT])
                    cmask = sb(s2, "cmp_mask", [P, 2, 4, NC_P])
                    pr = sb(s2, "probs", [P, 2, 1024])
                    pc = sb(s2, "probs_cmp", [P, 8, NC_P])
                    c8 = sb(s2, "cmp_stats", [P, 3, 8])
                    prt = sb(s2, "probs_T", [P, 2, 1024])
                    pct = sb(s2, "probs_cmp_T", [NC_P, 2, PT])
                    stat = sb(s2, "att_stats", [P, 2, 2, 2])
                    sums = sb(s2, "att_sums", [P, 4, 2])
                    ls = sb(s2, "att_gates", [P, 2, 2])
                    ot = sb(s2, "o_by_token", [P, 4, P])
                with ExitStack() as s2:
                    kp = sb(s2, "k_pages", [P, NPG, 2, PAGE])
                    vp = sb(s2, "v_pages", [P, NPG, 256])
                    kw = sb(s2, "k_window", [P, 2, WIN])
                    vw = sb(s2, "v_window", [P, 4, 256])
                    qbd = sb(s2, "q_block_diagonal", [P, 2, 64])
                    kcs = sb(s2, "kc_of_batch", [P, 2, NC_S])
                    vcs = sb(s2, "vc_of_batch", [NC_S, 256])
                    ps_ = sb(s2, "sample_probs", [P, 1088 + 576])
                    pcs = sb(s2, "sample_probs_cmp", [P, NC_S])
                    pst = sb(s2, "sample_probs_T", [P, 8, P])
                    small = sb(s2, "sample_small_T", [ST, 3, P])
                    smask = sb(s2, "new_key_mask", [P, SB, 64])
                    wmask = sb(s2, "window_mask", [P, 8])
                    iot = sb(s2, "block_numbers", [P, 14])
                    ovl = sb(s2, "overlap", [NC_S, 14])
                    drop = sb(s2, "dropped_block", [P, NSEL])
                    dtmp = sb(s2, "block_choice", [P, 2, 14])
                    sst2 = sb(s2, "sample_stats", [P, 16])
                    oa = sb(s2, "sample_o", [P, DH])
                    os_ = sb(s2, "sample_o_T", [P, KT, ST])
        ps = ctx.enter_context(nc.psum_tensor("ps", [P, 8, 512], F32))

        def wide(t):
            return t.rearrange("p (h n) -> p h n", h=2)

        def bank2(b):
            return ps[:, b:b + 2, 0:HALF]

        consts_in, tab_in, out_done = sem("consts_in"), sem("stage_tables_in"), sem("output_written")
        landed = [sem("block_landed_0"), sem("block_landed_1")]
        hi_ready, lo_ready, w_used = sem("w_high_ready"), sem("w_low_ready"), sem("block_used")
        free = [sem("slot0_free"), sem("slot1_free")]
        phase = sem("phase_done")
        chain_v, chain_a, chain_g = sem("vector_steps"), sem("scalar_steps"), sem("pool_steps")
        sq_ready, sq_used = sem("squares_ready"), sem("squares_summed")
        eps_added, root_ready, rb_ready = sem("eps_added"), sem("root_ready"), sem("stats_spread")
        r_sum, r_ready = sem("rstd_in_psum"), sem("rstd_ready")
        xf_ready, xh_ready, xn_ready = sem("x_normed"), sem("x_high_ready"), sem("x_split_ready")
        sg_ready, h_ready = sem("silu_ready"), sem("h_split_ready")

        st_set = sem("token_stats_set")
        consts = [(x, "x"), (gain, "gain"), (mats, "mats"), (mcol, "mcol"), (causal, "causal"), (pgt, "pt")]
        N_CONST = len(consts)

        block = ctx.enter_context(nc.Block())

        TILES = [(i * P, min(P, NT - i * P)) for i in range(5)]

        def barrier(eng, n):
            eng.drain().then_inc(phase, 1)
            eng.wait_ge(phase, 4 * n)

        def split_high(act, u, slot, size, after=True):
            act.wait_ge(landed[slot], (u - slot) * 8 + 16)
            if after:
                act.wait_ge(w_used, u - 1)
            act.activation(wh[:, slot, 0:size], wf[:, slot, 0:size], ACT.Copy).then_inc(hi_ready, 1)

        def split_low(dve, u, slot, size):
            dve.wait_ge(hi_ready, u + 1)
            dve.tensor_tensor(wl[:, slot, 0:size], wf[:, slot, 0:size], wh[:, slot, 0:size].bitcast(F32),
                              ALU.subtract).then_inc(lo_ready, 1)

        def sums_pe(pe, src, tiles, cols, first, last, bank=4):
            w = cols.shape[-1]
            for i, (c0, m) in enumerate(tiles):
                mm = pe.matmul(ps[0:m, bank, 2 * i:2 * i + w], src[:, c0:c0 + m], cols,
                               start=(first and i == 0), stop=(last and i == len(tiles) - 1),
                               skip_group_check=True)
            return mm

        def stats_dve(dve, cv, n, tiles, w, bank=4):
            whole = [i for i, (_, m) in enumerate(tiles) if m == P]
            parts = [(0, P, whole)] if whole else []
            parts += [(i, m, [i]) for i, (_, m) in enumerate(tiles) if m < P]
            for i0, m, idx in parts:
                src = ps[0:m, bank, 2 * i0:2 * (i0 + len(idx))].rearrange("p (i w) -> p i w", w=2)
                ins = dve.tensor_scalar(st[0:m, i0:i0 + len(idx), 0:w], src[:, :, 0:w], EPS, None, ALU.add)
                if i0 == parts[-1][0]:
                    ins.then_inc(eps_added, 1)
                else:
                    cv.step(ins)
            dve.wait_ge(root_ready, n + 1)
            cv.link(dve.reciprocal(st[:, :, 0:w], st[:, :, 0:w]))
            dve.tensor_copy(rb[:, 0:len(tiles), :].rearrange("p i (w d) -> p i w d", w=w),
                            st[:, 0:len(tiles), 0:w].unsqueeze(3).to_broadcast([P, len(tiles), w, P // w])
                            ).then_inc(rb_ready, 1)

        def root_act(act, n, w):
            act.wait_ge(eps_added, n + 1)
            act.activation(st[:, :, 0:w], st[:, :, 0:w], ACT.Sqrt).then_inc(root_ready, 1)

        def spread_pe(pe, n, tiles):
            pe.wait_ge(rb_ready, n + 1)
            for i, (c0, m) in enumerate(tiles):
                mm = pe.matmul(ps[:, 5 + c0 // 512, c0 % 512:c0 % 512 + m], rb[0:m, i, :], ident[0:m, 0:m],
                               start=True, stop=True)
            mm.then_inc(r_sum, 1)

        def spread_act(act, ca, n, width):
            act.wait_ge(r_sum, n + 1)
            ins = act.activation(r[:, 0:min(width, 512)], ps[:, 5, 0:min(width, 512)], ACT.Copy)
            if width > 512:
                ca.step(ins)
                ins = act.activation(r[:, 512:width], ps[:, 6, 0:width - 512], ACT.Copy)
            ins.then_inc(r_ready, 1)

        def norm_pe(pe, n, m):
            for k in range(KT):
                pe.wait_ge(sq_ready, 8 * m + k + 1)
                sums_pe(pe, sq[:, k % 2, :], TILES, mcol[:, 0:1], k == 0, k == KT - 1).then_inc(sq_used, 1)
            spread_pe(pe, n, TILES)

        def norm_act(act, ca, n, m, xh, s):
            if m == 0:
                act.wait_ge(consts_in, 16 * N_CONST)
            else:
                act.wait_ge(free[0], F0[s])
                act.wait_ge(free[1], F1[s])
            for k in range(KT):
                if m or k >= 2:
                    act.wait_ge(sq_used, 8 * m + k - 1)
                act.activation(sq[:, k % 2, :], x[:, k, :], ACT.Square).then_inc(sq_ready, 1)
            root_act(act, n, 1)
            spread_act(act, ca, n, NT)
            for k in range(KT):
                act.wait_ge(xf_ready, 8 * m + k + 1)
                act.activation(xh[:, k, :], xf[:, k % 2, :], ACT.Copy).then_inc(xh_ready, 1)

        def norm_dve(dve, cv, n, m, xh, xl, g0):
            dve.wait_ge(sq_used, 8 * m + KT)
            stats_dve(dve, cv, n, TILES, 1)
            dve.wait_ge(r_ready, n + 1)

            def low(k):
                dve.wait_ge(xh_ready, 8 * m + k + 1)
                dve.tensor_tensor(xl[:, k, :], xf[:, k % 2, :], xh[:, k, :].bitcast(F32),
                                  ALU.subtract).then_inc(xn_ready, 1)

            for k in range(KT):
                if k >= 2:
                    dve.wait_ge(xn_ready, 8 * m + k - 1)
                dve.scalar_tensor_tensor(xf[:, k % 2, :], x[:, k, :], gain[:, g0 + k:g0 + k + 1], r[:, :],
                                         ALU.mult, ALU.mult).then_inc(xf_ready, 1)
                if k:
                    low(k - 1)
            low(KT - 1)

        def passes(pe, out, slot, cols, m_hi, m_lo, first, last):
            for n, (w, m) in enumerate(((wh, m_hi), (wh, m_lo), (wl, m_hi))):
                for h in range(2):
                    mm = pe.matmul(ps[:, out + h, 0:HALF], w[:, slot, cols:cols + P],
                                   m[:, h * HALF:(h + 1) * HALF], start=(first and n == 0),
                                   stop=(last and n == 2))
            return mm

        def take_block(pe, u, slot, uses):
            pe.wait_ge(lo_ready, u + 1)
            if not (isinstance(uses, int) and uses == 0):
                pe.wait_ge(free[slot], uses)

        def unit_pe(pe, u, slot, uses, nk, hi, lo, m=None):
            take_block(pe, u, slot, uses)
            for k in range(nk):
                if m is not None:
                    pe.wait_ge(xn_ready, 8 * m + k + 1)
                mm = passes(pe, 2 * slot, slot, k * P, hi[:, k, :], lo[:, k, :], k == 0, k == nk - 1)
            mm.then_inc(w_used, 1)

        def stored(eng, f):
            if f == 1:
                eng.wait_ge(st_sent, 16 * RH)
                for q_ in sout:
                    eng.wait_ge(q_, 32 * RH)
            if f == 2:
                eng.wait_ge(kv_sent, 16 * 4)

        def ffn_pe(pe, f, s, n, m):
            norm_pe(pe, n, m)
            for h in range(2):
                ub, f0, f1 = U0[s] + 30 * h, F0[s] + 15 * h, F1[s] + 15 * h

                def pair(j, first=None):
                    unit_pe(pe, ub + 2 * j, 0, f0 + j, KT, xh_f, xl_f, first)
                    unit_pe(pe, ub + 2 * j + 1, 1, f1 + j, KT, xh_f, xl_f)

                def outs(i):
                    unit_pe(pe, ub + 22 + 2 * i, 0, f0 + FH + i, FH, hh, hl)
                    unit_pe(pe, ub + 23 + 2 * i, 1, f1 + FH + i, FH, hh, hl)

                pair(0, m if h == 0 else None)
                with pe.Fori(1, FH) as j:
                    pair(j)
                pe.wait_ge(h_ready, FH * (2 * f + h + 1))
                with pe.Fori(0, KT // 2) as i:
                    outs(i)

        def ffn_act(act, ca, f, s, n, m, last):
            stored(act, f)
            norm_act(act, ca, n, m, xh_f, s)
            for h in range(2):
                ub = U0[s] + 30 * h

                def pair(j, size):
                    u = ub + 2 * j
                    act.wait_ge(w_used, u + 1)
                    if not (isinstance(j, int) and f == h == j == 0):
                        act.wait_ge(h_ready, FH * (2 * f + h) + j)
                    act.activation(wide(sg[:, :]), bank2(0), ACT.Silu).then_inc(free[0], 1)
                    split_high(act, u + 2, 0, size)
                    split_high(act, u + 3, 1, size)

                def outs(i, more=True):
                    if more:
                        split_high(act, ub + 24 + 2 * i, 0, UB if more == 2 else UA)
                        split_high(act, ub + 25 + 2 * i, 1, UB if more == 2 else UA)

                pair(0, UA)
                with act.Fori(1, FH - 1) as j:
                    pair(j, UA)
                pair(FH - 1, UB)
                with act.Fori(0, KT // 2 - 1) as i:
                    outs(i, 2)
                outs(KT // 2 - 1, not (last and h == 1))

        def ffn_dve(dve, cv, f, s, n, m, last):
            stored(dve, f)
            norm_dve(dve, cv, n, m, xh_f, xl_f, G_FFN + 8 * f)
            for h in range(2):
                ub, f0, f1 = U0[s] + 30 * h, F0[s] + 15 * h, F1[s] + 15 * h

                def pair(j, size):
                    u = ub + 2 * j
                    split_low(dve, u + 2, 0, size)
                    dve.wait_ge(w_used, u + 2)
                    dve.wait_ge(free[0], f0 + j + 1)
                    if not (isinstance(j, int) and f == h == j == 0):
                        dve.wait_ge(h_ready, FH * (2 * f + h) + j)
                    dve.tensor_tensor(wide(hf[:, :]), wide(sg[:, :]), bank2(2), ALU.mult).then_inc(free[1], 1)
                    dve.wait_ge(free[1], f1 + j + 1)
                    cv.link(dve.tensor_copy(hh[:, ds(j, 1), :], hf[:, :].unsqueeze(1)))
                    dve.tensor_tensor(hl[:, ds(j, 1), :], hf[:, :].unsqueeze(1),
                                      hh[:, ds(j, 1), :].bitcast(F32), ALU.subtract).then_inc(h_ready, 1)
                    split_low(dve, u + 3, 1, size)

                def outs(i, more):
                    for k in range(2):
                        if more:
                            split_low(dve, ub + 24 + 2 * i + k, k, UB if more == 2 else UA)
                        dve.wait_ge(w_used, ub + 23 + 2 * i + k)
                        t = wide_d(x[:, ds(2 * i + k, 1), :])
                        dve.scalar_tensor_tensor(t, bank2(2 * k), 0.5, t, ALU.mult, ALU.add
                                                 ).then_inc(free[k], 1)

                cv.loop(FH - 1, 1, lambda j: pair(j, UA))
                pair(FH - 1, UB)
                with dve.Fori(0, KT // 2 - 1) as i:
                    outs(i, 2)
                outs(KT // 2 - 1, 0 if last and h == 1 else 1)

        def wide_d(t):
            return t.rearrange("p o (h n) -> p (o h) n", h=2)

        raw_ready, rope_ready = sem("raw_ready"), sem("rope_ready")
        v_ready, st_sent = sem("ret_v_ready"), sem("state_sent")
        s_done, sk_ready, o_done, o_taken = sem("scores_done"), sem("scores_k_ready"), sem("o_done"), sem("o_taken")
        st_done, km_ready = sem("state_done"), sem("batch_k_ready")
        smp_done, smp_new = sem("sample_state_product"), sem("sample_state_new")
        sin = [sem(f"sample_state_in_{i}") for i in range(4)]
        sout = [sem(f"sample_state_out_{i}") for i in range(4)]
        mu_done, d_ready, dq_ready, dq_used = (sem(n) for n in ("mean_done", "centred", "centred_sq", "centred_sq_used"))
        rg_ready, og_ready = sem("ret_silu_ready"), sem("ret_gated")
        U, A0, A1 = U0["ret"], F0["ret"], F1["ret"]
        ret_tabs = sem("ret_tables_in")
        N_RET = 1

        def ret_pe(pe):
            norm_pe(pe, N_RET, 1)
            pe.wait_ge(xn_ready, 8 * 2)

            def head(h):
                u0, a0, a1 = U + h * RU, A0 + h * RU0, A1 + h * RU1
                for i in range(4):
                    unit_pe(pe, u0 + i, i % 2, (a0, a1)[i % 2] + i // 2, KT, xh_r, xl_r)
                pe.wait_ge(free[0], a0 + 2)
                pe.wait_ge(o_taken, 5 * h)
                pe.wait_ge(smp_new, 8 * h)
                pe.wait_ge(r_ready, N_RET + 1 + h)
                for i in range(4):
                    pe.wait_ge(lo_ready, u0 + 5 + i)
                    for kk in range(2):
                        k = 2 * i + kk
                        for t, (c0, m) in enumerate(TILES):
                            b = 4 + t if t < 4 else 0
                            for n, (xx, w) in enumerate(((xh_r, wh), (xh_r, wl), (xl_r, wh))):
                                mm = pe.matmul(ps[0:m, b, :], xx[:, k, c0:c0 + m],
                                               w[:, i % 2, kk * DV:(kk + 1) * DV],
                                               start=(k == 0 and n == 0), stop=(k == KT - 1 and n == 2))
                    mm.then_inc(w_used, 1)

                def scores(c):
                    c0, m = TILES[c]
                    for t in range(2):
                        pe.matmul(ps[0:m, 4, 0:m], rk[:, t, c0:c0 + m], rq[:, t, c0:c0 + m],
                                  start=(t == 0), stop=(t == 1))
                    for t in range(2):
                        mm = pe.transpose(ps[0:m, 4, P + P * t:2 * P + P * t], rk[:, t, c0:c0 + m], ident)
                    mm.then_inc(s_done, 1)

                pe.wait_ge(rope_ready, h + 1)
                pe.wait_ge(v_ready, h + 1)
                pe.wait_ge(free[0], a0 + 3)
                scores(0)
                for c in range(NCH):
                    pe.wait_ge(sk_ready, 5 * h + c + 1)
                    scores(c + 1)
                    pe.wait_ge(st_done, 4 * h + c)
                    for t in range(2):
                        pe.matmul(ps[:, 6 + t, :], ktk[:, c % 2, t * P:(t + 1) * P], rv[:, c, :],
                                  start=True, stop=True)
                    pe.wait_ge(o_taken, 5 * h + c)
                    for v in range(4):
                        mm = pe.matmul(ps[:, 5, v * P:(v + 1) * P], rv[:, c, v * P:(v + 1) * P],
                                       ssb[:, c % 2, :], start=(v == 0), stop=(c == 0),
                                       skip_group_check=True)
                        for t in range(2 if c else 0):
                            mm = pe.matmul(ps[:, 5, v * P:(v + 1) * P], state[:, t, v * P:(v + 1) * P],
                                           rqd[:, t, c * CH:(c + 1) * CH], start=False, stop=(t == 1),
                                           skip_group_check=True)
                    mm.then_inc(o_done, 1)
                pe.wait_ge(sk_ready, 5 * h + 5)
                pe.wait_ge(o_taken, 5 * h + 4)
                pe.wait_ge(st_done, 4 * h + 4)
                for v in range(4):
                    pe.matmul(ps[:, 5, v * ST:(v + 1) * ST], rv[0:ST, 4, v * P:(v + 1) * P],
                              ssb[0:ST, 0, 0:ST], start=(v == 0), stop=False, skip_group_check=True)
                for b in range(SB):
                    pe.wait_ge(sin[b % 4], 32 * h + 16 * (b // 4) + 16)
                    for v in range(4):
                        for t in range(2):
                            c0 = v * ST + b * SQ
                            mm = pe.matmul(ps[:, 5, c0:c0 + SQ], sst[:, b % 4, t, v * P:(v + 1) * P],
                                           rqd[:, t, PT + b * SQ:PT + (b + 1) * SQ], start=False,
                                           stop=(t == 1), skip_group_check=True)
                    if b == SB - 1:
                        mm.then_inc(o_done, 1)
                    pe.wait_ge(km_ready, 8 * h + b + 1)
                    if b:
                        pe.wait_ge(smp_new, 8 * h + b)
                    for t in range(2):
                        mm = pe.matmul(ps[:, 6 + t, :], km[:, b % 2, t * P:(t + 1) * P], rv[0:ST, 4, :],
                                       start=True, stop=True)
                    mm.then_inc(smp_done, 1)

                pe.wait_ge(o_taken, 5 * h + 5)
                for v in range(4):
                    for hf_ in range(2):
                        mm = pe.matmul(ps[:, hf_, 0:HALF], ones_v, ro[:, v, hf_ * HALF:(hf_ + 1) * HALF],
                                       start=(v == 0), stop=(v == 3))
                mm.then_inc(mu_done, 1)
                for v in range(4):
                    pe.wait_ge(dq_ready, 4 * h + v + 1)
                    sums_pe(pe, sq[:, v % 2, :], TILES, mcol[:, 1:2], v == 0, v == 3).then_inc(dq_used, 1)
                spread_pe(pe, N_RET + 1 + h, TILES)
                for i in range(4):
                    unit_pe(pe, u0 + 8 + i, i % 2, (a0 + 3, a1 + 2)[i % 2] + i // 2, KT, xh_r, xl_r)
                pe.wait_ge(og_ready, 4 * h + 4)
                for i in range(4):
                    for k in range(2):
                        take_block(pe, u0 + 12 + i, k, (a0 + 5, a1 + 4)[k] + i)
                        for v in range(4):
                            mm = passes(pe, 2 * k, i % 2, (4 * k + v) * P, oh_r[:, v, :], ol_r[:, v, :],
                                        v == 0, v == 3)
                    mm.then_inc(w_used, 1)

            with pe.Fori(0, RH) as h:
                head(h)

        def ret_act(act, ca):
            norm_act(act, ca, N_RET, 1, xh_r, "ret")

            def head(h):
                u0 = U + h * RU
                act.wait_ge(og_ready, 4 * h)
                for i in range(4):
                    act.wait_ge(w_used, u0 + i + 1)
                    act.activation(wide(ro[:, i, :]), bank2(2 * (i % 2)), ACT.Copy).then_inc(free[i % 2], 1)
                    split_high(act, u0 + i + 2, i % 2, UA)
                for i in range(4, 8):
                    split_high(act, u0 + i + 2, i % 2, UA)
                act.wait_ge(w_used, u0 + 8)
                act.activation(rv[0:ST, 4, :], ps[0:ST, 0, :], ACT.Copy).then_inc(free[0], 1)
                act.activation(rv[:, 0:4, :], ps[:, 4:8, :], ACT.Copy).then_inc(v_ready, 1)
                for c in range(5):
                    c0, m = TILES[c]
                    act.wait_ge(o_done, 5 * h + c + 1)
                    act.activation(ro[:, :, c0:c0 + m], ps[:, 5, 0:4 * m].rearrange("p (v m) -> p v m", v=4),
                                   ACT.Copy).then_inc(o_taken, 1)
                for v in range(4):
                    act.wait_ge(d_ready, 4 * h + v + 1)
                    if v >= 2:
                        act.wait_ge(dq_used, 4 * h + v - 1)
                    act.activation(sq[:, v % 2, :], ro[:, v, :], ACT.Square).then_inc(dq_ready, 1)
                root_act(act, N_RET + 1 + h, 1)
                spread_act(act, ca, N_RET + 1 + h, NT)
                for v in range(4):
                    act.wait_ge(w_used, u0 + 9 + v)
                    if v >= 2:
                        act.wait_ge(og_ready, 4 * h + v - 1)
                    act.activation(wide(sg_r[:, v % 2, :]), bank2(2 * (v % 2)), ACT.Silu
                                   ).then_inc(free[v % 2], 1)
                    split_high(act, u0 + 10 + v, v % 2, UA)
                for i in range(4):
                    split_high(act, u0 + 14 + i, i % 2, UA)

            ca.loop(RH, 1, head)

        def ret_dve(dve, cv):
            dve.wait_ge(ret_tabs, 96)
            norm_dve(dve, cv, N_RET, 1, xh_r, xl_r, G_RET)

            def head(h):
                u0, a0, a1 = U + h * RU, A0 + h * RU0, A1 + h * RU1
                for i in range(8):
                    split_low(dve, u0 + 2 + i, i % 2, UA)

                def scores(c):
                    m = TILES[c][1]
                    dve.wait_ge(s_done, 5 * h + c + 1)
                    dec = rdec[:, ds(h, 1), :] if c < 4 else rsdec[:, ds(h, 1), :]
                    cv.step(dve.tensor_tensor(ssb[0:m, c % 2, 0:m].unsqueeze(1), ps[0:m, 4, 0:m].unsqueeze(1),
                                              dec, ALU.mult))
                    kd = rcol[0:m, 0 if c < 4 else 1, ds(h, 1)]
                    dve.tensor_scalar(ktk[0:m, c % 2, :], ps[0:m, 4, P:3 * P], kd, None, ALU.mult
                                      ).then_inc(sk_ready, 1)

                scores(0)
                for c in range(NCH):
                    scores(c + 1)
                    dve.wait_ge(o_done, 5 * h + c + 1)
                    two = ps[:, 6:8, :]
                    if c == 0:
                        dve.wait_ge(st_sent, 16 * h)
                        dve.tensor_copy(state[:, :, :], two).then_inc(st_done, 1)
                    else:
                        dve.wait_ge(st_done, 4 * h + c)
                        dve.scalar_tensor_tensor(state[:, :, :], state[:, :, :], rcol[:, 2, ds(h, 1)], two,
                                                 ALU.mult, ALU.add).then_inc(st_done, 1)
                for b in range(SB):
                    dve.wait_ge(smp_done, 8 * h + b + 1)
                    dve.scalar_tensor_tensor(sst[:, b % 4, :, :], sst[:, b % 4, :, :], rcol[:, 3, ds(h, 1)],
                                             ps[:, 6:8, :], ALU.mult, ALU.add).then_inc(smp_new, 1)
                dve.wait_ge(mu_done, h + 1)
                for v in range(4):
                    dve.tensor_tensor(wide(ro[:, v, :]), wide(ro[:, v, :]), bank2(0), ALU.subtract
                                      ).then_inc(d_ready, 1)
                dve.wait_ge(dq_used, 4 * h + 4)
                stats_dve(dve, cv, N_RET + 1 + h, TILES, 1)
                dve.wait_ge(r_ready, N_RET + 2 + h)
                for v in range(4):
                    cv.link(dve.tensor_tensor(ro[:, v, :], ro[:, v, :], r[:, :], ALU.mult))
                    dve.wait_ge(free[v % 2], (a0 + 4, a1 + 3)[v % 2] + v // 2)
                    cv.link(dve.tensor_tensor(ro[:, v, :], ro[:, v, :], sg_r[:, v % 2, :], ALU.mult))
                    cv.link(dve.tensor_copy(oh_r[:, v, :], ro[:, v, :]))
                    dve.tensor_tensor(ol_r[:, v, :], ro[:, v, :], oh_r[:, v, :].bitcast(F32),
                                      ALU.subtract).then_inc(og_ready, 1)
                    split_low(dve, u0 + 10 + v, v % 2, UA)
                for i in range(4):
                    dve.wait_ge(w_used, u0 + 13 + i)
                    for k in range(2):
                        t = wide(x[:, 2 * i + k, :])
                        dve.tensor_tensor(t, t, bank2(2 * k), ALU.add).then_inc(free[k], 1)
                    split_low(dve, u0 + 14 + i, i % 2, UA)

            cv.loop(RH, 5 + 2 + 12, head)

        def ret_pool(pool, cg):
            pool.wait_ge(free[0], A0)
            pool.wait_ge(free[1], A1)
            for t, name in ((rtab, "rtab"), (rdec, "rdec"), (rqdec, "rqdec"), (rsdec, "rsdec"),
                            (rcol, "rcol"), (rbm, "rbm")):
                pool.dma_start(t[:], a[name]).then_inc(ret_tabs, 16)
            pool.wait_ge(ret_tabs, 96)

            def state_in(h, b):
                pool.nop(nofuse=True)
                pool.dma_start(sst[:, b % 4, :, :], a["state"][ds(h, 1), b].rearrange("o p t v -> p (o t) v")
                               ).then_inc(sin[b % 4], 16)

            def head(h):
                for i in range(4):
                    pool.wait_ge(sout[i], 32 * h)
                    state_in(h, i)
                pool.wait_ge(free[0], A0 + h * RU0 + 2)
                pool.wait_ge(free[1], A1 + h * RU1 + 2)
                cos, sin_ = rtab[:, 0, :], rtab[:, 1, :]
                for i, out in ((0, rq), (2, rk)):
                    lo, hi = ro[:, i, :], ro[:, i + 1, :]
                    cg.step(pool.tensor_tensor(pm[:, 0, :], lo, cos, ALU.mult))
                    cg.link(pool.tensor_tensor(pm[:, 1, :], hi, sin_, ALU.mult))
                    cg.link(pool.tensor_tensor(out[:, 0, :], pm[:, 0, :], pm[:, 1, :], ALU.subtract))
                    cg.step(pool.tensor_tensor(pm[:, 0, :], lo, sin_, ALU.mult))
                    cg.link(pool.tensor_tensor(pm[:, 1, :], hi, cos, ALU.mult))
                    cg.link(pool.tensor_tensor(out[:, 1, :], pm[:, 0, :], pm[:, 1, :], ALU.add))
                for t in range(2):
                    dec = rqdec[:, ds(h, 1), :]
                    cg.step(pool.tensor_tensor(
                        rqd[:, t, 0:PT].rearrange("p (c i) -> p c i", c=NCH),
                        rq[:, t, 0:PT].rearrange("p (c i) -> p c i", c=NCH),
                        dec.to_broadcast([P, NCH, CH]), ALU.mult))
                    ins = pool.tensor_tensor(
                        rqd[:, t, PT:NT].rearrange("p (b i) -> p b i", b=SB),
                        rq[:, t, PT:NT].rearrange("p (b i) -> p b i", b=SB),
                        rqdec[:, ds(h, 1), 0:SQ].to_broadcast([P, SB, SQ]), ALU.mult)
                    if t == 0:
                        cg.step(ins)
                    else:
                        ins.then_inc(rope_ready, 1)

                def batch_k(b):
                    if b >= 2:
                        pool.wait_ge(smp_done, 8 * h + b - 1)
                    pool.nop(nofuse=True)
                    pool.tensor_scalar(km[:, b % 2, :], ktk[0:ST, 0, :], rbm[:, b:b + 1], None, ALU.mult
                                       ).then_inc(km_ready, 1)

                pool.wait_ge(sk_ready, 5 * h + 5)
                batch_k(0)
                batch_k(1)
                for b in range(SB):
                    pool.wait_ge(smp_new, 8 * h + b + 1)
                    pool.nop(nofuse=True)
                    pool.dma_start(o["state_s"][ds(h, 1), b].rearrange("o p t v -> p (o t) v"),
                                   sst[:, b % 4, :, :]).then_inc(sout[b % 4], 16)
                    if b + 2 < SB:
                        batch_k(b + 2)
                    if 1 <= b <= 4:
                        c = b - 1
                        pool.wait_ge(sout[c], 32 * h + 16)
                        state_in(h, c + 4)
                pool.dma_start(o["state_p"][ds(h, 1)].rearrange("o p t v -> p (o t) v"), state[:, :, :]
                               ).then_inc(st_sent, 16)

            cg.loop(RH, 15, head)

        hr_sq, hr_sum, hr_n, hr_rot = (sem(n) for n in ("head_sq", "head_sum", "head_normed", "head_rotated"))
        CMP_P, CMP_S = [(0, 2 * NC_P)], [(0, 2 * NC_S)]

        def head_pe(pe, n, i, tiles, part):
            pe.wait_ge(hr_sq, i + 1)
            sums_pe(pe, sq[:, 0, :], tiles, mcol[:, 2:4], True, True).then_inc(hr_sum, 1)
            spread_pe(pe, n, tiles)
            pe.wait_ge(hr_n, i + 1)
            width = sum(m for _, m in tiles)
            mm = pe.matmul(ps[:, 7, 0:min(width, 512)], rot, part[:, 0, 0:min(width, 512)], start=True, stop=True)
            if width > 512:
                mm = pe.matmul(ps[:, 6, 64:64 + width - 512], rot, part[:, 0, 512:width], start=True, stop=True)
            mm.then_inc(hr_rot, 1)

        def head_act(act, ca, n, raw, width):
            act.activation(sq[:, 0, 0:width], raw, ACT.Square).then_inc(hr_sq, 1)
            root_act(act, n, 2)
            spread_act(act, ca, n, width)

        def head_dve(dve, cv, n, i, tiles, part, raw, g0, out, cos, sin_):
            width = sum(m for _, m in tiles)
            dve.wait_ge(hr_sum, i + 1)
            stats_dve(dve, cv, n, tiles, 2)
            dve.wait_ge(r_ready, n + 1)
            dve.scalar_tensor_tensor(part[:, 0, 0:width], raw, gain[:, g0:g0 + 1], r[:, 0:width],
                                     ALU.mult, ALU.mult).then_inc(hr_n, 1)
            dve.wait_ge(hr_n, i + 1)
            three = len(cos.shape) == 3
            pair = (lambda t: t.rearrange("p (g c) -> p g c", g=2)) if three else (lambda t: t)
            cv.step(dve.tensor_tensor(pair(part[:, 1, 0:width]), pair(part[:, 0, 0:width]), cos, ALU.mult))
            dve.wait_ge(hr_rot, i + 1)
            if width > 512:
                cv.step(dve.tensor_tensor(part[:, 2, 0:512], ps[:, 7, 0:512], sin_[:, 0:512], ALU.mult))
                cv.link(dve.tensor_tensor(part[:, 2, 512:width], ps[:, 6, 64:64 + width - 512],
                                          sin_[:, 512:width], ALU.mult))
            else:
                cv.link(dve.tensor_tensor(pair(part[:, 2, 0:width]), pair(ps[:, 7, 0:width]), sin_, ALU.mult))
            cv.link(dve.tensor_tensor(out, part[:, 1, 0:width], part[:, 2, 0:width], ALU.add))

        kv_tabs, kvv_ready, kv_sent = sem("kv_tables_in"), sem("kv_v_ready"), sem("kv_rows_sent")
        pin = [sem("cmp_pages_in_0"), sem("cmp_pages_in_1")]
        pos_ready = sem("cmp_position_part")
        bias_done, bias_ready, xp_ready = sem("cmp_bias_product"), sem("cmp_bias_ready"), sem("cmp_prompt_ready")
        cp_h, cp_p1, cp_hid, cp_ge, cp_kc, cp_vc, ck_ready, vc_taken = (
            sem(n) for n in ("cmp_product", "cmp_next_ready", "cmp_hidden_ready", "cmp_gelu_ready",
                             "kc_product", "vc_product", "kc_raw_ready", "vc_taken"))
        UK, N_KV, N_CMP = U0["kv"], 8, 12
        KV_BARRIER, ATT_BARRIER = 1, 2

        def kv_pe(pe):
            norm_pe(pe, N_KV - 1, 3)
            pe.wait_ge(xn_ready, 8 * 4)
            for i in range(8):
                unit_pe(pe, UK + i, i % 2, (F0, F1)[i % 2]["kv"] + i // 2, KT, xh_k, xl_k)
            pe.wait_ge(free[0], F0["kv"] + 4)
            for i in range(4):
                pe.wait_ge(lo_ready, UK + 9 + i)
                for kk in range(2):
                    k = 2 * i + kk
                    for t, (c0, m) in enumerate(TILES):
                        for n, (xx, w) in enumerate(((xh_k, wh), (xh_k, wl), (xl_k, wh))):
                            mm = pe.matmul(ps[0:m, 4 + t if t < 4 else 0, :], xx[:, k, c0:c0 + m],
                                           w[:, i % 2, kk * 512:(kk + 1) * 512],
                                           start=(k == 0 and n == 0), stop=(k == KT - 1 and n == 2))
                mm.then_inc(w_used, 1)
            pe.wait_ge(kvv_ready, 1)
            for i in range(4):
                head_pe(pe, N_KV + i, i, TILES, parts_k)
            barrier(pe, KV_BARRIER)
            pe.wait_ge(kv_tabs, 16 * 5)
            for v in range(2):
                for t in range(8):
                    mm = pe.matmul(ps[:, 3, 2 * v:2 * v + 2], w1[:, v, t, :], pe_t[:, v, t, :],
                                   start=(t == 0), stop=(t == 7))
            mm.then_inc(bias_done, 1)

            def compress(e, tiles, rhs, nc_, ch):
                for v in range(2):
                    for t in range(8):
                        mm = pe.matmul(ps[:, v, 0:G * ch], w1[:, v, t, :], rhs(v, t),
                                       start=(t == 0), stop=(t == 7))
                    mm.then_inc(cp_h, 1)
                pe.wait_ge(cp_ge, 2 * e + 2)
                pe.wait_ge(ck_ready, e)
                pe.wait_ge(vc_taken, e)
                pe.nop(nofuse=True)
                for g in range(G):
                    mm = pe.matmul(ps[DH * (g % 2):DH * (g % 2 + 1), 2, g // 2 * nc_:(g // 2 + 1) * nc_],
                                   w2[:, 0, :], hge[:, 0, g, 0:nc_], start=True, stop=True)
                mm.then_inc(cp_kc, 1)
                for g in range(G):
                    mm = pe.matmul(ps[0:nc_, 3, g * DH:(g + 1) * DH], hge[:, 1, g, 0:nc_], w2[:, 1, :],
                                   start=True, stop=True)
                mm.then_inc(cp_vc, 1)
                head_pe(pe, N_CMP + e, 4 + e, tiles, parts_k)

            pe.wait_ge(xp_ready, 8)
            compress(0, CMP_P, lambda v, t: xp[:, v, :, t, :], NC_P, 32)
            with pe.Fori(0, SB // 2) as bp:
                for s in range(2):
                    pe.wait_ge(pin[s], bp * 16 * NPG + 16 * NPG)
                    pages = [pgs[:, s, :, v * 256:(v + 1) * 256].rearrange("p j (g t c) -> p t g j c", g=G, t=8)
                             for v in range(2)]
                    compress(2 * bp + s + 1, CMP_S, lambda v, t: pages[v][:, t], NC_S, 64)

        def kv_act(act, ca):
            norm_act(act, ca, N_KV - 1, 3, xh_k, "kv")
            for i in range(8):
                act.wait_ge(w_used, UK + i + 1)
                act.activation(wide(kraw[:, i, :]), bank2(2 * (i % 2)), ACT.Copy).then_inc(free[i % 2], 1)
                split_high(act, UK + i + 2, i % 2, UA)
            for i in range(8, 12):
                split_high(act, UK + i + 2, i % 2, UA)
            act.wait_ge(w_used, UK + 12)
            act.activation(v_tok[0:ST, 4, :], ps[0:ST, 0, :], ACT.Copy).then_inc(free[0], 1)
            act.activation(v_tok[:, 0:4, :], ps[:, 4:8, :], ACT.Copy).then_inc(kvv_ready, 1)
            act.wait_ge(free[1], F1["kv"] + 4)
            for i in range(4):
                head_act(act, ca, N_KV + i, kraw[:, 4 + i, :], NT)
            barrier(act, KV_BARRIER)
            act.wait_ge(bias_done, 1)
            act.activation(cb[:, :, 0], ps[DH:P, 3, 1:4:2], ACT.Copy).then_inc(pos_ready, 1)

            def compress(e, nc_, ch):
                for v in range(2):
                    act.wait_ge(cp_h, 2 * e + v + 1)
                    act.activation(p1[:, v, 0:G * ch], ps[DH:P, v, 0:G * ch], ACT.Identity,
                                   bias=cb[:, v, 1:2]).then_inc(cp_p1, 1)
                for v in range(2):
                    act.wait_ge(cp_hid, 2 * e + v + 1)
                    act.activation(hge[:, v, :, 0:nc_], hid[:, v, :, 0:nc_], ACT.Gelu_apprx_tanh
                                   ).then_inc(cp_ge, 1)
                act.wait_ge(cp_kc, e + 1)
                act.activation(ck[:, 0:2 * nc_], ps[:, 2, 0:2 * nc_], ACT.Copy).then_inc(ck_ready, 1)
                act.wait_ge(ck_ready, e + 1)
                head_act(act, ca, N_CMP + e, ck[:, 0:2 * nc_], 2 * nc_)

            act.wait_ge(bias_ready, 1)
            compress(0, NC_P, 32)
            with act.Fori(0, SB // 2) as bp:
                for s in range(2):
                    compress(2 * bp + s + 1, NC_S, 64)

        def kv_dve(dve, cv):
            norm_dve(dve, cv, N_KV - 1, 3, xh_k, xl_k, G_KV)
            for i in range(12):
                split_low(dve, UK + i + 2, i % 2, UA)
            dve.wait_ge(kv_tabs, 16 * 2)
            for i in range(4):
                head_dve(dve, cv, N_KV + i, i, TILES, parts_k, kraw[:, 4 + i, :], G_K + 1 + i // 2,
                         k_t[:, i, :], atab[:, 0, :], atab[:, 1, :])
            barrier(dve, KV_BARRIER)
            for par in range(2):
                for g in range(2):
                    for v in range(2):
                        src = kraw[g * DH:(g + 1) * DH, 2 * v:2 * v + 2, 0:PT].rearrange(
                            "d g (c t y) -> d g t c y", t=8, y=2)[:, :, :, :, par]
                        dst = xp[par * DH:(par + 1) * DH, v, :, :, :].rearrange(
                            "d (q g) t c -> d q g t c", g=2)[:, :, g]
                        dve.tensor_copy(dst, src).then_inc(xp_ready, 1)
            dve.wait_ge(pos_ready, 1)
            cv.link(dve.tensor_tensor(cb[:, :, 1], ps[0:DH, 3, 0:4:2], cb[:, :, 0], ALU.add))
            dve.tensor_tensor(cb[:, :, 1], cb[:, :, 1], gain[0:DH, G_B1:G_B1 + 2], ALU.add
                              ).then_inc(bias_ready, 1)

            def compress(e, tiles, nc_, ch, out_k, out_v):
                for v in range(2):
                    dve.wait_ge(cp_p1, 2 * e + v + 1)
                    dve.tensor_tensor(
                        hid[:, v, :, 0:nc_],
                        ps[0:DH, v, 0:G * ch].rearrange("p (g c) -> p g c", g=G)[:, :, 0:nc_],
                        p1[:, v, 0:G * ch].rearrange("p (g c) -> p g c", g=G)[:, :, 1:nc_ + 1],
                        ALU.add).then_inc(cp_hid, 1)
                dve.wait_ge(cp_vc, e + 1)
                dve.tensor_copy(out_v, ps[0:nc_, 3, 0:256]).then_inc(vc_taken, 1)
                cos, sin_ = (ctab[:, j, 0:nc_].unsqueeze(1).to_broadcast([P, 2, nc_]) for j in range(2))
                dve.wait_ge(ck_ready, e + 1)
                head_dve(dve, cv, N_CMP + e, 4 + e, tiles, parts_k, ck[:, 0:2 * nc_], G_K, out_k, cos, sin_)

            compress(0, CMP_P, NC_P, 32, kc_p[:, :, :].rearrange("p g c -> p (g c)"), vc_p[:, :])

            def two(bp):
                for s in range(2):
                    b = 2 * bp + s
                    compress(b + 1, CMP_S, NC_S, 64, kc_s[:, ds(b, 1)].rearrange("p o g c -> p (o g c)"),
                             vc_s[:, ds(b, 1)].rearrange("p o c -> p (o c)"))
            cv.loop(SB // 2, 8, two)

        def kv_pool(pool, cg):
            pool.wait_ge(free[0], F0["kv"])
            pool.wait_ge(free[1], F1["kv"])
            for t, name in ((atab, "atab"), (ctab, "ctab")):
                pool.dma_start(t[:], a[name]).then_inc(kv_tabs, 16)
            pool.wait_ge(free[0], F0["kv"] + 4)
            pool.wait_ge(free[1], F1["kv"] + 4)
            pool.dma_start(o["kv_fm"][:, 0:4, :], kraw[:, 0:4, :]).then_inc(kv_sent, 16)
            barrier(pool, KV_BARRIER)
            for t, name in ((w1, "w1"), (w2, "w2"), (pe_t, "pe")):
                pool.dma_start(t[:], a[name]).then_inc(kv_tabs, 16)
            pool.dma_start(o["kv_fm"][:, 4:8, :], k_t[:, :, :]).then_inc(kv_sent, 16)
            pool.dma_start(o["kv_tok"][:, 0:4, :], v_tok[:, 0:4, :]).then_inc(kv_sent, 16)
            pool.dma_start(o["kv_tok"][0:ST, 4, :], v_tok[0:ST, 4, :]).then_inc(kv_sent, 16)

            def batch(b, s, wait):
                if wait:
                    pool.wait_ge(cp_h, 2 * b)
                    pool.nop(nofuse=True)
                for j in range(NPG):
                    page = pool.value_load(pgt[0:1, ds(b * NPG + j, 1)], min_val=0, max_val=NPHYS - 1)
                    pool.dma_start(pgs[:, s, j, :], a["pages_cmp"][ds(page, 1)].rearrange("o p c -> p (o c)")
                                   ).then_inc(pin[s], 16)

            batch(0, 0, False)
            batch(1, 1, False)
            with pool.Fori(1, SB // 2) as bp:
                for s in range(2):
                    batch(2 * bp + s, s, True)

        UN, N_Q, I_Q = U0["nsa"], 23, 13
        gate_ready, gsel_done, gs_ready = sem("gates_ready"), sem("gate_rows_done"), sem("sample_gates_ready")
        gs_mid, gate_tabs, proj_done = sem("gates_masked"), sem("gate_tables_in"), sem("q_projected")

        def q_pe(pe):
            norm_pe(pe, N_Q - 1, 5)
            pe.wait_ge(xn_ready, 8 * 6)
            with pe.Fori(0, KT // 2) as i:
                for s in range(2):
                    unit_pe(pe, UN + 2 * i + s, s, (F0, F1)[s]["nsa"] + i, KT, xh_n, xl_n)
            for un in range(2):
                pe.wait_ge(lo_ready, UN + 9 + un)
                for kk in range(4):
                    k = 4 * un + kk
                    for t, (c0, m) in enumerate(TILES):
                        for n, (xx, w) in enumerate(((xh_n, wh), (xh_n, wl), (xl_n, wh))):
                            mm = pe.matmul(ps[0:m, 4, 48 * t:48 * t + 48], xx[:, k, c0:c0 + m],
                                           w[:, un, kk * 48:kk * 48 + 48], start=(k == t == n == 0),
                                           stop=(k == KT - 1 and n == 2), skip_group_check=True)
                mm.then_inc(w_used, 1)
            pe.wait_ge(gate_ready, 2)
            pe.wait_ge(gate_tabs, 16 * 2)
            for b in range(SB):
                mm = pe.matmul(ps[:, 5, 48 * b:48 * b + 48], sel_e[:, b, :], gt[0:ST, 4, :],
                               start=True, stop=True)
            mm.then_inc(gsel_done, 1)
            pe.wait_ge(gs_mid, 1)
            with pe.Fori(0, KT) as t:
                head_pe(pe, N_Q + t, I_Q + t, TILES, parts_n)

        def q_act(act, ca):
            norm_act(act, ca, N_Q - 1, 5, xh_n, "nsa")
            with act.Fori(0, KT // 2) as i:
                for s in range(2):
                    act.wait_ge(w_used, UN + 2 * i + s + 1)
                    act.activation(wide_d(q[:, ds(2 * i + s, 1), :]), bank2(2 * s), ACT.Copy
                                   ).then_inc(free[s], 1)
                    split_high(act, UN + 2 * i + s + 2, s, UA)
            split_high(act, UN + 10, 0, UA)
            split_high(act, UN + 11, 1, UA)
            act.activation(gt[:, 0:4, :], ps[:, 4, 0:192].rearrange("p (t c) -> p t c", t=4), ACT.Sigmoid
                           ).then_inc(gate_ready, 1)
            act.activation(gt[0:ST, 4, :], ps[0:ST, 4, 192:240], ACT.Sigmoid).then_inc(gate_ready, 1)
            act.wait_ge(free[0], F0["nsa"] + 4)
            act.wait_ge(free[1], F1["nsa"] + 4)
            ca.loop(KT, 1, lambda t: head_act(act, ca, N_Q + t, q[:, ds(t, 1), :].rearrange("p o c -> p (o c)"),
                                              NT))

        def q_dve(dve, cv):
            norm_dve(dve, cv, N_Q - 1, 5, xh_n, xl_n, G_NSA)
            for i in range(10):
                split_low(dve, UN + 2 + i, i % 2, UA)
            dve.wait_ge(gsel_done, 1)
            dve.tensor_tensor(gw[:, :, :], ps[:, 5, 0:384].rearrange("p (b c) -> p b c", b=SB),
                              sel_m[:, :].unsqueeze(1).to_broadcast([P, SB, 48]), ALU.mult).then_inc(gs_mid, 1)
            dve.wait_ge(gs_mid, 1)
            dve.tensor_reduce(gs[:, :, :], gw[:, :, :].rearrange("p b (h r) -> p b r h", r=3), AX_X, ALU.add
                              ).then_inc(gs_ready, 1)

            def tile(t):
                row = q[:, ds(t, 1), :].rearrange("p o c -> p (o c)")
                head_dve(dve, cv, N_Q + t, I_Q + t, TILES, parts_n, row, G_Q, row, atab[:, 0, :], atab[:, 1, :])
            cv.loop(KT, 6, tile)

        att_in = sem("attention_tables_in")
        (qs_ready, cs_done, cx_ready, cx_exp, cp_ready, ct_done, ct_v, ct_a, cv_done, ot_ready, tr_done, tr_mid,
         tr_taken) = (sem(f"cmp_{n}") for n in (
             "q_pair_ready", "scores_done", "shifted", "exp_done", "probs_ready", "probs_turned",
             "turned_taken_v", "turned_taken_a", "o_done", "o_taken", "o_turned", "o_high", "o_split"))
        a_s, a_mx, a_exp, a_t, a_ptv, a_pta, a_v, a_o = (sem(f"att_{n}") for n in (
            "scores_done", "max_ready", "exp_done", "probs_turned", "turned_taken_v", "turned_taken_a",
            "o_done", "o_added"))

        def unit(n):
            return n % 2, n // 2

        def att_pe(pe):
            def turn(gp, s, T):
                def scores(n):
                    g, i = unit(n)
                    pe.wait_ge(a_exp, 8 * T + max(n - 1, 0))
                    lo = DH * g
                    for j in range(2):
                        mm = pe.matmul(ps[:, 2 * (n % 2) + j, 0:P * (i + 1)],
                                       qst[lo:lo + DH, s, i * P:(i + 1) * P],
                                       k_t[lo:lo + DH, 2 * j + gp, 0:P * (i + 1)], start=True, stop=True)
                    mm.then_inc(a_s, 1)

                def turned(n):
                    g, i = unit(n)
                    pe.wait_ge(a_exp, 8 * T + n + 1)
                    pe.wait_ge(a_ptv, 8 * T + n)
                    pe.wait_ge(a_pta, 8 * T + n)
                    if n == 0:
                        pe.wait_ge(ct_v, T + 1)
                        pe.wait_ge(ct_a, T + 1)
                    for j in range(2):
                        for k in range(i + 1):
                            mm = pe.transpose(ps[:, 5 + j, k * P:(k + 1) * P],
                                              pr[:, n % 2, 512 * j + k * P:512 * j + (k + 1) * P], ident)
                    mm.then_inc(a_t, 1)

                def values(n):
                    g, i = unit(n)
                    pe.wait_ge(a_ptv, 8 * T + n + 1)
                    pe.wait_ge(a_pta, 8 * T + n + 1)
                    pe.wait_ge(a_o, 8 * T + n)
                    for j in range(2):
                        for k in range(i + 1):
                            c0 = 256 * j + (2 * gp + g) * DH
                            mm = pe.matmul(ps[:, 7, j * DH:(j + 1) * DH],
                                           prt[:, n % 2, 512 * j + k * P:512 * j + (k + 1) * P],
                                           v_tok[:, k, c0:c0 + DH], start=(k == 0), stop=(k == i))
                    mm.then_inc(a_v, 1)

                pe.wait_ge(qs_ready, T + 1)
                pe.wait_ge(tr_taken, T)
                pe.wait_ge(a_o, 8 * T)
                pe.nop(nofuse=True)
                for g in range(2):
                    for i in range(4):
                        mm = pe.matmul(ps[:, 4 + 3 * g, i * NC_P:(i + 1) * NC_P], qst[DH * g:DH * (g + 1), s, i * P:(i + 1) * P],
                                       kc_p[DH * g:DH * (g + 1), gp, :], start=True, stop=True)
                mm.then_inc(cs_done, 1)
                scores(0)
                scores(1)
                pe.wait_ge(cp_ready, T + 1)
                for g in range(2):
                    for i in range(4):
                        mm = pe.transpose(ps[0:NC_P, 5 + g, i * P:(i + 1) * P], pc[:, 4 * g + i, :], ident)
                mm.then_inc(ct_done, 1)
                pe.wait_ge(ct_v, T + 1)
                pe.wait_ge(ct_a, T + 1)
                for i in range(4):
                    for g in range(2):
                        c0 = i * P + g * DH
                        mm = pe.matmul(ps[:, 4, c0:c0 + DH], pct[:, g, i * P:(i + 1) * P],
                                       vc_p[:, (2 * gp + g) * DH:(2 * gp + g + 1) * DH], start=True, stop=True)
                mm.then_inc(cv_done, 1)
                for n in range(8):
                    turned(n)
                    if n:
                        values(n - 1)
                    if n + 2 < 8:
                        scores(n + 2)
                values(7)
                pe.wait_ge(a_o, 8 * T + 8)
                pe.wait_ge(ot_ready, T + 1)
                for i in range(4):
                    mm = pe.transpose(ps[:, 4, i * P:(i + 1) * P], ot[:, i, :], ident)
                mm.then_inc(tr_done, 1)

            for gp in range(2):
                with pe.Fori(0, 2) as hh:
                    for s in range(2):
                        turn(gp, s, 4 * gp + 2 * hh + s)

        def att_act(act, ca):
            def turn(gp, s, T):
                def probs(n):
                    g, i = unit(n)
                    act.wait_ge(a_mx, 8 * T + n + 1)
                    act.wait_ge(a_t, 8 * T + max(n - 1, 0))
                    w = P * (i + 1)
                    for j in range(2):
                        ins = act.activation(pr[:, n % 2, 512 * j:512 * j + w], ps[:, 2 * (n % 2) + j, 0:w],
                                             ACT.Exp, bias=stat[:, n % 2, 1, j:j + 1], scale=SCALE,
                                             accum_out=sums[:, n % 4, j:j + 1])
                    ins.then_inc(a_exp, 1)

                act.wait_ge(cx_ready, T + 1)
                act.activation(pc[:, :, :], pc[:, :, :], ACT.Exp, scale=SCALE).then_inc(cx_exp, 1)
                probs(0)
                probs(1)
                act.wait_ge(ct_done, T + 1)
                act.activation(pct[:, 1, :], ps[0:NC_P, 6, :], ACT.Copy).then_inc(ct_a, 1)
                for n in range(8):
                    g, i = unit(n)
                    act.wait_ge(a_t, 8 * T + n + 1)
                    act.wait_ge(a_v, 8 * T + max(n - 1, 0))
                    w = P * (i + 1)
                    act.activation(prt[:, n % 2, 512:512 + w], ps[:, 6, 0:w], ACT.Copy).then_inc(a_pta, 1)
                    if n + 2 < 8:
                        probs(n + 2)

            for gp in range(2):
                with act.Fori(0, 2) as hh:
                    for s in range(2):
                        turn(gp, s, 4 * gp + 2 * hh + s)

        def att_dve(dve, cv):
            def turn(gp, s, T):
                def maxima(n):
                    g, i = unit(n)
                    dve.wait_ge(a_s, 8 * T + n + 1)
                    two = ps[:, 2 * (n % 2):2 * (n % 2) + 2, :]
                    cv.link(dve.tensor_tensor(two[:, :, i * P:(i + 1) * P], two[:, :, i * P:(i + 1) * P],
                                              causal[:, :].unsqueeze(1).to_broadcast([P, 2, P]), ALU.add))
                    cv.link(dve.tensor_reduce(stat[:, n % 2, 0, :], two[:, :, 0:P * (i + 1)], AX_X, ALU.max))
                    dve.tensor_scalar(stat[:, n % 2, 1, :], stat[:, n % 2, 0, :], -SCALE, None, ALU.mult
                                      ).then_inc(a_mx, 1)

                def gate(r0, n):
                    return gt[:, n // 2, ds(6 * T + 3 * (n % 2) + r0, 2)]

                def add(n):
                    g, i = unit(n)
                    dve.wait_ge(a_exp, 8 * T + n + 1)
                    cv.link(dve.reciprocal(ls[:, n % 2, :], sums[:, n % 4, :]))
                    cv.link(dve.tensor_tensor(ls[:, n % 2, :], ls[:, n % 2, :], gate(1, n), ALU.mult))
                    dve.wait_ge(a_v, 8 * T + n + 1)
                    to = ot[:, i, g * DH:(g + 1) * DH]
                    cv.link(dve.scalar_tensor_tensor(to, ps[:, 7, 0:DH], ls[:, n % 2, 0:1], to,
                                                     ALU.mult, ALU.add))
                    dve.scalar_tensor_tensor(to, ps[:, 7, DH:2 * DH], ls[:, n % 2, 1:2], to,
                                             ALU.mult, ALU.add).then_inc(a_o, 1)

                def eight(t):
                    return t.rearrange("p (g i) c -> p g i c", g=2)

                def over(t, k):
                    return t[:, k].unsqueeze(1).to_broadcast([P, 2, 4, NC_P])

                dve.wait_ge(cs_done, T + 1)
                cv.link(dve.tensor_tensor(
                    eight(pc[:, :, :]), ps[:, 4:8:3, 0:4 * NC_P].rearrange("p g (i c) -> p g i c", i=4),
                    over(cmask, 0), ALU.add))
                cv.link(dve.tensor_reduce(c8[:, 0, :], pc[:, :, :], AX_X, ALU.max))
                dve.tensor_tensor(pc[:, :, :], pc[:, :, :], c8[:, 0, :].unsqueeze(2).to_broadcast([P, 8, NC_P]),
                                  ALU.subtract).then_inc(cx_ready, 1)
                maxima(0)
                maxima(1)
                dve.wait_ge(cx_exp, T + 1)
                cv.link(dve.tensor_reduce(c8[:, 0, :], pc[:, :, :], AX_X, ALU.add))
                cv.link(dve.reciprocal(c8[:, 1, :], c8[:, 0, :]))
                cv.step(dve.tensor_tensor(
                    c8[:, 2, :].rearrange("p (g i) -> p g i", g=2),
                    c8[:, 1, :].rearrange("p (g i) -> p g i", g=2),
                    gt[:, 0:4, ds(6 * T, 6)].rearrange("p i (g r) -> p g i r", g=2)[:, :, :, 0], ALU.mult))
                cv.link(dve.tensor_tensor(eight(pc[:, :, :]), eight(pc[:, :, :]), over(cmask, 1), ALU.mult))
                dve.tensor_tensor(pc[:, :, :], pc[:, :, :], c8[:, 2, :].unsqueeze(2).to_broadcast([P, 8, NC_P]),
                                  ALU.mult).then_inc(cp_ready, 1)
                dve.wait_ge(ct_done, T + 1)
                dve.tensor_copy(pct[:, 0, :], ps[0:NC_P, 5, :]).then_inc(ct_v, 1)
                dve.wait_ge(cv_done, T + 1)
                dve.wait_ge(tr_done, T)
                dve.tensor_copy(ot[:, :, :], ps[:, 4, :].rearrange("p (i c) -> p i c", i=4)).then_inc(ot_ready, 1)
                dve.wait_ge(ot_ready, T + 1)
                for n in range(8):
                    g, i = unit(n)
                    dve.wait_ge(a_t, 8 * T + n + 1)
                    dve.wait_ge(a_v, 8 * T + max(n - 1, 0))
                    dve.tensor_copy(prt[:, n % 2, 0:P * (i + 1)], ps[:, 5, 0:P * (i + 1)]).then_inc(a_ptv, 1)
                    if n:
                        add(n - 1)
                    if n + 2 < 8:
                        maxima(n + 2)
                add(7)
                dve.wait_ge(tr_done, T + 1)
                row = ah[:, ds(T, 1), 0:PT].rearrange("p o c -> p (o c)")
                dve.tensor_copy(row, ps[:, 4, :]).then_inc(tr_mid, 1)
                dve.wait_ge(tr_mid, T + 1)
                dve.tensor_tensor(al[:, ds(T, 1), 0:PT].rearrange("p o c -> p (o c)"), ps[:, 4, :],
                                  row.bitcast(F32), ALU.subtract).then_inc(tr_taken, 1)

            for gp in range(2):
                def two(hh):
                    for s in range(2):
                        turn(gp, s, 4 * gp + 2 * hh + s)
                cv.loop(2, 2 * (2 + 4 + 8 * 2 + 8 * 3), two)

        def att_pool(pool):
            for gp in range(2):
                with pool.Fori(0, 2) as hh:
                    for s in range(2):
                        T = 4 * gp + 2 * hh + s
                        pool.wait_ge(a_s, 8 * T)
                        pool.nop(nofuse=True)
                        pool.tensor_copy(qst[:, s, :], q[:, ds(T, 1), 0:PT].rearrange("p o c -> p (o c)")
                                         ).then_inc(qs_ready, 1)

        kin, vin, win_in, smp_tabs = (sem(n) for n in ("k_pages_in", "v_pages_in", "window_in", "sample_tables_in"))
        win_sent, qb_ready, vb_ready = sem("window_sent"), sem("batch_q_ready"), sem("batch_vc_ready")
        (b_c, b_cm, b_cexp, b_cp, b_ct, b_ctk, b_imp, b_s, b_mx, b_exp, b_t1, b_t1v, b_t1a, b_v1, b_t2, b_t2v,
         b_t2a, b_v2, b_o, b_ot, b_otk) = (sem(f"sample_{n}") for n in (
             "cmp_scores", "cmp_max", "cmp_exp", "cmp_probs", "cmp_turned", "cmp_taken", "importance", "scores",
             "max", "exp", "turned1", "taken1_v", "taken1_a", "values1", "turned2", "taken2_v", "taken2_a",
             "values2", "o_ready", "o_turned", "o_taken"))

        def smp_pe(pe):
            def batch(b):
                pe.wait_ge(qb_ready, b + 1)
                pe.wait_ge(b_otk, 2 * b)
                pe.nop(nofuse=True)
                for g in range(2):
                    mm = pe.matmul(ps[64 * g:64 * g + 64, 5, 0:NC_S], qbd[:, g, :], kcs[:, g, :],
                                   start=True, stop=True)
                mm.then_inc(b_c, 1)
                pe.wait_ge(kin, 16 * NPG * (b + 1))
                pe.wait_ge(b_o, b)
                pe.nop(nofuse=True)
                for g in range(2):
                    for h in range(2):
                        pe.matmul(ps[64 * g:64 * g + 64, h, :], qbd[:, g, :], kp[:, 4 * h:4 * h + 4, g, :],
                                  start=True, stop=True)
                    pe.matmul(ps[64 * g:64 * g + 64, 2, 0:ST], qbd[:, g, :], k_t[:, g, PT:NT],
                              start=True, stop=True)
                pe.wait_ge(win_in, 32 * (b + 1))
                pe.nop(nofuse=True)
                for g in range(2):
                    pe.matmul(ps[64 * g:64 * g + 64, 3, :], qbd[:, g, :], kw[:, g, :], start=True, stop=True)
                    mm = pe.matmul(ps[64 * g:64 * g + 64, 4, 0:ST], qbd[:, g, :], k_t[:, 2 + g, PT:NT],
                                   start=True, stop=True)
                mm.then_inc(b_s, 1)
                pe.wait_ge(b_cp, b + 1)
                pe.matmul(ps[0:NC_S, 5, 64:192], pcs[:, :], same, start=True, stop=True)
                pe.transpose(ps[0:NC_S, 5, 256:384], pcs[:, :], ident).then_inc(b_ct, 1)
                pe.wait_ge(b_ctk, 2 * b + 2)
                pe.matmul(ps[:, 5, 192:206], small[0:NC_S, 0, :], ovl[:, :], start=True, stop=True
                          ).then_inc(b_imp, 1)
                pe.wait_ge(b_exp, b + 1)
                pe.wait_ge(b_t2v, 2 * b)
                pe.wait_ge(b_t2a, b)
                for k in range(8):
                    mm = pe.transpose(ps[:, 6 + k // 4, k % 4 * P:(k % 4 + 1) * P], ps_[:, k * P:(k + 1) * P],
                                      ident)
                mm.then_inc(b_t1, 1)
                pe.wait_ge(vb_ready, b + 1)
                pe.matmul(ps[:, 2, 0:256], small[0:NC_S, 1, :], vcs[:, :], start=True, stop=True)
                pe.wait_ge(vin, 16 * NPG * (b + 1))
                pe.wait_ge(b_t1v, b + 1)
                pe.wait_ge(b_t1a, b + 1)
                for k in range(8):
                    mm = pe.matmul(ps[:, 0, 0:256], pst[:, k, :], vp[:, k, :], start=(k == 0), stop=False)
                mm.then_inc(b_v1, 1)
                for k in range(4):
                    pe.transpose(ps[:, 6, k * P:(k + 1) * P], ps_[:, 1088 + k * P:1088 + (k + 1) * P], ident)
                pe.transpose(ps[0:ST, 7, 0:P], ps_[:, 1024:1088], ident)
                pe.transpose(ps[0:ST, 7, P:2 * P], ps_[:, 1600:1664], ident).then_inc(b_t2, 1)
                pe.wait_ge(b_t2v, 2 * b + 2)
                pe.wait_ge(b_t2a, b + 1)
                pe.matmul(ps[:, 0, 0:256], small[:, 0, :], v_tok[0:ST, 4, 0:256], start=False, stop=True)
                for k in range(4):
                    pe.matmul(ps[:, 1, 0:256], pst[:, k, :], vw[:, k, :], start=(k == 0), stop=False)
                pe.matmul(ps[:, 1, 0:256], small[:, 2, :], v_tok[0:ST, 4, 256:512], start=False, stop=True
                          ).then_inc(b_v2, 1)
                pe.wait_ge(b_o, b + 1)
                pe.nop(nofuse=True)
                pe.transpose(ps[0:DH, 5, 0:P], oa[:, :], ident).then_inc(b_ot, 1)

            pe.wait_ge(smp_tabs, 16 * 4)
            with pe.Fori(0, SB) as b:
                batch(b)

        def smp_act(act):
            def batch(b):
                act.wait_ge(b_cm, b + 1)
                act.activation(pcs[:, :], ps[:, 5, 0:NC_S], ACT.Exp, bias=sst2[:, 1:2], scale=SCALE,
                               accum_out=sst2[:, 2:3]).then_inc(b_cexp, 1)
                act.wait_ge(b_mx, b + 1)
                act.activation(ps_[:, 0:1088], ps[:, 0:3, :].rearrange("p b c -> p (b c)")[:, 0:1088], ACT.Exp,
                               bias=sst2[:, 6:7], scale=SCALE, accum_out=sst2[:, 8:9])
                act.activation(ps_[:, 1088:1664], ps[:, 3:5, :].rearrange("p b c -> p (b c)")[:, 0:576], ACT.Exp,
                               bias=sst2[:, 7:8], scale=SCALE, accum_out=sst2[:, 9:10]).then_inc(b_exp, 1)
                act.wait_ge(b_t1, b + 1)
                act.activation(pst[:, 4:8, :], ps[:, 7, :].rearrange("p (k c) -> p k c", k=4), ACT.Copy
                               ).then_inc(b_t1a, 1)
                act.wait_ge(b_t2, b + 1)
                act.activation(small[:, 0, :], ps[0:ST, 7, 0:P], ACT.Copy)
                act.activation(small[:, 2, :], ps[0:ST, 7, P:2 * P], ACT.Copy).then_inc(b_t2a, 1)

            with act.Fori(0, SB) as b:
                batch(b)

        def smp_dve(dve, cv):
            dve.memset(drop[:, :], 0.0).then_inc(drop_set, 1)
            dve.wait_ge(drop_set, 1)
            dve.wait_ge(smp_tabs, 16 * 4)
            slc = ps[:, 0:3, :].rearrange("p b c -> p (b c)")
            win = ps[:, 3:5, :].rearrange("p b c -> p (b c)")

            def batch(b):
                dve.wait_ge(b_c, b + 1)
                cv.link(dve.tensor_reduce(sst2[:, 0:1], ps[:, 5, 0:NC_S], AX_X, ALU.max))
                dve.tensor_scalar(sst2[:, 1:2], sst2[:, 0:1], -SCALE, None, ALU.mult).then_inc(b_cm, 1)
                dve.wait_ge(b_s, b + 1)
                new = smask[:, ds(b, 1), :].rearrange("p o c -> p (o c)")
                cv.step(dve.tensor_tensor(slc[:, 1024:1088], slc[:, 1024:1088], new, ALU.add))
                cv.step(dve.tensor_tensor(win[:, 512:576], win[:, 512:576], new, ALU.add))
                cv.link(dve.tensor_tensor(win[:, 0:SQ], win[:, 0:SQ], wmask[:, :], ALU.add))
                cv.step(dve.tensor_reduce(sst2[:, 5:6], win[:, 0:576], AX_X, ALU.max))
                dve.wait_ge(b_cexp, b + 1)
                cv.link(dve.reciprocal(sst2[:, 3:4], sst2[:, 2:3]))
                dve.tensor_scalar(pcs[:, :], pcs[:, :], sst2[:, 3:4], None, ALU.mult).then_inc(b_cp, 1)
                dve.wait_ge(b_ct, b + 1)
                dve.tensor_copy(small[0:NC_S, 0, :], ps[0:NC_S, 5, 64:192]).then_inc(b_ctk, 1)
                dve.tensor_copy(small[0:NC_S, 1, :], ps[0:NC_S, 5, 256:384]).then_inc(b_ctk, 1)
                dve.wait_ge(b_imp, b + 1)
                cv.link(dve.tensor_reduce(sst2[:, 10:11], ps[:, 5, 192:206], AX_X, ALU.min))
                cv.link(dve.scalar_tensor_tensor(dtmp[:, 0, :], ps[:, 5, 192:206], sst2[:, 10:11], iot[:, :],
                                                 ALU.is_equal, ALU.mult))
                cv.link(dve.tensor_reduce(sst2[:, 11:12], dtmp[:, 0, :], AX_X, ALU.max))
                cv.link(dve.tensor_scalar(drop[:, 1:15], iot[:, :], sst2[:, 11:12], NEG, ALU.is_equal, ALU.mult))
                past = slc[:, 0:PAST].rearrange("p (s t) -> p s t", s=NSEL)
                cv.link(dve.tensor_tensor(past, past, drop[:, :].unsqueeze(2).to_broadcast([P, NSEL, SEL]),
                                          ALU.add))
                cv.link(dve.tensor_reduce(sst2[:, 4:5], slc[:, 0:1088], AX_X, ALU.max))
                dve.tensor_scalar(sst2[:, 6:8], sst2[:, 4:6], -SCALE, None, ALU.mult).then_inc(b_mx, 1)
                dve.wait_ge(b_exp, b + 1)
                cv.link(dve.reciprocal(sst2[:, 12:14], sst2[:, 8:10]))
                cv.step(dve.tensor_tensor(sst2[:, 14:16], sst2[:, 12:14],
                                          gs[:, ds(b, 1), 1:3].rearrange("p o c -> p (o c)"), ALU.mult))
                dve.wait_ge(b_t1, b + 1)
                dve.tensor_copy(pst[:, 0:4, :], ps[:, 6, :].rearrange("p (k c) -> p k c", k=4)).then_inc(b_t1v, 1)
                dve.wait_ge(b_t2, b + 1)
                dve.tensor_copy(pst[:, 0:2, :], ps[:, 6, 0:256].rearrange("p (k c) -> p k c", k=2)
                                ).then_inc(b_t2v, 1)
                dve.tensor_copy(pst[:, 2:4, :], ps[:, 6, 256:512].rearrange("p (k c) -> p k c", k=2)
                                ).then_inc(b_t2v, 1)
                dve.wait_ge(b_v2, b + 1)
                for n, (bank, col) in enumerate(((2, gs[:, ds(b, 1), 0:1].rearrange("p o c -> p (o c)")),
                                                 (0, sst2[:, 14:15]), (1, sst2[:, 15:16]))):
                    for g in range(G):
                        rows = slice(32 * g, 32 * g + 32)
                        src = ps[rows, bank, g * DH:(g + 1) * DH]
                        if n == 0:
                            ins = dve.tensor_scalar(oa[rows, :], src, col[rows], None, ALU.mult)
                        else:
                            ins = dve.scalar_tensor_tensor(oa[rows, :], src, col[rows], oa[rows, :],
                                                           ALU.mult, ALU.add)
                        if n == 2 and g == G - 1:
                            ins.then_inc(b_o, 1)
                        else:
                            cv.step(ins)
                    if n < 2:
                        cv.wait()
                dve.wait_ge(b_ot, b + 1)
                for g in range(2):
                    dve.tensor_copy(
                        os_[g * DH:(g + 1) * DH, :, ds(b * SQ, SQ)].rearrange("d (p h) q -> d p h q", p=2),
                        ps[0:DH, 5, 0:P].rearrange("d (p g h q) -> d p g h q", p=2, g=2, h=HG)[:, :, g]
                    ).then_inc(b_otk, 1)

            cv.loop(SB, 1 + 4 + 1 + 6 + 2 + 11, batch)
            dve.wait_ge(b_otk, 2 * SB)
            cv.link(dve.tensor_copy(ah[:, :, PT:NT], os_[:, :, :]))
            cv.step(dve.tensor_tensor(al[:, :, PT:NT], os_[:, :, :], ah[:, :, PT:NT].bitcast(F32), ALU.subtract))

        def smp_pool(pool, cg):
            for t, name in ((smask, "smask"), (wmask, "wmask"), (iot, "iot"), (ovl, "ovl")):
                pool.dma_start(t[:], a[name]).then_inc(smp_tabs, 16)
            cg.link(pool.memset(qbd[:, :, :], 0.0))

            def batch(b):
                pool.wait_ge(b_s, b)
                pool.nop(nofuse=True)
                for j in range(NPG):
                    page = pool.value_load(pgt[0:1, ds(b * NPG + j, 1)], min_val=0, max_val=NPHYS - 1)
                    pool.dma_start(kp[:, j, :, :].rearrange("p g c -> p (g c)"),
                                   a["pages_k"][ds(page, 1)].rearrange("o p c -> p (o c)")).then_inc(kin, 16)
                for g in range(2):
                    rows = slice(g * DH, (g + 1) * DH)
                    cg.link(pool.tensor_copy(
                        qbd[rows, :, 32 * g:32 * g + 32].rearrange("p t (h q) -> p t h q", h=HG),
                        q[rows, :, ds(PT + b * SQ, SQ)].rearrange("p (t h) q -> p t h q", t=2)))
                pool.tensor_copy(kcs[:, :, :], kc_s[:, ds(b, 1)].rearrange("p o g c -> p (o g) c")
                                 ).then_inc(qb_ready, 1)
                pool.wait_ge(b_v2, b)
                pool.wait_ge(win_sent, 32 * b)
                pool.wait_ge(qb_ready, b + 1)
                pool.nop(nofuse=True)
                pool.tensor_copy(vcs[:, :], vc_s[:, ds(b, 1), :].rearrange("p o c -> p (o c)")
                                 ).then_inc(vb_ready, 1)
                pool.dma_start(kw[:, :, :], a["win_k"][ds(b, 1)].rearrange("o p g c -> p (o g) c")
                               ).then_inc(win_in, 16)
                pool.dma_start(vw[:, :, :], a["win_v"][ds(b, 1)].rearrange("o p g c -> p (o g) c")
                               ).then_inc(win_in, 16)
                for j in range(NPG):
                    page = pool.value_load(pgt[0:1, ds(b * NPG + j, 1)], min_val=0, max_val=NPHYS - 1)
                    pool.dma_start(vp[:, j, :], a["pages_v"][ds(page, 1)].rearrange("o p c -> p (o c)")
                                   ).then_inc(vin, 16)
                pool.wait_ge(win_in, 32 * (b + 1))
                pool.nop(nofuse=True)
                pool.dma_start(o["win_k"][ds(b, 1)].rearrange("o p g c -> p (o g) c"), kw[:, :, :]
                               ).then_inc(win_sent, 16)
                pool.dma_start(o["win_v"][ds(b, 1)].rearrange("o p g c -> p (o g) c"), vw[:, :, :]
                               ).then_inc(win_sent, 16)

            cg.loop(SB, 2, batch)
            pool.wait_ge(win_sent, 32 * SB)

        drop_set = sem("drop_cleared")

        def nsa_pe(pe):
            q_pe(pe)
            barrier(pe, ATT_BARRIER)
            pe.wait_ge(att_in, 16)
            att_pe(pe)
            barrier(pe, ATT_BARRIER + 1)
            smp_pe(pe)
            barrier(pe, ATT_BARRIER + 2)
            for i in range(8):
                unit_pe(pe, UN + 10 + i, i % 2, (F0, F1)[i % 2]["nsa"] + 4 + i // 2, KT, ah, al)

        def nsa_act(act, ca):
            q_act(act, ca)
            barrier(act, ATT_BARRIER)
            att_act(act, ca)
            barrier(act, ATT_BARRIER + 1)
            smp_act(act)
            barrier(act, ATT_BARRIER + 2)
            for i in range(8):
                split_high(act, UN + 12 + i, i % 2, UA)

        def nsa_dve(dve, cv):
            q_dve(dve, cv)
            barrier(dve, ATT_BARRIER)
            dve.wait_ge(att_in, 16)
            att_dve(dve, cv)
            barrier(dve, ATT_BARRIER + 1)
            smp_dve(dve, cv)
            barrier(dve, ATT_BARRIER + 2)
            for i in range(8):
                dve.wait_ge(w_used, UN + 11 + i)
                t = wide(x[:, i, :])
                dve.tensor_tensor(t, t, bank2(2 * (i % 2)), ALU.add).then_inc(free[i % 2], 1)
                split_low(dve, UN + 12 + i, i % 2, UA)

        def nsa_pool(pool, cg):
            pool.wait_ge(free[0], F0["nsa"])
            pool.wait_ge(free[1], F1["nsa"])
            pool.dma_start(sel_e[:], a["sel_e"]).then_inc(gate_tabs, 16)
            pool.dma_start(sel_m[:], a["sel_m"]).then_inc(gate_tabs, 16)
            barrier(pool, ATT_BARRIER)
            pool.dma_start(cmask[:], a["cmask"]).then_inc(att_in, 16)
            att_pool(pool)
            barrier(pool, ATT_BARRIER + 1)
            smp_pool(pool, cg)
            barrier(pool, ATT_BARRIER + 2)

        ROOTS = {"ffn0": 0, "ret": 1, "ffn1": 6, "kv": 7, "ffn2": 21, "nsa": 22, "ffn3": 31}
        NORMS = {s: i for i, s in enumerate(STAGES)}

        @block.sync
        def _(sp):
            for t, name in consts:
                sp.dma_start(t[:], a[name]).then_inc(consts_in, 16)

            def load(u, slot, src, size):
                if not (isinstance(u, int) and u < 2):
                    sp.wait_ge(lo_ready, u - 1)
                sp.dma_start(wf[:, slot, 0:size], src).then_inc(landed[slot], 16)

            def load_run(u0, first, count, src, size):
                def two(i, j):
                    for k in range(2):
                        load(u0 + 2 * i + k, k, src[ds(first + 2 * i + k, 1)].rearrange("o p c -> p (o c)"),
                             size)
                start = 0
                if u0 == 0:
                    two(0, 0)
                    start = 1
                with sp.Fori(start, count // 2) as i:
                    two(i, 0)

            ia = ib = 0
            for s in STAGES:
                if s.startswith("ffn"):
                    for h in range(2):
                        load_run(U0[s] + 30 * h, ia, 2 * FH, a["wa"], UA)
                        load_run(U0[s] + 30 * h + 2 * FH, ib, KT, a["wb"], UB)
                        ia, ib = ia + 2 * FH, ib + KT
                else:
                    load_run(U0[s], ia, UNITS[s], a["wa"], UA)
                    ia += UNITS[s]
            sp.wait_ge(free[0], F0_END)
            sp.wait_ge(free[1], F1_END)
            sp.dma_start(o["y"], x[:, :, :]).then_inc(out_done, 16)
            sp.wait_ge(out_done, 16)

        @block.tensor
        def _(pe):
            pe.wait_ge(consts_in, 16 * N_CONST)
            for s in STAGES:
                if s.startswith("ffn"):
                    ffn_pe(pe, int(s[3]), s, ROOTS[s], NORMS[s])
                if s == "ret":
                    ret_pe(pe)
                if s == "kv":
                    kv_pe(pe)
                if s == "nsa":
                    nsa_pe(pe)

        @block.scalar
        def _(act):
            ca = Chain(act, chain_a)
            split_high(act, 0, 0, UA, False)
            split_high(act, 1, 1, UA, False)
            for s in STAGES:
                if s.startswith("ffn"):
                    ffn_act(act, ca, int(s[3]), s, ROOTS[s], NORMS[s], s == STAGES[-1])
                if s == "ret":
                    ret_act(act, ca)
                if s == "kv":
                    kv_act(act, ca)
                if s == "nsa":
                    nsa_act(act, ca)

        @block.vector
        def _(dve):
            cv = Chain(dve, chain_v)
            dve.memset(st[:, :, :], 1.0).then_inc(st_set, 1)
            dve.wait_ge(st_set, 1)
            dve.wait_ge(consts_in, 16 * N_CONST)
            split_low(dve, 0, 0, UA)
            split_low(dve, 1, 1, UA)
            for s in STAGES:
                if s.startswith("ffn"):
                    ffn_dve(dve, cv, int(s[3]), s, ROOTS[s], NORMS[s], s == STAGES[-1])
                if s == "ret":
                    ret_dve(dve, cv)
                if s == "kv":
                    kv_dve(dve, cv)
                if s == "nsa":
                    nsa_dve(dve, cv)

        @block.gpsimd
        def _(pool):
            cg = Chain(pool, chain_g)
            for s in STAGES:
                if s == "ret":
                    ret_pool(pool, cg)
                if s == "kv":
                    kv_pool(pool, cg)
                if s == "nsa":
                    nsa_pool(pool, cg)
            pool.wait_ge(st_sent, 16 * RH)
            for i in range(4):
                pool.wait_ge(sout[i], 32 * RH)



def constants():
    f = np.float32
    c = {}
    eye = np.eye(P, dtype=f)
    rot = np.zeros((P, P), f)
    for b in range(0, P, DH):
        for i in range(DH // 2):
            rot[b + DH // 2 + i, b + i] = -1.0
            rot[b + i, b + DH // 2 + i] = 1.0
    row = np.arange(P)
    same = ((row[:, None] // 32 == row[None] // 32) & (row[:, None] % SQ == row[None] % SQ)).astype(f)
    c["mats"] = np.stack([np.full((P, P), 1 / DV, f), rot, eye, same], 1)
    mcol = np.zeros((P, 4), f)
    mcol[:, 0], mcol[:, 1] = 1 / D, 1 / DV
    mcol[:DH, 2] = mcol[DH:, 3] = 1 / DH
    c["mcol"] = mcol
    c["causal"] = np.where(row[None] <= row[:, None], 0, NEG).astype(f)
    pos = np.concatenate([np.arange(PT), np.tile(PAST + np.arange(SQ), SB)]).astype(f)

    def angles(width, at):
        inv = f(10000.0) ** (-np.arange(width // 2, dtype=f) / f(width // 2))
        ang = at[None, :].astype(f) * inv.astype(f)[:, None]
        return np.cos(ang).astype(f), np.sin(ang).astype(f)

    cos, sin = angles(DK, pos)
    c["rtab"] = np.stack([cos, sin], 1)
    cos, sin = angles(DH, pos)
    c["atab"] = np.stack([np.tile(cos, (4, 1)), np.tile(sin, (4, 1))], 1)
    cos, sin = angles(DH, (np.arange(NC_S) * 16 + 31).astype(f))
    c["ctab"] = np.stack([np.tile(cos, (4, 1)), np.tile(sin, (4, 1))], 1)
    lg = np.log(f(1.0) - f(2.0) ** (f(-5.0) - np.arange(RH, dtype=f))).astype(f)
    rel = (row[None, :] - row[:, None]).astype(f)
    dec = np.where(rel >= 0, np.exp(np.maximum(rel, 0)[None] * lg[:, None, None]), 0).astype(f)
    ks = f(DK ** -0.5)
    c["rdec"] = (dec * ks).transpose(1, 0, 2)
    c["rqdec"] = np.tile(np.exp((row + 1.0)[None, :].astype(f) * lg[:, None]).astype(f)[None], (P, 1, 1))
    tok = np.arange(ST)
    blk = (tok[:, None] // SQ == tok[None] // SQ)
    c["rsdec"] = np.where(blk[None], dec[:, tok % SQ][:, :, tok % SQ] * ks, 0).transpose(1, 0, 2)
    rcol = np.zeros((P, 4, RH), f)
    rcol[:, 0] = np.exp((CH - 1.0 - row)[:, None].astype(f) * lg[None]) * ks
    rcol[:, 1] = np.exp((SQ - 1.0 - row % SQ)[:, None].astype(f) * lg[None]) * ks
    rcol[:, 2], rcol[:, 3] = np.exp(f(CH) * lg), np.exp(f(SQ) * lg)
    c["rcol"] = rcol
    c["rbm"] = (tok[:, None] // SQ == np.arange(SB)[None])
    qpos = np.arange(PT).reshape(4, P).T
    valid = (np.arange(NC_P) * 16 + 31)[None, None, :] <= qpos[:, :, None]
    c["cmask"] = np.stack([np.where(valid, 0, NEG), valid], 1)
    sel_e = np.zeros((ST, SB, P), f)
    for b in range(SB):
        sel_e[b * SQ + row % SQ, b, row] = 1
    c["sel_e"] = sel_e
    sel_m = np.zeros((P, 16, 3), f)
    for i in row:
        g, hh = i // 32, i // SQ % HG
        sel_m[i, 2 * ((g // 2) * HG + hh) + g % 2] = 1
    c["sel_m"] = sel_m.reshape(P, 48)
    c["smask"] = np.where((tok[None, None] // SQ == np.arange(SB)[None, :, None])
                          & (tok[None, None] % SQ <= (row % SQ)[:, None, None]), 0, NEG)
    c["wmask"] = np.where(np.arange(SQ)[None] > (row % SQ)[:, None], 0, NEG)
    c["iot"] = np.tile(np.arange(1, 15), (P, 1))
    ci, sj = np.arange(NC_S)[:, None], np.arange(1, 15)[None]
    c["ovl"] = (ci * 16 < (sj + 1) * SEL) & (ci * 16 + 32 > sj * SEL)
    return {k: np.ascontiguousarray(v, f) for k, v in c.items()}


def by_tile(v):
    return v.reshape(v.shape[:-1] + (-1, P)).swapaxes(-1, -2)


def blocks(w, nk=None):
    k, n = w.shape[0] // P, w.shape[1] // P
    return w.reshape(k, P, n, P).transpose(2, 1, 0, 3).reshape(n, P, k * P)


def by_rows(w, nk):
    k = w.shape[0] // P
    return w.reshape(k // nk, nk, P, -1).transpose(0, 2, 1, 3).reshape(k // nk, P, -1)


def layouts(v):
    d = {}
    xt = np.concatenate([v["x_prompt"].reshape(PT, D), v["x_sample"].reshape(ST, D)]).T
    d["x"] = xt.reshape(KT, P, NT).transpose(1, 0, 2)
    wi, wo = v["ffn_w_in"], v["ffn_w_out"]

    def ffn_in(f):
        w = wi.reshape(4, D, 2 * FF)[f]
        ab = np.stack([blocks(w[:, :FF]), blocks(w[:, FF:])], 1)
        return [ab.reshape(2 * FT, P, UA)]

    heads = [[(2 * gp + g) * HG + h for g in range(2)] for gp in range(2) for h in range(HG)]
    heads = np.array(heads).reshape(-1)
    qcol = (heads[:, None] * DH + np.arange(DH)).reshape(-1)
    gcol = D + (heads[:, None] * 3 + np.arange(3)).reshape(-1)
    rw, nw = v["ret_w_in"][0], v["nsa_w_in"][0]
    ret = []
    for h in range(RH):
        ret += [blocks(rw[:, h * DK:(h + 1) * DK]), blocks(rw[:, D + h * DK:D + (h + 1) * DK])]
        ret += [by_rows(rw[:, 2 * D + h * DV:2 * D + (h + 1) * DV], 2)]
        ret += [blocks(rw[:, 4 * D + h * DV:4 * D + (h + 1) * DV])]
        out = blocks(v["ret_w_out"][0][h * DV:(h + 1) * DV])
        ret += [out.reshape(4, 2, P, 4 * P).transpose(0, 2, 1, 3).reshape(4, P, UA)]
    kw = v["kv_w"].reshape(D, 6, 256)
    kv = [blocks(np.concatenate([kw[:, i] for i in (0, 1, 2, 4)], 1)),
          by_rows(np.concatenate([kw[:, 3], kw[:, 5]], 1), 2)]
    gates = np.zeros((2, P, UA), np.float32)
    gates[:, :, :4 * 48] = by_rows(nw[:, gcol], 4)
    nsa = [blocks(nw[:, qcol]), gates, blocks(v["nsa_w_out"][0][qcol])]
    d["wa"] = np.concatenate(ffn_in(0) + ret + ffn_in(1) + kv + ffn_in(2) + nsa + ffn_in(3))
    d["wb"] = np.concatenate([blocks(wo.reshape(4, FF, D)[f, h * FH * P:(h + 1) * FH * P])
                              for f in range(4) for h in range(2)])
    two = [np.concatenate([n, n])[:, None] for n in (*v["k_norm"], v["q_norm"][0])]
    b1 = np.zeros((P, 2), np.float32)
    b1[:DH] = v["cmp_b1"].T
    d["gain"] = np.concatenate(
        [by_tile(v["ffn_norm"].reshape(4, D)).transpose(1, 0, 2).reshape(P, 32), by_tile(v["ret_norm"][0]),
         by_tile(v["kv_norm"]), by_tile(v["nsa_norm"][0]), *two, b1], 1)
    d["state"] = v["state_ret"][0].reshape(SB, RH, 2, P, DV).transpose(1, 0, 3, 2, 4)
    d["w1"] = v["cmp_w1"].reshape(2, 2, 8, 2, DH, DH).transpose(3, 4, 0, 2, 1, 5).reshape(P, 2, 8, P)
    d["w2"] = v["cmp_w2"].transpose(1, 0, 2)
    d["pe"] = v["cmp_pe"].reshape(2, 2, 8, 2, DH).transpose(3, 4, 0, 2, 1).reshape(P, 2, 8, 2)
    pg = v["cache_kv"].reshape(NPHYS, 8, 8, 2, 4, G, DH)
    d["pages_cmp"] = pg[:, :, :, :, :2].transpose(0, 3, 6, 4, 5, 2, 1).reshape(NPHYS, P, 512)
    pg = v["cache_kv"]
    d["pages_k"] = pg[:, :, 2].reshape(NPHYS, PAGE, 2, 2, DH).transpose(0, 3, 4, 2, 1).reshape(NPHYS, P, 256)
    d["pages_v"] = pg[:, :, 3].reshape(NPHYS, PAGE, 256)
    cw = v["cache_win"]
    d["win_k"] = cw[:, :, 0].reshape(SB, WIN, 2, 2, DH).transpose(0, 3, 4, 2, 1).reshape(SB, P, 2, WIN)
    d["win_v"] = cw[:, :, 1].reshape(SB, 4, P, 256).transpose(0, 2, 1, 3)
    d["pt"] = v["page_table"].reshape(1, SB * NPG)
    return {k: np.ascontiguousarray(t) for k, t in d.items()}


OUTPUTS = {"y": (P, KT, NT), "state_p": (RH, P, 2, DV), "state_s": (RH, SB, P, 2, DV),
           "kv_fm": (P, 8, NT), "kv_tok": (P, 5, 512), "win_k": (SB, P, 2, WIN), "win_v": (SB, P, 4, 256)}


def kernel(**inputs):
    import concourse.bacc as bacc
    from concourse.bass_utils import run_bass_kernel_spmd

    v = {k: np.asarray(t) for k, t in inputs.items()}
    arrays = {f"in_{k}": t for k, t in {**constants(), **layouts(v)}.items()}
    nc = bacc.Bacc("TRN2", target_bir_lowering=False, num_devices=1)
    a = {k[3:]: nc.dram_tensor(k, t.shape, mybir.dt.from_np(t.dtype), kind="ExternalInput").ap()
         for k, t in arrays.items()}
    o = {k: nc.dram_tensor(f"out_{k}", s, F32, kind="ExternalOutput").ap() for k, s in OUTPUTS.items()}
    trunk_program(nc, a, o)
    res = run_bass_kernel_spmd(nc, [arrays], core_ids=[0]).results[0]
    return assemble({k: np.asarray(res[f"out_{k}"]) for k in OUTPUTS})


def assemble(res):
    y = res["y"].transpose(2, 1, 0).reshape(NT, D)
    fm = res["kv_fm"].transpose(2, 1, 0).reshape(NT, 4, G, DH)
    tok = res["kv_tok"].transpose(1, 0, 2).reshape(5 * P, 2, G, DH)[:NT]
    rows = np.stack([fm[:, 0], fm[:, 1], fm[:, 2], tok[:, 0]], 1)
    win = np.stack([fm[:, 3], tok[:, 1]], 1)
    old_k = res["win_k"].reshape(SB, 2, DH, 2, WIN).transpose(0, 4, 3, 1, 2).reshape(SB, WIN, G, DH)
    old_v = res["win_v"].transpose(0, 2, 1, 3).reshape(SB, WIN, G, DH)
    win_s = np.concatenate([np.stack([old_k, old_v], 2)[:, SQ:], win[PT:].reshape(SB, SQ, 2, G, DH)], 1)
    return (y[None, :PT], y[PT:].reshape(SB, SQ, D),
            res["state_p"].transpose(0, 2, 1, 3).reshape(1, 1, RH, DK, DV),
            res["state_s"].transpose(1, 0, 3, 2, 4).reshape(1, SB, RH, DK, DV),
            rows[None, :PT], rows[PT:].reshape(SB, SQ, 4, G, DH), win[None, :PT], win_s)
```

```python
from contextlib import ExitStack

import numpy as np

import concourse.bass as bass
from concourse import mybir

ALU = mybir.AluOpType
ACT = mybir.ActivationFunctionType
AX_X = mybir.AxisListType.X
F32 = mybir.dt.float32
F32R = mybir.dt.float32r
I32 = mybir.dt.int32
ds = bass.ds

P = 128
D = 1024
KT = D // P
PT, SB, SQ = 512, 8, 8
ST = SB * SQ
NT = PT + ST
HALF = NT // 2
FF = 2816
FT = FF // P
FH = FT // 2
RH, DK, DV = 4, 256, 512
CH = 128
NCH = PT // CH
DH, G, HG = 64, 4, 4
PAST, PAGE, NPHYS = 1024, 128, 80
NPG = PAST // PAGE
SEL = 64
NSEL = PAST // SEL
NC_P, NC_S = 31, 63
WIN = 512
EPS = 1e-6
NEG = -1e30
SCALE = DH ** -0.5

UA = KT * P
UB = FH * P

FFN_UNITS, FFN_USES = 2 * (2 * FH + KT), 2 * (FH + KT // 2)
RU, RU0, RU1 = 16, 9, 8
STAGES = ["ffn0", "ret", "ffn1", "kv", "ffn2", "nsa", "ffn3"]
UNITS = {"ret": RH * RU, "kv": 12, "nsa": 18}
USES = {"ret": (RH * RU0, RH * RU1), "kv": (5, 4), "nsa": (8, 8)}


def running(count):
    at, out = 0, {}
    for s in STAGES:
        out[s] = at
        at += count(s)
    return out, at


U0, _ = running(lambda s: UNITS.get(s, FFN_UNITS))
F0, F0_END = running(lambda s: USES.get(s, (FFN_USES,) * 2)[0])
F1, F1_END = running(lambda s: USES.get(s, (FFN_USES,) * 2)[1])

G_FFN, G_RET, G_KV, G_NSA, G_K, G_Q, G_B1, N_GAIN = 0, 32, 40, 48, 56, 59, 60, 62


class Chain:

    def __init__(self, eng, sem):
        self.eng, self.sem, self.base, self.n = eng, sem, 0, 0

    def step(self, ins):
        ins.then_inc(self.sem, 1)
        self.n += 1

    def wait(self):
        self.eng.wait_ge(self.sem, self.base + self.n)

    def link(self, ins):
        self.step(ins)
        self.wait()

    def loop(self, count, per, body):
        outer_base, outer_n = self.base, self.n
        with self.eng.Fori(0, count) as i:
            self.base, self.n = outer_base + outer_n + i * per, 0
            body(i)
            assert self.n == per, f"a turn of this loop takes {self.n} steps, not {per}"
        self.base, self.n = outer_base, outer_n + count * per


def trunk_program(nc, a, o):
    with ExitStack() as ctx:
        def sb(stack, name, shape, dt=F32):
            return stack.enter_context(nc.sbuf_tensor(name, shape, dt))

        def sem(name):
            return ctx.enter_context(nc.semaphore(name))

        x = sb(ctx, "x", [P, KT, NT])
        wf = sb(ctx, "w_staged", [P, 2, UB])
        wh = sb(ctx, "w_high", [P, 2, UB], F32R)
        wl = sb(ctx, "w_low", [P, 2, UB], F32R)
        gain = sb(ctx, "gain", [P, N_GAIN])
        mats = sb(ctx, "mats", [P, 4, P])
        ones_v, rot, ident, same = (mats[:, i, :] for i in range(4))
        mcol = sb(ctx, "mean_columns", [P, 4])
        causal = sb(ctx, "causal", [P, P])
        with ExitStack() as s:
            qh, ql = sb(s, "q_pair_h", [P, 2, PT], F32R), sb(s, "q_pair_l", [P, 2, PT], F32R)
        sq = sb(ctx, "squares", [P, 2, NT])
        xf = sb(ctx, "x_normed", [P, 2, NT])
        r = sb(ctx, "rstd", [P, NT])
        st = sb(ctx, "token_stats", [P, SB + 1, 5, 2])
        pgt = sb(ctx, "page_table", [1, SB * NPG], I32)
        rb = sb(ctx, "stats_broadcast", [P, 2, 5, P])

        with ExitStack() as s:
            xh_r, xl_r = sb(s, "xh_r", [P, KT, NT], F32R), sb(s, "xl_r", [P, KT, NT], F32R)
            oh_r, ol_r = sb(s, "oh_r", [P, 4, NT], F32R), sb(s, "ol_r", [P, 4, NT], F32R)
            rtab = sb(s, "ret_cos_sin", [P, 2, NT])
            rq, rk = sb(s, "ret_q", [P, 2, NT]), sb(s, "ret_k", [P, 2, NT])
            rqd = sb(s, "ret_q_decayed", [P, 2, NT])
            rv = sb(s, "ret_v", [P, 5, DV])
            ro = sb(s, "ret_o", [P, 4, NT])
            with ExitStack() as s2:
                kth, ktl = sb(s2, "k_by_token_h", [P, 2, DK], F32R), sb(s2, "k_by_token_l", [P, 2, DK], F32R)
            pm = sb(s, "rope_parts", [P, 2, NT])
            sg_r = sb(s, "silu_gate_r", [P, 2, NT])
            ssb = sb(s, "ret_scores_T", [P, 2, P])
            ktk = sb(s, "k_by_token", [P, 2, DK])
            kmh, kml = sb(s, "k_of_batch_h", [ST, 2, DK], F32R), sb(s, "k_of_batch_l", [ST, 2, DK], F32R)
            rsh, rsl = sb(s, "sample_v_h", [ST, DV], F32R), sb(s, "sample_v_l", [ST, DV], F32R)
            state = sb(s, "state", [P, 2, DV])
            sst = sb(s, "sample_state", [P, 4, 2, DV])
            rdec = sb(s, "ret_decay_T", [P, RH, P])
            rqdec = sb(s, "ret_q_decay", [P, RH, P])
            rsdec = sb(s, "ret_sample_decay_T", [ST, RH, ST])
            rcol = sb(s, "ret_columns", [P, 4, RH])
            rbm = sb(s, "batch_mask", [ST, SB])
        kvp = ExitStack()
        with kvp:
            k_t = sb(kvp, "k_T", [P, 4, NT])
            v_tok = sb(kvp, "v_tok", [P, 5, 512])
            kc_p = sb(kvp, "kc_prompt_T", [P, 2, NC_P])
            vc_p = sb(kvp, "vc_prompt", [NC_P, 256])
            kc_s = sb(kvp, "kc_sample_T", [P, SB, 2, NC_S])
            vc_s = sb(kvp, "vc_sample", [NC_S, SB, 256])
            atab = sb(kvp, "att_cos_sin", [P, 2, NT])
            ctab = sb(kvp, "cmp_cos_sin", [P, 2, NC_S])
            with ExitStack() as s:
                xh_f, xl_f = sb(s, "xh_f", [P, KT, NT], F32R), sb(s, "xl_f", [P, KT, NT], F32R)
                hh, hl = sb(s, "hh", [P, FH, NT], F32R), sb(s, "hl", [P, FH, NT], F32R)
                sg = sb(s, "silu_gate", [P, NT])
                hf = sb(s, "h_full", [P, NT])
            with ExitStack() as s:
                kraw = sb(s, "kv_raw", [P, 8, NT])
                parts_k = sb(s, "head_parts_k", [P, 4, NT])
                pg0 = sb(s, "cmp_pages_0", [P, NPG, 512])
                w1 = sb(s, "cmp_w1", [P, 2, 8, P])
                w2 = sb(s, "cmp_w2", [DH, 2, DH])
                pe_t = sb(s, "cmp_pe", [P, 2, 8, 2])
                with ExitStack() as s2:
                    xh_k = sb(s2, "xh_k", [P, KT, NT], F32R)
                    xl_k = sb(s2, "xl_k", [P, KT, NT], F32R)
                pages_in = [pg0, sb(s, "cmp_pages_1", [P, NPG, 512])]
                xp = sb(s, "cmp_prompt", [P, 2, G, 8, 32])
                cb = sb(s, "cmp_bias", [DH, 2, 2])
                p1 = sb(s, "cmp_next", [DH, 2, 256])
                hid = sb(s, "cmp_hidden", [DH, 2, 4, NC_S])
                hge = sb(s, "cmp_gelu", [DH, 2, 4, NC_S])
                ck = sb(s, "kc_raw", [P, SB + 1, 2 * NC_S])
            with ExitStack() as s:
                q = sb(s, "q_T", [P, KT, NT])
                gt = sb(s, "gates", [P, 5, 48])
                gs = sb(s, "sample_gates", [P, SB, 3])
                kp = sb(s, "k_pages", [P, NPG, 2, PAGE])
                with ExitStack() as s2:
                    xh_n = sb(s2, "xh_n", [P, KT, NT], F32R)
                    xl_n = sb(s2, "xl_n", [P, KT, NT], F32R)
                    parts_n = sb(s2, "head_parts_n", [P, 4, NT])
                    sel_e = sb(s2, "gate_rows", [ST, SB, P])
                    sel_m = sb(s2, "gate_mask", [P, 48])
                    gw = sb(s2, "gates_by_row", [P, SB, 48])
                ah, al = sb(s, "ah", [P, KT, NT], F32R), sb(s, "al", [P, KT, NT], F32R)
                with ExitStack() as s2:
                    qst = sb(s2, "q_pair", [P, 2, PT])
                    kh, kl = sb(s2, "att_kh", [P, 2, PT], F32R), sb(s2, "att_kl", [P, 2, PT], F32R)
                    cmask = sb(s2, "cmp_mask", [P, 2, 4, NC_P])
                    pr = sb(s2, "probs", [P, 2, 1024])
                    pc = sb(s2, "probs_cmp", [P, 8, NC_P])
                    c8 = sb(s2, "cmp_stats", [P, 3, 8])
                    prt = sb(s2, "probs_T", [P, 2, 1024])
                    stat = sb(s2, "att_stats", [P, 2, 2, 2])
                    sums = sb(s2, "att_sums", [P, 4, 2])
                    ls = sb(s2, "att_gates", [P, 2, 2])
                    ot = sb(s2, "o_by_token", [P, 4, P])
                with ExitStack() as s2:
                    vp = sb(s2, "v_pages", [P, NPG, 256])
                    kw = sb(s2, "k_window", [P, 2, WIN])
                    vw = sb(s2, "v_window", [P, 4, 256])
                    ps_ = sb(s2, "sample_probs", [P, 1088 + 576])
                    qb = sb(s2, "q_of_batch", [P, 2, 2, 64])
                    pcs = sb(s2, "past_probs_cmp", [P, SB, NC_S])
                    new_t = sb(s2, "new_probs_T", [ST, 2, P])
                    smask = sb(s2, "new_key_mask", [P, SB, 64])
                    wmask = sb(s2, "window_mask", [P, 8])
                    iot = sb(s2, "block_numbers", [P, 14])
                    ovl = sb(s2, "overlap", [NC_S, 14])
                    drop = sb(s2, "dropped_block", [P, SB, NSEL])
                    dtmp = sb(s2, "block_choice", [P, 2, SB, 14])
                    cst = sb(s2, "past_cmp_stats", [P, 3, SB])
                    sst2 = sb(s2, "sample_stats", [P, 16])
                    oa = sb(s2, "sample_o", [P, SB, DH])
        def over_resting(t, rows, k):
            return t.rearrange("p a c -> p (a c)")[0:rows, 0:k * P].rearrange("p (k c) -> p k c", k=k)

        imp_t, prob_t = over_resting(xf, NC_S, SB), over_resting(sq, NC_S, SB)
        pst = over_resting(rb.rearrange("p a i d -> p (a i) d"), P, 8)
        qbd = over_resting(atab, P, SB).rearrange("p b (t r) -> p b t r", t=2)
        os_ = r[:, 0:KT * ST].rearrange("p (t c) -> p t c", t=KT)
        rvh, rvl = (t.rearrange("p a c -> p (a c)")[:, 0:NCH * DV].rearrange("p (k c) -> p k c", k=NCH)
                    for t in (oh_r, ol_r))
        pct = rb.rearrange("p a i d -> p (a i d)")[0:NC_P, 0:2 * PT].rearrange("p (k c) -> p k c", k=2)
        kp_flat = kp.rearrange("p j g c -> p j (g c)")
        ps = ctx.enter_context(nc.psum_tensor("ps", [P, 8, 512], F32))

        def wide(t):
            return t.rearrange("p (h n) -> p h n", h=2)

        def bank2(b):
            return ps[:, b:b + 2, 0:HALF]

        consts_in, out_done = sem("consts_in"), sem("output_written")
        landed = [sem("block_landed_0"), sem("block_landed_1")]
        hi_ready, lo_ready, w_used = sem("w_high_ready"), sem("w_low_ready"), sem("block_used")
        free = [sem("slot0_free"), sem("slot1_free")]
        phase = sem("phase_done")
        chain_v, chain_a, chain_g = sem("vector_steps"), sem("scalar_steps"), sem("pool_steps")
        sq_ready, sq_used, sq_sum = sem("squares_ready"), sem("squares_added"), sem("squares_mean")
        eps_added, root_ready, rb_ready = sem("eps_added"), sem("root_ready"), sem("stats_spread")
        r_sum, r_ready = sem("rstd_in_psum"), sem("rstd_ready")
        xf_ready, xh_ready, xn_ready = sem("x_normed"), sem("x_high_ready"), sem("x_split_ready")
        h_ready = sem("h_split_ready")

        st_set = sem("token_stats_set")
        consts = [(x, "x"), (gain, "gain"), (mats, "mats"), (mcol, "mcol"), (causal, "causal"), (pgt, "pt")]
        N_CONST = len(consts)

        block = ctx.enter_context(nc.Block())

        TILES = [(i * P, min(P, NT - i * P)) for i in range(5)]

        def barrier(eng, n):
            eng.drain().then_inc(phase, 1)
            eng.wait_ge(phase, 4 * n)

        def split_high(act, u, slot, size, after=True):
            act.wait_ge(landed[slot], (u - slot) * 8 + 16)
            if after:
                act.wait_ge(w_used, u - 1)
            act.activation(wh[:, slot, 0:size], wf[:, slot, 0:size], ACT.Copy).then_inc(hi_ready, 1)

        def split_low(dve, u, slot, size):
            dve.wait_ge(hi_ready, u + 1)
            dve.tensor_tensor(wl[:, slot, 0:size], wf[:, slot, 0:size], wh[:, slot, 0:size].bitcast(F32),
                              ALU.subtract).then_inc(lo_ready, 1)

        def sums_pe(pe, cols):
            for i, (c0, m) in enumerate(TILES):
                mm = pe.matmul(ps[0:m, 4, 2 * i:2 * i + 1], r[:, c0:c0 + m], cols, start=True, stop=True)
            return mm

        def add_squares(dve, ready, n_ready, used, n_used, slot):
            dve.wait_ge(ready, n_ready)
            if n_used is not None:
                dve.wait_ge(used, n_used)
            dve.tensor_tensor(r[:, :], r[:, :], sq[:, slot, :], ALU.add).then_inc(used, 1)

        LAG = 3
        KEPT, SQUARED = 4, (1, 3, 5)

        def roots_before(m):
            return m - (m > KEPT)

        def square(act, m, k, slot, row):
            q_ = roots_before(m)
            if not isinstance(k, int) or k >= 3:
                act.wait_ge(sq_used, 7 * q_ + k - 2)
            act.activation(row, x[:, ds(k, 1), :].rearrange("p o c -> p (o c)"), ACT.Square).then_inc(sq_ready, 1)

        def add_square(dve, m, j, slot):
            q_ = roots_before(m)
            first = isinstance(j, int) and j == 1
            add_squares(dve, sq_ready, 8 * q_ + j + 1, sq_used, None if first else 7 * q_ + j - 1, slot)

        def stats_dve(dve, cv, n, tiles, w, bank=4):
            whole = [i for i, (_, m) in enumerate(tiles) if m == P]
            parts = [(0, P, whole)] if whole else []
            parts += [(i, m, [i]) for i, (_, m) in enumerate(tiles) if m < P]
            for i0, m, idx in parts:
                src = ps[0:m, bank, 2 * i0:2 * (i0 + len(idx))].rearrange("p (i w) -> p i w", w=2)
                ins = dve.tensor_scalar(st[0:m, 0, i0:i0 + len(idx), 0:w], src[:, :, 0:w], EPS, None, ALU.add)
                if i0 == parts[-1][0]:
                    ins.then_inc(eps_added, 1)
                else:
                    cv.step(ins)
            dve.wait_ge(root_ready, n + 1)
            cv.link(dve.reciprocal(st[:, 0, :, 0:w], st[:, 0, :, 0:w]))
            dve.tensor_copy(rb[:, 0, 0:len(tiles), :].rearrange("p i (w d) -> p i w d", w=w),
                            st[:, 0, 0:len(tiles), 0:w].unsqueeze(3).to_broadcast([P, len(tiles), w, P // w])
                            ).then_inc(rb_ready, 1)

        def root_act(act, n, w):
            act.wait_ge(eps_added, n + 1)
            act.activation(st[:, 0, :, 0:w], st[:, 0, :, 0:w], ACT.Sqrt).then_inc(root_ready, 1)

        def spread_pe(pe, n, tiles):
            pe.wait_ge(rb_ready, n + 1)
            for i, (c0, m) in enumerate(tiles):
                mm = pe.matmul(ps[:, 5 + c0 // 512, c0 % 512:c0 % 512 + m], rb[0:m, 0, i, :], ident[0:m, 0:m],
                               start=True, stop=True)
            mm.then_inc(r_sum, 1)

        def spread_act(act, ca, n, width):
            act.wait_ge(r_sum, n + 1)
            ins = act.activation(r[:, 0:min(width, 512)], ps[:, 5, 0:min(width, 512)], ACT.Copy)
            if width > 512:
                ca.step(ins)
                ins = act.activation(r[:, 512:width], ps[:, 6, 0:width - 512], ACT.Copy)
            ins.then_inc(r_ready, 1)

        def norm_pe(pe, n, m):
            if m == KEPT:
                return
            pe.wait_ge(sq_used, 7 * roots_before(m) + 7)
            sums_pe(pe, mcol[:, 0:1]).then_inc(sq_sum, 1)
            spread_pe(pe, n, TILES)

        def norm_act(act, ca, n, m, xh, s):
            if m == 0:
                act.wait_ge(consts_in, 16 * N_CONST)
            elif m not in SQUARED:
                act.wait_ge(free[0], F0[s])
                act.wait_ge(free[1], F1[s])
            if m != KEPT:
                for k in range(0 if m not in SQUARED else KT, KT):
                    square(act, m, k, k % 2, sq[:, k % 2, :] if k else r[:, :])
                root_act(act, n, 1)
                spread_act(act, ca, n, NT)
            for k in range(KT):
                act.wait_ge(xf_ready, 8 * m + k + 1)
                act.activation(xh[:, k, :], xf[:, k % 2, :], ACT.Copy).then_inc(xh_ready, 1)

        def norm_dve(dve, cv, n, m, xh, xl, g0):
            if m != KEPT:
                for k in range(KT - 1 if m in SQUARED else 1, KT):
                    add_square(dve, m, k, k % 2)
                dve.wait_ge(sq_sum, roots_before(m) + 1)
                stats_dve(dve, cv, n, TILES, 1)
                dve.wait_ge(r_ready, n + 1)

            def low(k):
                dve.wait_ge(xh_ready, 8 * m + k + 1)
                dve.tensor_tensor(xl[:, k, :], xf[:, k % 2, :], xh[:, k, :].bitcast(F32),
                                  ALU.subtract).then_inc(xn_ready, 1)

            for k in range(KT):
                if k >= 2:
                    dve.wait_ge(xn_ready, 8 * m + k - 1)
                dve.scalar_tensor_tensor(xf[:, k % 2, :], x[:, k, :], gain[:, g0 + k:g0 + k + 1], r[:, :],
                                         ALU.mult, ALU.mult).then_inc(xf_ready, 1)
                if k:
                    low(k - 1)
            low(KT - 1)

        def passes(pe, out, slot, cols, m_hi, m_lo, first, last):
            for n, (w, m) in enumerate(((wh, m_hi), (wh, m_lo), (wl, m_hi))):
                for h in range(2):
                    mm = pe.matmul(ps[:, out + h, 0:HALF], w[:, slot, cols:cols + P],
                                   m[:, h * HALF:(h + 1) * HALF], start=(first and n == 0),
                                   stop=(last and n == 2))
            return mm

        def take_block(pe, u, slot, uses):
            pe.wait_ge(lo_ready, u + 1)
            if not (isinstance(uses, int) and uses == 0):
                pe.wait_ge(free[slot], uses)

        def first_pair_pe(pe, u, uses, hi, lo, m):
            take_block(pe, u, 0, uses[0])
            for k in range(KT + LAG):
                if k < KT:
                    pe.wait_ge(xn_ready, 8 * m + k + 1)
                    mm = passes(pe, 0, 0, k * P, hi[:, k, :], lo[:, k, :], k == 0, k == KT - 1)
                    if k == KT - 1:
                        mm.then_inc(w_used, 1)
                if k == LAG:
                    take_block(pe, u + 1, 1, uses[1])
                if k >= LAG:
                    j = k - LAG
                    mm = passes(pe, 2, 1, j * P, hi[:, j, :], lo[:, j, :], j == 0, j == KT - 1)
            mm.then_inc(w_used, 1)

        def unit_pe(pe, u, slot, uses, nk, hi, lo):
            take_block(pe, u, slot, uses)
            for k in range(nk):
                mm = passes(pe, 2 * slot, slot, k * P, hi[:, k, :], lo[:, k, :], k == 0, k == nk - 1)
            mm.then_inc(w_used, 1)

        def stored(eng, f):
            if f == 1:
                eng.wait_ge(st_sent, 16 * RH)
                for q_ in sout:
                    eng.wait_ge(q_, 32 * RH)
            if f == 2:
                eng.wait_ge(kv_sent, 16 * 4)

        def ffn_pe(pe, f, s, n, m):
            norm_pe(pe, n, m)
            for h in range(2):
                ub, f0, f1 = U0[s] + 30 * h, F0[s] + 15 * h, F1[s] + 15 * h

                def pair(j):
                    unit_pe(pe, ub + 2 * j, 0, f0 + j, KT, xh_f, xl_f)
                    unit_pe(pe, ub + 2 * j + 1, 1, f1 + j, KT, xh_f, xl_f)

                def outs(i):
                    unit_pe(pe, ub + 22 + 2 * i, 0, f0 + FH + i, FH, hh, hl)
                    unit_pe(pe, ub + 23 + 2 * i, 1, f1 + FH + i, FH, hh, hl)

                if h == 0:
                    first_pair_pe(pe, ub, (f0, f1), xh_f, xl_f, m)
                else:
                    pair(0)
                with pe.Fori(1, FH) as j:
                    pair(j)
                pe.wait_ge(h_ready, 1 + FH * (2 * f + h + 1))
                with pe.Fori(0, KT // 2) as i:
                    outs(i)

        def ffn_act(act, ca, f, s, n, m, last):
            stored(act, f)
            norm_act(act, ca, n, m, xh_f, s)
            for h in range(2):
                ub = U0[s] + 30 * h

                def pair(j, size):
                    u = ub + 2 * j
                    act.wait_ge(w_used, u + 1)
                    if not (isinstance(j, int) and f == h == j == 0):
                        act.wait_ge(h_ready, 1 + FH * (2 * f + h) + j)
                    act.activation(wide(sg[:, :]), bank2(0), ACT.Silu).then_inc(free[0], 1)
                    split_high(act, u + 2, 0, size)
                    split_high(act, u + 3, 1, size)

                def outs(i, more=True):
                    if more:
                        split_high(act, ub + 24 + 2 * i, 0, UB if more == 2 else UA)
                        split_high(act, ub + 25 + 2 * i, 1, UB if more == 2 else UA)
                    if h and m + 1 in SQUARED:
                        for k in range(2):
                            act.wait_ge(free[k], (F0, F1)[k][s] + 15 * h + FH + i + 1)
                            first = isinstance(i, int) and i == k == 0
                            square(act, m + 1, 2 * i + k, k, r[:, :] if first else sq[:, k, :])

                pair(0, UA)
                with act.Fori(1, FH - 1) as j:
                    pair(j, UA)
                pair(FH - 1, UB)
                outs(0, 2)
                with act.Fori(1, KT // 2 - 1) as i:
                    outs(i, 2)
                outs(KT // 2 - 1, not (last and h == 1))

        def ffn_dve(dve, cv, f, s, n, m, last):
            stored(dve, f)
            norm_dve(dve, cv, n, m, xh_f, xl_f, G_FFN + 8 * f)
            for h in range(2):
                ub, f0, f1 = U0[s] + 30 * h, F0[s] + 15 * h, F1[s] + 15 * h

                def pair(j, size):
                    u = ub + 2 * j
                    split_low(dve, u + 2, 0, size)
                    dve.wait_ge(w_used, u + 2)
                    dve.wait_ge(free[0], f0 + j + 1)
                    if not (isinstance(j, int) and f == h == j == 0):
                        dve.wait_ge(h_ready, 1 + FH * (2 * f + h) + j)
                    dve.tensor_tensor(wide(hf[:, :]), wide(sg[:, :]), bank2(2), ALU.mult).then_inc(free[1], 1)
                    dve.wait_ge(free[1], f1 + j + 1)
                    cv.link(dve.tensor_copy(hh[:, ds(j, 1), :], hf[:, :].unsqueeze(1)))
                    dve.tensor_tensor(hl[:, ds(j, 1), :], hf[:, :].unsqueeze(1),
                                      hh[:, ds(j, 1), :].bitcast(F32), ALU.subtract).then_inc(h_ready, 1)
                    split_low(dve, u + 3, 1, size)

                def outs(i, more):
                    for k in range(2):
                        if more == 2:
                            split_low(dve, ub + 24 + 2 * i + k, k, UB)
                        dve.wait_ge(w_used, ub + 23 + 2 * i + k)
                        t = wide_d(x[:, ds(2 * i + k, 1), :])
                        dve.scalar_tensor_tensor(t, bank2(2 * k), 0.5, t, ALU.mult, ALU.add
                                                 ).then_inc(free[k], 1)
                        if h and m + 1 in SQUARED and not (isinstance(i, int) and i == 0):
                            add_square(dve, m + 1, 2 * i + k - 1, 1 - k)
                        if more == 1:
                            split_low(dve, ub + 24 + 2 * i + k, k, UA)

                cv.loop(FH - 1, 1, lambda j: pair(j, UA))
                pair(FH - 1, UB)
                outs(0, 2)
                with dve.Fori(1, KT // 2 - 1) as i:
                    outs(i, 2)
                outs(KT // 2 - 1, 0 if last and h == 1 else 1)

        def wide_d(t):
            return t.rearrange("p o (h n) -> p (o h) n", h=2)

        raw_ready, rope_ready = sem("raw_ready"), sem("rope_ready")
        v_ready, st_sent = sem("ret_v_ready"), sem("state_sent")
        s_done, sk_ready, o_done, o_taken = sem("scores_done"), sem("scores_k_ready"), sem("o_done"), sem("o_taken")
        st_done, km_ready = sem("state_done"), sem("batch_k_ready")
        smp_done, smp_new = sem("sample_state_product"), sem("sample_state_new")
        sin = [sem(f"sample_state_in_{i}") for i in range(4)]
        sout = [sem(f"sample_state_out_{i}") for i in range(4)]
        mu_done, d_ready, dq_ready, dq_used = (sem(n) for n in ("mean_done", "centred", "centred_sq", "centred_sq_used"))
        dq_sum, og_ready = sem("centred_sq_mean"), sem("ret_gated")
        U, A0, A1 = U0["ret"], F0["ret"], F1["ret"]
        vh_ready, vl_ready = sem("ret_v_high_ready"), sem("ret_v_low_ready")
        ret_tabs, ret_half = sem("ret_tables_in"), sem("ret_first_tile_out")
        N_RET = 1

        def ret_pe(pe):
            norm_pe(pe, N_RET, 1)
            def head(h):
                u0, a0, a1 = U + h * RU, A0 + h * RU0, A1 + h * RU1
                first_pair_pe(pe, u0, (a0, a1), xh_r, xl_r, 1)
                for i in range(2, 4):
                    unit_pe(pe, u0 + i, i % 2, (a0, a1)[i % 2] + 1, KT, xh_r, xl_r)
                pe.wait_ge(free[0], a0 + 2)
                pe.wait_ge(o_taken, 1 + 5 * h)
                pe.wait_ge(smp_new, 1 + 8 * h)
                pe.wait_ge(r_ready, N_RET + 1 + h)
                for i in range(4):
                    pe.wait_ge(lo_ready, u0 + 5 + i)
                    for kk in range(2):
                        k = 2 * i + kk
                        for t, (c0, m) in enumerate(TILES):
                            b = 4 + t if t < 4 else 0
                            for n, (xx, w) in enumerate(((xh_r, wh), (xh_r, wl), (xl_r, wh))):
                                mm = pe.matmul(ps[0:m, b, :], xx[:, k, c0:c0 + m],
                                               w[:, i % 2, kk * DV:(kk + 1) * DV],
                                               start=(k == 0 and n == 0), stop=(k == KT - 1 and n == 2))
                    mm.then_inc(w_used, 1)

                def scores(c):
                    c0, m = TILES[c]
                    for t in range(2):
                        pe.matmul(ps[0:m, 4, 0:m], rk[:, t, c0:c0 + m], rq[:, t, c0:c0 + m],
                                  start=(t == 0), stop=(t == 1))
                    for t in range(2):
                        mm = pe.transpose(ps[0:m, 4, P + P * t:2 * P + P * t], rk[:, t, c0:c0 + m], ident)
                    mm.then_inc(s_done, 1)

                def gate(i):
                    unit_pe(pe, u0 + 8 + i, i % 2, (a0 + 3, a1 + 2)[i % 2] + i // 2, KT, xh_r, xl_r)

                gate(0)
                pe.wait_ge(rope_ready, h + 1)
                pe.wait_ge(v_ready, h + 1)
                pe.wait_ge(free[0], a0 + 3)
                scores(0)
                for c in range(NCH):
                    pe.wait_ge(sk_ready, 5 * h + c + 1)
                    scores(c + 1)
                    pe.wait_ge(st_done, 1 + 4 * h + c)
                    if c == 0:
                        pe.wait_ge(vl_ready, h + 1)
                    for t in range(2):
                        for n, (kk, vv) in enumerate(((kth, rvh), (kth, rvl), (ktl, rvh))):
                            pe.matmul(ps[:, 6 + t, :], kk[:, c % 2, t * P:(t + 1) * P], vv[:, c, :],
                                      start=(n == 0), stop=(n == 2))
                    pe.wait_ge(o_taken, 1 + 5 * h + c)
                    for v in range(4):
                        mm = pe.matmul(ps[:, 5, v * P:(v + 1) * P], rv[:, c, v * P:(v + 1) * P],
                                       ssb[:, c % 2, :], start=(v == 0), stop=(c == 0),
                                       skip_group_check=True)
                        for t in range(2 if c else 0):
                            mm = pe.matmul(ps[:, 5, v * P:(v + 1) * P], state[:, t, v * P:(v + 1) * P],
                                           rqd[:, t, c * CH:(c + 1) * CH], start=False, stop=(t == 1),
                                           skip_group_check=True)
                    mm.then_inc(o_done, 1)
                pe.wait_ge(sk_ready, 5 * h + 5)
                pe.wait_ge(o_taken, 1 + 5 * h + 4)
                pe.wait_ge(st_done, 1 + 4 * h + 4)
                for v in range(4):
                    pe.matmul(ps[:, 5, v * ST:(v + 1) * ST], rv[0:ST, 4, v * P:(v + 1) * P],
                              ssb[0:ST, 0, 0:ST], start=(v == 0), stop=False, skip_group_check=True)
                for b in range(SB):
                    pe.wait_ge(sin[b % 4], 32 * h + 16 * (b // 4) + 16)
                    for v in range(4):
                        for t in range(2):
                            c0 = v * ST + b * SQ
                            mm = pe.matmul(ps[:, 5, c0:c0 + SQ], sst[:, b % 4, t, v * P:(v + 1) * P],
                                           rqd[:, t, PT + b * SQ:PT + (b + 1) * SQ], start=False,
                                           stop=(t == 1), skip_group_check=True)
                    if b == SB - 1:
                        mm.then_inc(o_done, 1)
                    pe.wait_ge(km_ready, 8 * h + b + 1)
                    if b:
                        pe.wait_ge(smp_new, 1 + 8 * h + b)
                    for t in range(2):
                        for n, (kk, vv) in enumerate(((kmh, rsh), (kmh, rsl), (kml, rsh))):
                            mm = pe.matmul(ps[:, 6 + t, :], kk[:, b % 2, t * P:(t + 1) * P], vv[:, :],
                                           start=(n == 0), stop=(n == 2))
                    mm.then_inc(smp_done, 1)

                pe.wait_ge(o_taken, 1 + 5 * h + 5)
                pe.wait_ge(smp_new, 1 + 8 * h + 8)
                for v in range(4):
                    for hf_ in range(2):
                        mm = pe.matmul(ps[:, 6 + hf_, 0:HALF], ones_v, ro[:, v, hf_ * HALF:(hf_ + 1) * HALF],
                                       start=(v == 0), stop=(v == 3))
                mm.then_inc(mu_done, 1)
                gate(1)
                pe.wait_ge(dq_used, 3 * h + 3)
                sums_pe(pe, mcol[:, 1:2]).then_inc(dq_sum, 1)
                spread_pe(pe, N_RET + 1 + h, TILES)
                gate(2)
                gate(3)
                for i in range(4):
                    for k in range(2):
                        take_block(pe, u0 + 12 + i, k, (a0 + 5, a1 + 4)[k] + i)
                        for v in range(4):
                            if i == k == 0:
                                pe.wait_ge(og_ready, 1 + 4 * h + v + 1)
                            mm = passes(pe, 2 * k, i % 2, (4 * k + v) * P, oh_r[:, v, :], ol_r[:, v, :],
                                        v == 0, v == 3)
                        if k == 0:
                            mm.then_inc(ret_half, 1)
                    mm.then_inc(w_used, 1)

            with pe.Fori(0, RH) as h:
                head(h)

        def ret_act(act, ca):
            norm_act(act, ca, N_RET, 1, xh_r, "ret")

            def head(h):
                u0 = U + h * RU
                def silu(v):
                    act.wait_ge(w_used, u0 + 9 + v)
                    if v >= 2:
                        act.wait_ge(og_ready, 1 + 4 * h + v - 1)
                    act.activation(wide(sg_r[:, v % 2, :]), bank2(2 * (v % 2)), ACT.Silu
                                   ).then_inc(free[v % 2], 1)
                    split_high(act, u0 + 10 + v, v % 2, UA)

                act.wait_ge(og_ready, 1 + 4 * h)
                for i in range(4):
                    act.wait_ge(w_used, u0 + i + 1)
                    act.activation(wide(ro[:, i, :]), bank2(2 * (i % 2)), ACT.Copy).then_inc(free[i % 2], 1)
                    split_high(act, u0 + i + 2, i % 2, UA)
                for i in range(4, 8):
                    split_high(act, u0 + i + 2, i % 2, UA)
                act.wait_ge(w_used, u0 + 8)
                act.activation(rv[0:ST, 4, :], ps[0:ST, 0, :], ACT.Copy).then_inc(free[0], 1)
                act.activation(rv[:, 0:4, :], ps[:, 4:8, :], ACT.Copy).then_inc(v_ready, 1)
                act.wait_ge(v_ready, h + 1)
                ca.step(act.activation(rsh[:, :], rv[0:ST, 4, :], ACT.Copy))
                act.activation(rvh[:, :, :], rv[:, 0:4, :], ACT.Copy).then_inc(vh_ready, 1)
                silu(0)
                for c in range(5):
                    c0, m = TILES[c]
                    if c == 4:
                        act.wait_ge(sk_ready, 5 * h + 5)
                        for b in range(SB):
                            if b >= 2:
                                act.wait_ge(smp_done, 8 * h + b - 1)
                            for to, part in ((kmh, kth), (kml, ktl)):
                                ins = act.activation(to[:, b % 2, :], part[0:ST, 0, :].bitcast(F32), ACT.Copy,
                                                     scale=rbm[:, b:b + 1])
                                if part is kth:
                                    ca.step(ins)
                                else:
                                    ins.then_inc(km_ready, 1)
                    act.wait_ge(o_done, 5 * h + c + 1)
                    act.activation(ro[:, :, c0:c0 + m], ps[:, 5, 0:4 * m].rearrange("p (v m) -> p v m", v=4),
                                   ACT.Copy).then_inc(o_taken, 1)
                for v in range(4):
                    act.wait_ge(d_ready, 4 * h + v + 1)
                    if v == 3:
                        act.wait_ge(dq_used, 3 * h + 1)
                    act.activation(sq[:, v % 2, :] if v else r[:, :], ro[:, v, :], ACT.Square).then_inc(dq_ready, 1)
                root_act(act, N_RET + 1 + h, 1)
                spread_act(act, ca, N_RET + 1 + h, NT)
                for v in range(1, 4):
                    silu(v)
                for i in range(4):
                    split_high(act, u0 + 14 + i, i % 2, UA)

            ca.loop(RH, 2 + SB, head)

        def ret_dve(dve, cv):
            norm_dve(dve, cv, N_RET, 1, xh_r, xl_r, G_RET)
            dve.wait_ge(ret_tabs, 96)

            def head(h):
                u0, a0, a1 = U + h * RU, A0 + h * RU0, A1 + h * RU1
                for i in range(8):
                    split_low(dve, u0 + 2 + i, i % 2, UA)
                dve.wait_ge(vh_ready, h + 1)
                cv.step(dve.tensor_tensor(rsl[:, :], rv[0:ST, 4, :], rsh[:, :].bitcast(F32), ALU.subtract))
                dve.tensor_tensor(rvl[:, :, :], rv[:, 0:4, :], rvh[:, :, :].bitcast(F32), ALU.subtract
                                  ).then_inc(vl_ready, 1)

                def scores(c):
                    m = TILES[c][1]
                    dve.wait_ge(s_done, 5 * h + c + 1)
                    dec = rdec[:, ds(h, 1), :] if c < 4 else rsdec[:, ds(h, 1), :]
                    cv.step(dve.tensor_tensor(ssb[0:m, c % 2, 0:m].unsqueeze(1), ps[0:m, 4, 0:m].unsqueeze(1),
                                              dec, ALU.mult))
                    kd = rcol[0:m, 0 if c < 4 else 1, ds(h, 1)]
                    keys = ps[0:m, 4, P:3 * P]
                    cv.step(dve.tensor_scalar(ktk[0:m, c % 2, :], keys, kd, None, ALU.mult))
                    cv.link(dve.tensor_scalar(kth[0:m, c % 2, :], keys, kd, None, ALU.mult))
                    dve.tensor_tensor(ktl[0:m, c % 2, :], ktk[0:m, c % 2, :], kth[0:m, c % 2, :].bitcast(F32),
                                      ALU.subtract).then_inc(sk_ready, 1)

                scores(0)
                split_low(dve, u0 + 10, 0, UA)
                for c in range(NCH):
                    scores(c + 1)
                    dve.wait_ge(o_done, 5 * h + c + 1)
                    two = ps[:, 6:8, :]
                    if c == 0:
                        dve.wait_ge(rope_ready, h + 1)
                        dve.tensor_copy(state[:, :, :], two).then_inc(st_done, 1)
                    else:
                        dve.wait_ge(st_done, 1 + 4 * h + c)
                        dve.scalar_tensor_tensor(state[:, :, :], state[:, :, :], rcol[:, 2, ds(h, 1)], two,
                                                 ALU.mult, ALU.add).then_inc(st_done, 1)
                for b in range(SB):
                    dve.wait_ge(smp_done, 8 * h + b + 1)
                    dve.scalar_tensor_tensor(sst[:, b % 4, :, :], sst[:, b % 4, :, :], rcol[:, 3, ds(h, 1)],
                                             ps[:, 6:8, :], ALU.mult, ALU.add).then_inc(smp_new, 1)
                dve.wait_ge(mu_done, h + 1)
                for v in range(4):
                    dve.tensor_tensor(wide(ro[:, v, :]), wide(ro[:, v, :]), bank2(6), ALU.subtract
                                      ).then_inc(d_ready, 1)
                for v in range(1, 4):
                    add_squares(dve, dq_ready, 4 * h + v + 1, dq_used, 3 * h + v - 1 if v > 1 else None, v % 2)
                dve.wait_ge(dq_sum, h + 1)
                stats_dve(dve, cv, N_RET + 1 + h, TILES, 1)
                dve.wait_ge(r_ready, N_RET + 2 + h)
                split_low(dve, u0 + 11, 1, UA)
                for v in range(4):
                    cv.link(dve.tensor_tensor(ro[:, v, :], ro[:, v, :], r[:, :], ALU.mult))
                    dve.wait_ge(free[v % 2], (a0 + 4, a1 + 3)[v % 2] + v // 2)
                    cv.link(dve.tensor_tensor(ro[:, v, :], ro[:, v, :], sg_r[:, v % 2, :], ALU.mult))
                    cv.link(dve.tensor_copy(oh_r[:, v, :], ro[:, v, :]))
                    dve.tensor_tensor(ol_r[:, v, :], ro[:, v, :], oh_r[:, v, :].bitcast(F32),
                                      ALU.subtract).then_inc(og_ready, 1)
                    if v >= 2:
                        split_low(dve, u0 + 10 + v, v % 2, UA)
                for i in range(4):
                    for k in range(2):
                        if k == 0:
                            dve.wait_ge(ret_half, 4 * h + i + 1)
                        else:
                            dve.wait_ge(w_used, u0 + 13 + i)
                        t = wide(x[:, 2 * i + k, :])
                        dve.tensor_tensor(t, t, bank2(2 * k), ALU.add).then_inc(free[k], 1)
                    split_low(dve, u0 + 14 + i, i % 2, UA)

            cv.loop(RH, 5 * 3 + 1 + 2 + 12, head)

        def ret_pool(pool, cg):
            pool.wait_ge(free[0], A0)
            pool.wait_ge(free[1], A1)
            for t, name in ((rtab, "rtab"), (rdec, "rdec"), (rqdec, "rqdec"), (rsdec, "rsdec"),
                            (rcol, "rcol"), (rbm, "rbm")):
                pool.dma_start(t[:], a[name]).then_inc(ret_tabs, 16)
            pool.wait_ge(ret_tabs, 96)

            def state_in(h, b):
                pool.nop(nofuse=True)
                pool.dma_start(sst[:, b % 4, :, :], a["state"][ds(h, 1), b].rearrange("o p t v -> p (o t) v")
                               ).then_inc(sin[b % 4], 16)

            def head(h):
                for i in range(4):
                    state_in(h, i)
                pool.wait_ge(free[0], A0 + h * RU0 + 2)
                pool.wait_ge(free[1], A1 + h * RU1 + 2)
                cos, sin_ = rtab[:, 0, :], rtab[:, 1, :]
                for i, out in ((0, rq), (2, rk)):
                    lo, hi = ro[:, i, :], ro[:, i + 1, :]
                    cg.step(pool.tensor_tensor(pm[:, 0, :], lo, cos, ALU.mult))
                    cg.link(pool.tensor_tensor(pm[:, 1, :], hi, sin_, ALU.mult))
                    cg.link(pool.tensor_tensor(out[:, 0, :], pm[:, 0, :], pm[:, 1, :], ALU.subtract))
                    cg.step(pool.tensor_tensor(pm[:, 0, :], lo, sin_, ALU.mult))
                    cg.link(pool.tensor_tensor(pm[:, 1, :], hi, cos, ALU.mult))
                    cg.link(pool.tensor_tensor(out[:, 1, :], pm[:, 0, :], pm[:, 1, :], ALU.add))
                for t in range(2):
                    dec = rqdec[:, ds(h, 1), :]
                    cg.step(pool.tensor_tensor(
                        rqd[:, t, 0:PT].rearrange("p (c i) -> p c i", c=NCH),
                        rq[:, t, 0:PT].rearrange("p (c i) -> p c i", c=NCH),
                        dec.to_broadcast([P, NCH, CH]), ALU.mult))
                    ins = pool.tensor_tensor(
                        rqd[:, t, PT:NT].rearrange("p (b i) -> p b i", b=SB),
                        rq[:, t, PT:NT].rearrange("p (b i) -> p b i", b=SB),
                        rqdec[:, ds(h, 1), 0:SQ].to_broadcast([P, SB, SQ]), ALU.mult)
                    if t == 0:
                        cg.step(ins)
                    else:
                        ins.then_inc(rope_ready, 1)

                for b in range(SB):
                    pool.wait_ge(smp_new, 1 + 8 * h + b + 1)
                    pool.nop(nofuse=True)
                    pool.dma_start(o["state_s"][ds(h, 1), b].rearrange("o p t v -> p (o t) v"),
                                   sst[:, b % 4, :, :]).then_inc(sout[b % 4], 16)
                    if 1 <= b <= 4:
                        c = b - 1
                        pool.wait_ge(sout[c], 32 * h + 16)
                        state_in(h, c + 4)
                pool.dma_start(o["state_p"][ds(h, 1)].rearrange("o p t v -> p (o t) v"), state[:, :, :]
                               ).then_inc(st_sent, 16)
                for i in range(4):
                    pool.wait_ge(sout[i], 32 * h + 32)
                pool.wait_ge(st_sent, 16 * h + 16)

            cg.loop(RH, 15, head)

        hr_sq, hr_sum, hr_eps, hr_root, hr_rb, hr_spread, hr_r, hr_n, hr_rot, hr_out = (sem(n) for n in (
            "head_sq", "head_sum", "head_eps_added", "head_root", "head_stats_wide", "head_stats_spread",
            "head_rstd", "head_normed", "head_rotated", "head_out"))
        SPREAD, ROTATED = ((5, 6), (2, 3)), ((7, 6), (1, 3))
        CMP_P, CMP_S = [(0, 2 * NC_P)], [(0, 2 * NC_S)]

        def pieces(width, banks, c1):
            out = [(banks[0], slice(0, min(width, 512)), slice(0, min(width, 512)))]
            if width > 512:
                out.append((banks[1], slice(c1, c1 + width - 512), slice(512, width)))
            return out

        def width_of(tiles):
            return sum(m for _, m in tiles)

        def heads_pe(pe, i0, count, tiles_of, part):
            for j in range(count):
                pe.wait_ge(hr_sq, i0 + j + 1)
                for i, (c0, m) in enumerate(tiles_of(j)):
                    mm = pe.matmul(ps[0:m, 4, 10 * j + 2 * i:10 * j + 2 * i + 2], sq[:, j % 2, c0:c0 + m],
                                   mcol[:, 2:4], start=True, stop=True)
                mm.then_inc(hr_sum, 1)

            def spread(j):
                pe.wait_ge(hr_rb, i0 + j + 1)
                if j >= 2:
                    pe.wait_ge(hr_out, i0 + j - 1)
                for i, (c0, m) in enumerate(tiles_of(j)):
                    b = SPREAD[j % 2][c0 // 512]
                    mm = pe.matmul(ps[:, b, c0 % 512:c0 % 512 + m], rb[0:m, j % 2, i, :], ident[0:m, 0:m],
                                   start=True, stop=True)
                mm.then_inc(hr_spread, 1)

            spread(0)
            for j in range(count):
                if j + 1 < count:
                    spread(j + 1)
                pe.wait_ge(hr_n, i0 + j + 1)
                for b, at, cols in pieces(width_of(tiles_of(j)), ROTATED[j % 2], 64):
                    mm = pe.matmul(ps[:, b, at], rot, part[:, j % 2, cols], start=True, stop=True)
                mm.then_inc(hr_rot, 1)

        def heads_act(act, ca, e, i0, count, tiles_of, raw):
            for j in range(count):
                if j >= 2:
                    act.wait_ge(hr_sum, i0 + j - 1)
                act.activation(sq[:, j % 2, 0:width_of(tiles_of(j))], raw(j), ACT.Square).then_inc(hr_sq, 1)
            act.wait_ge(hr_eps, e + 1)
            act.activation(st[:, 0:count, :, :], st[:, 0:count, :, :], ACT.Sqrt).then_inc(hr_root, 1)
            for j in range(count):
                act.wait_ge(hr_spread, i0 + j + 1)
                if j >= 2:
                    act.wait_ge(hr_n, i0 + j - 1)
                both = pieces(width_of(tiles_of(j)), SPREAD[j % 2], 0)
                for b, at, cols in both:
                    ins = act.activation(xf[:, j % 2, cols], ps[:, b, at], ACT.Copy)
                    if b == both[-1][0]:
                        ins.then_inc(hr_r, 1)
                    else:
                        ca.step(ins)

        def heads_dve(dve, cv, e, i0, count, tiles_of, part, raw, gain_of, out, cos, sin_):
            dve.wait_ge(hr_sum, i0 + count)
            for m in sorted({m for j in range(count) for _, m in tiles_of(j)}):
                js = [j for j in range(count) if any(w == m for _, w in tiles_of(j))]
                ts = [i for i, (_, w) in enumerate(tiles_of(js[0])) if w == m]
                src = ps[0:m, 4, 0:10 * count].rearrange("p (j i w) -> p j i w", j=count, w=2)
                cv.link(dve.tensor_scalar(st[0:m, js[0]:js[-1] + 1, ts[0]:ts[-1] + 1, :],
                                          src[:, js[0]:js[-1] + 1, ts[0]:ts[-1] + 1, :], EPS, None, ALU.add))
            cv.eng.drain().then_inc(hr_eps, 1)
            dve.wait_ge(hr_root, e + 1)
            cv.link(dve.reciprocal(st[:, 0:count, :, :], st[:, 0:count, :, :]))

            def widen(j):
                if j >= 2:
                    dve.wait_ge(hr_spread, i0 + j - 1)
                n = len(tiles_of(j))
                dve.tensor_copy(rb[:, j % 2, 0:n, :].rearrange("p i (w d) -> p i w d", w=2),
                                st[:, j, 0:n, :].unsqueeze(3).to_broadcast([P, n, 2, DH])).then_inc(hr_rb, 1)

            def normed(j):
                dve.wait_ge(hr_r, i0 + j + 1)
                w = width_of(tiles_of(j))
                dve.scalar_tensor_tensor(part[:, j % 2, 0:w], raw(j), gain[:, gain_of(j):gain_of(j) + 1],
                                         xf[:, j % 2, 0:w], ALU.mult, ALU.mult).then_inc(hr_n, 1)

            widen(0)
            if count > 1:
                widen(1)
            normed(0)
            for j in range(count):
                if j + 2 < count:
                    widen(j + 2)
                if j + 1 < count:
                    normed(j + 1)
                w = width_of(tiles_of(j))
                three = len(cos(j).shape) == 3
                pair = (lambda t: t.rearrange("p (g c) -> p g c", g=2)) if three else (lambda t: t)
                dve.wait_ge(hr_n, i0 + j + 1)
                cv.step(dve.tensor_tensor(pair(part[:, 2, 0:w]), pair(part[:, j % 2, 0:w]), cos(j), ALU.mult))
                dve.wait_ge(hr_rot, i0 + j + 1)
                for b, at, cols in pieces(w, ROTATED[j % 2], 64):
                    table = sin_(j) if three else sin_(j)[:, cols]
                    cv.step(dve.tensor_tensor(pair(part[:, 3, cols]), pair(ps[:, b, at]), table, ALU.mult))
                cv.wait()
                dve.tensor_tensor(out(j), part[:, 2, 0:w], part[:, 3, 0:w], ALU.add).then_inc(hr_out, 1)
                dve.wait_ge(hr_out, i0 + j + 1)

        kv_tabs, kvv_ready, kv_sent = sem("kv_tables_in"), sem("kv_v_ready"), sem("kv_rows_sent")
        pin = [sem("cmp_pages_in_0"), sem("cmp_pages_in_1")]
        pos_ready = sem("cmp_position_part")
        bias_done, bias_ready, xp_ready = sem("cmp_bias_product"), sem("cmp_bias_ready"), sem("cmp_prompt_ready")
        cp_h, cp_p1, cp_hid, cp_ge, cp_kc, cp_vc, ck_ready, vc_taken = (
            sem(n) for n in ("cmp_product", "cmp_next_ready", "cmp_hidden_ready", "cmp_gelu_ready",
                             "kc_product", "vc_product", "kc_raw_ready", "vc_taken"))
        UK, N_KV = U0["kv"], 7
        KV_BARRIER, ATT_BARRIER = 1, 2

        def kv_pe(pe):
            norm_pe(pe, N_KV, 3)
            first_pair_pe(pe, UK, (F0["kv"], F1["kv"]), xh_k, xl_k, 3)
            for i in range(2, 8):
                unit_pe(pe, UK + i, i % 2, (F0, F1)[i % 2]["kv"] + i // 2, KT, xh_k, xl_k)
            pe.wait_ge(free[0], F0["kv"] + 4)
            for i in range(4):
                pe.wait_ge(lo_ready, UK + 9 + i)
                for kk in range(2):
                    k = 2 * i + kk
                    for t, (c0, m) in enumerate(TILES):
                        for n, (xx, w) in enumerate(((xh_k, wh), (xh_k, wl), (xl_k, wh))):
                            mm = pe.matmul(ps[0:m, 4 + t if t < 4 else 0, :], xx[:, k, c0:c0 + m],
                                           w[:, i % 2, kk * 512:(kk + 1) * 512],
                                           start=(k == 0 and n == 0), stop=(k == KT - 1 and n == 2))
                mm.then_inc(w_used, 1)
            pe.wait_ge(kvv_ready, 1)
            pe.wait_ge(free[0], F0["kv"] + 5)
            pe.wait_ge(free[1], F1["kv"] + 4)
            heads_pe(pe, 0, 4, lambda j: TILES, parts_k)
            barrier(pe, KV_BARRIER)
            pe.wait_ge(kv_tabs, 16 * 5)
            for v in range(2):
                for t in range(8):
                    mm = pe.matmul(ps[:, 3, 2 * v:2 * v + 2], w1[:, v, t, :], pe_t[:, v, t, :],
                                   start=(t == 0), stop=(t == 7))
            mm.then_inc(bias_done, 1)

            def compress(e, rhs, nc_, ch):
                for v in range(2):
                    for t in range(8):
                        mm = pe.matmul(ps[:, v, 0:G * ch], w1[:, v, t, :], rhs(v, t),
                                       start=(t == 0), stop=(t == 7))
                    mm.then_inc(cp_h, 1)
                pe.wait_ge(cp_ge, 2 * e + 2)
                pe.wait_ge(ck_ready, e)
                pe.wait_ge(vc_taken, e)
                pe.nop(nofuse=True)
                for g in range(G):
                    mm = pe.matmul(ps[DH * (g % 2):DH * (g % 2 + 1), 2, g // 2 * nc_:(g // 2 + 1) * nc_],
                                   w2[:, 0, :], hge[:, 0, g, 0:nc_], start=True, stop=True)
                mm.then_inc(cp_kc, 1)
                for g in range(G):
                    mm = pe.matmul(ps[0:nc_, 3, g * DH:(g + 1) * DH], hge[:, 1, g, 0:nc_], w2[:, 1, :],
                                   start=True, stop=True)
                mm.then_inc(cp_vc, 1)

            pe.wait_ge(xp_ready, 8)
            compress(0, lambda v, t: xp[:, v, :, t, :], NC_P, 32)
            with pe.Fori(0, SB // 2) as bp:
                for s in range(2):
                    pe.wait_ge(pin[s], bp * 16 * NPG + 16 * NPG)
                    pages = [pages_in[s][:, :, v * 256:(v + 1) * 256].rearrange("p j (g t c) -> p t g j c", g=G, t=8)
                             for v in range(2)]
                    compress(2 * bp + s + 1, lambda v, t: pages[v][:, t], NC_S, 64)
            pe.wait_ge(ck_ready, SB + 1)
            pe.wait_ge(vc_taken, SB + 1)
            heads_pe(pe, 4, SB + 1, lambda j: CMP_S if j else CMP_P, parts_k)

        def kv_act(act, ca):
            norm_act(act, ca, N_KV, 3, xh_k, "kv")
            for i in range(8):
                act.wait_ge(w_used, UK + i + 1)
                act.activation(wide(kraw[:, i, :]), bank2(2 * (i % 2)), ACT.Copy).then_inc(free[i % 2], 1)
                split_high(act, UK + i + 2, i % 2, UA)
            for i in range(8, 12):
                split_high(act, UK + i + 2, i % 2, UA)
            act.wait_ge(w_used, UK + 12)
            act.activation(v_tok[0:ST, 4, :], ps[0:ST, 0, :], ACT.Copy).then_inc(free[0], 1)
            act.activation(v_tok[:, 0:4, :], ps[:, 4:8, :], ACT.Copy).then_inc(kvv_ready, 1)
            act.wait_ge(free[1], F1["kv"] + 4)
            heads_act(act, ca, 0, 0, 4, lambda j: TILES, lambda j: kraw[:, 4 + j, :])
            barrier(act, KV_BARRIER)
            act.wait_ge(bias_done, 1)
            act.activation(cb[:, :, 0], ps[DH:P, 3, 1:4:2], ACT.Copy).then_inc(pos_ready, 1)

            def compress(e, nc_, ch):
                for v in range(2):
                    act.wait_ge(cp_h, 2 * e + v + 1)
                    act.activation(p1[:, v, 0:G * ch], ps[DH:P, v, 0:G * ch], ACT.Identity,
                                   bias=cb[:, v, 1:2]).then_inc(cp_p1, 1)
                for v in range(2):
                    act.wait_ge(cp_hid, 2 * e + v + 1)
                    act.activation(hge[:, v, :, 0:nc_], hid[:, v, :, 0:nc_], ACT.Gelu_apprx_tanh
                                   ).then_inc(cp_ge, 1)
                act.wait_ge(cp_kc, e + 1)
                act.activation(ck[:, ds(e, 1), 0:2 * nc_], ps[:, 2, 0:2 * nc_].unsqueeze(1), ACT.Copy
                               ).then_inc(ck_ready, 1)

            act.wait_ge(bias_ready, 1)
            compress(0, NC_P, 32)
            with act.Fori(0, SB // 2) as bp:
                for s in range(2):
                    compress(2 * bp + s + 1, NC_S, 64)
            act.wait_ge(ck_ready, SB + 1)
            heads_act(act, ca, 1, 4, SB + 1, lambda j: CMP_S if j else CMP_P,
                      lambda j: ck[:, j, 0:2 * (NC_S if j else NC_P)])

        def kv_dve(dve, cv):
            norm_dve(dve, cv, N_KV, 3, xh_k, xl_k, G_KV)
            for i in range(12):
                split_low(dve, UK + i + 2, i % 2, UA)
            dve.wait_ge(kv_tabs, 16 * 5)
            heads_dve(dve, cv, 0, 0, 4, lambda j: TILES, parts_k, lambda j: kraw[:, 4 + j, :],
                      lambda j: G_K + 1 + j // 2, lambda j: k_t[:, j, :], lambda j: atab[:, 0, :],
                      lambda j: atab[:, 1, :])
            barrier(dve, KV_BARRIER)
            for par in range(2):
                for g in range(2):
                    for v in range(2):
                        src = kraw[g * DH:(g + 1) * DH, 2 * v:2 * v + 2, 0:PT].rearrange(
                            "d g (c t y) -> d g t c y", t=8, y=2)[:, :, :, :, par]
                        dst = xp[par * DH:(par + 1) * DH, v, :, :, :].rearrange(
                            "d (q g) t c -> d q g t c", g=2)[:, :, g]
                        dve.tensor_copy(dst, src).then_inc(xp_ready, 1)
            dve.wait_ge(pos_ready, 1)
            cv.link(dve.tensor_tensor(cb[:, :, 1], ps[0:DH, 3, 0:4:2], cb[:, :, 0], ALU.add))
            dve.tensor_tensor(cb[:, :, 1], cb[:, :, 1], gain[0:DH, G_B1:G_B1 + 2], ALU.add
                              ).then_inc(bias_ready, 1)

            def compress(e, nc_, ch, out_v):
                for v in range(2):
                    dve.wait_ge(cp_p1, 2 * e + v + 1)
                    dve.tensor_tensor(
                        hid[:, v, :, 0:nc_],
                        ps[0:DH, v, 0:G * ch].rearrange("p (g c) -> p g c", g=G)[:, :, 0:nc_],
                        p1[:, v, 0:G * ch].rearrange("p (g c) -> p g c", g=G)[:, :, 1:nc_ + 1],
                        ALU.add).then_inc(cp_hid, 1)
                dve.wait_ge(cp_vc, e + 1)
                dve.tensor_copy(out_v, ps[0:nc_, 3, 0:256]).then_inc(vc_taken, 1)

            compress(0, NC_P, 32, vc_p[:, :])
            with dve.Fori(0, SB // 2) as bp:
                for s in range(2):
                    b = 2 * bp + s
                    compress(b + 1, NC_S, 64, vc_s[:, ds(b, 1)].rearrange("p o c -> p (o c)"))

            def table(k):
                return lambda j: (lambda n: ctab[:, k, 0:n].unsqueeze(1).to_broadcast([P, 2, n]))(
                    NC_S if j else NC_P)

            dve.wait_ge(ck_ready, SB + 1)
            heads_dve(dve, cv, 1, 4, SB + 1, lambda j: CMP_S if j else CMP_P, parts_k,
                      lambda j: ck[:, j, 0:2 * (NC_S if j else NC_P)], lambda j: G_K,
                      lambda j: (kc_s[:, j - 1] if j else kc_p[:, :, :]).rearrange("p g c -> p (g c)"),
                      table(0), table(1))

        def kv_pool(pool, cg):
            pool.wait_ge(free[0], F0["kv"])
            pool.wait_ge(free[1], F1["kv"])
            for t, name in ((atab, "atab"), (ctab, "ctab")):
                pool.dma_start(t[:], a[name]).then_inc(kv_tabs, 16)
            for t, name in ((w1, "w1"), (w2, "w2"), (pe_t, "pe")):
                pool.dma_start(t[:], a[name]).then_inc(kv_tabs, 16)

            def batch(b, s, wait):
                if wait:
                    pool.wait_ge(cp_h, 2 * b)
                    pool.nop(nofuse=True)
                for j in range(NPG):
                    page = pool.value_load(pgt[0:1, ds(b * NPG + j, 1)], min_val=0, max_val=NPHYS - 1)
                    pool.dma_start(pages_in[s][:, j, :], a["pages_cmp"][ds(page, 1)].rearrange("o p c -> p (o c)")
                                   ).then_inc(pin[s], 16)

            batch(0, 0, False)
            pool.wait_ge(free[0], F0["kv"] + 4)
            pool.wait_ge(free[1], F1["kv"] + 4)
            pool.dma_start(o["kv_fm"][:, 0:4, :], kraw[:, 0:4, :]).then_inc(kv_sent, 16)
            barrier(pool, KV_BARRIER)
            pool.dma_start(o["kv_fm"][:, 4:8, :], k_t[:, :, :]).then_inc(kv_sent, 16)
            pool.dma_start(o["kv_tok"][:, 0:4, :], v_tok[:, 0:4, :]).then_inc(kv_sent, 16)
            pool.dma_start(o["kv_tok"][0:ST, 4, :], v_tok[0:ST, 4, :]).then_inc(kv_sent, 16)

            batch(1, 1, False)
            with pool.Fori(1, SB // 2) as bp:
                for s in range(2):
                    batch(2 * bp + s, s, True)

        UN, N_Q, I_Q = U0["nsa"], 8, 13
        gate_ready, gsel_done, gs_ready = sem("gates_ready"), sem("gate_rows_done"), sem("sample_gates_ready")
        gs_mid, gate_tabs = sem("gates_masked"), sem("gate_tables_in")

        def q_pe(pe):
            norm_pe(pe, N_Q, 5)
            first_pair_pe(pe, UN, (F0["nsa"], F1["nsa"]), xh_n, xl_n, 5)
            with pe.Fori(1, KT // 2) as i:
                for s in range(2):
                    unit_pe(pe, UN + 2 * i + s, s, (F0, F1)[s]["nsa"] + i, KT, xh_n, xl_n)
            for un in range(2):
                pe.wait_ge(lo_ready, UN + 9 + un)
                for kk in range(4):
                    k = 4 * un + kk
                    for t, (c0, m) in enumerate(TILES):
                        for n, (xx, w) in enumerate(((xh_n, wh), (xh_n, wl), (xl_n, wh))):
                            mm = pe.matmul(ps[0:m, 4, 48 * t:48 * t + 48], xx[:, k, c0:c0 + m],
                                           w[:, un, kk * 48:kk * 48 + 48], start=(k == t == n == 0),
                                           stop=(k == KT - 1 and n == 2), skip_group_check=True)
                mm.then_inc(w_used, 1)
            pe.wait_ge(gate_ready, 2)
            pe.wait_ge(gate_tabs, 16 * 2)
            for b in range(SB):
                mm = pe.matmul(ps[:, 5, 48 * b:48 * b + 48], sel_e[:, b, :], gt[0:ST, 4, :],
                               start=True, stop=True)
            mm.then_inc(gsel_done, 1)
            pe.wait_ge(gs_mid, 1)
            pe.wait_ge(free[0], F0["nsa"] + 4)
            pe.wait_ge(free[1], F1["nsa"] + 4)
            heads_pe(pe, I_Q, KT, lambda j: TILES, parts_n)

        def q_act(act, ca):
            norm_act(act, ca, N_Q, 5, xh_n, "nsa")
            with act.Fori(0, KT // 2) as i:
                for s in range(2):
                    act.wait_ge(w_used, UN + 2 * i + s + 1)
                    act.activation(wide_d(q[:, ds(2 * i + s, 1), :]), bank2(2 * s), ACT.Copy
                                   ).then_inc(free[s], 1)
                    split_high(act, UN + 2 * i + s + 2, s, UA)
            split_high(act, UN + 10, 0, UA)
            split_high(act, UN + 11, 1, UA)
            act.activation(gt[:, 0:4, :], ps[:, 4, 0:192].rearrange("p (t c) -> p t c", t=4), ACT.Sigmoid
                           ).then_inc(gate_ready, 1)
            act.activation(gt[0:ST, 4, :], ps[0:ST, 4, 192:240], ACT.Sigmoid).then_inc(gate_ready, 1)
            act.wait_ge(free[0], F0["nsa"] + 4)
            act.wait_ge(free[1], F1["nsa"] + 4)
            heads_act(act, ca, 2, I_Q, KT, lambda j: TILES, lambda j: q[:, j, :])

        def q_dve(dve, cv):
            norm_dve(dve, cv, N_Q, 5, xh_n, xl_n, G_NSA)
            for i in range(10):
                split_low(dve, UN + 2 + i, i % 2, UA)
            dve.wait_ge(gsel_done, 1)
            dve.tensor_tensor(gw[:, :, :], ps[:, 5, 0:384].rearrange("p (b c) -> p b c", b=SB),
                              sel_m[:, :].unsqueeze(1).to_broadcast([P, SB, 48]), ALU.mult).then_inc(gs_mid, 1)
            dve.wait_ge(gs_mid, 1)
            dve.tensor_reduce(gs[:, :, :], gw[:, :, :].rearrange("p b (h r) -> p b r h", r=3), AX_X, ALU.add
                              ).then_inc(gs_ready, 1)

            heads_dve(dve, cv, 2, I_Q, KT, lambda j: TILES, parts_n, lambda j: q[:, j, :], lambda j: G_Q,
                      lambda j: q[:, j, :], lambda j: atab[:, 0, :], lambda j: atab[:, 1, :])

        att_in = sem("attention_tables_in")
        (qs_ready, cs_done, cx_ready, cx_exp, cp_ready, ct_done, ct_v, ct_a, cv_done, ot_ready, tr_done, tr_mid,
         tr_taken) = (sem(f"cmp_{n}") for n in (
             "q_pair_ready", "scores_done", "shifted", "exp_done", "probs_ready", "probs_turned",
             "turned_taken_v", "turned_taken_a", "o_done", "o_taken", "o_turned", "o_high", "o_split"))
        a_s, a_mx, a_exp, a_t, a_ptv, a_pta, a_v, a_o = (sem(f"att_{n}") for n in (
            "scores_done", "max_ready", "exp_done", "probs_turned", "turned_taken_v", "turned_taken_a",
            "o_done", "o_added"))

        def flat(t):
            return t.rearrange("p o c -> p (o c)")

        k_hi, k_lo, ql_ready = sem("att_k_high_ready"), sem("att_k_low_ready"), sem("att_q_split")

        def unit(n):
            return n % 2, n // 2

        def att_pe(pe):
            def turn(gp, s, T):
                def scores(n):
                    g, i = unit(n)
                    pe.wait_ge(a_exp, 1 + 8 * T + max(n - 1, 0))
                    lo = DH * g
                    if n == 0:
                        pe.wait_ge(ql_ready, T + 1)
                    for j in range(2):
                        whole = ((qst, k_t[:, gp:4:2, 0:P]),)
                        for m, (qq, kk) in enumerate(((qh, kh), (qh, kl), (ql, kh)) if i else whole):
                            mm = pe.matmul(ps[:, 2 * (n % 2) + j, 0:P * (i + 1)],
                                           qq[lo:lo + DH, s, i * P:(i + 1) * P],
                                           kk[lo:lo + DH, j, 0:P * (i + 1)], start=(m == 0),
                                           stop=(m == 2 or not i))
                    mm.then_inc(a_s, 1)

                def turned(n):
                    g, i = unit(n)
                    pe.wait_ge(a_exp, 1 + 8 * T + n + 1)
                    pe.wait_ge(a_ptv, 1 + 8 * T + n)
                    pe.wait_ge(a_pta, 1 + 8 * T + n)
                    if n == 0:
                        pe.wait_ge(ct_v, T + 1)
                        pe.wait_ge(ct_a, T + 1)
                    for j in range(2):
                        for k in range(i + 1):
                            mm = pe.transpose(ps[:, 5 + j, k * P:(k + 1) * P],
                                              pr[:, n % 2, 512 * j + k * P:512 * j + (k + 1) * P], ident)
                    mm.then_inc(a_t, 1)

                def values(n):
                    g, i = unit(n)
                    pe.wait_ge(a_ptv, 1 + 8 * T + n + 1)
                    pe.wait_ge(a_pta, 1 + 8 * T + n + 1)
                    pe.wait_ge(a_o, 1 + 8 * T + n)
                    for j in range(2):
                        for k in range(i + 1):
                            c0 = 256 * j + (2 * gp + g) * DH
                            mm = pe.matmul(ps[:, 7, j * DH:(j + 1) * DH],
                                           prt[:, n % 2, 512 * j + k * P:512 * j + (k + 1) * P],
                                           v_tok[:, k, c0:c0 + DH], start=(k == 0), stop=(k == i))
                    mm.then_inc(a_v, 1)

                pe.wait_ge(qs_ready, T + 1)
                pe.wait_ge(a_ptv, 1 + 8 * T)
                pe.wait_ge(a_pta, 1 + 8 * T)
                pe.nop(nofuse=True)
                for g in range(2):
                    for i in range(4):
                        rows = slice(DH * g, DH * (g + 1))
                        mm = pe.matmul(ps[:, 5 + g, i * NC_P:(i + 1) * NC_P],
                                       qst[rows, s, i * P:(i + 1) * P], kc_p[rows, gp, :], start=True, stop=True)
                mm.then_inc(cs_done, 1)
                scores(0)
                scores(1)
                pe.wait_ge(cp_ready, T + 1)
                for g in range(2):
                    for i in range(4):
                        mm = pe.transpose(ps[0:NC_P, 5 + g, i * P:(i + 1) * P], pc[:, 4 * g + i, :], ident)
                mm.then_inc(ct_done, 1)
                pe.wait_ge(ct_v, T + 1)
                pe.wait_ge(ct_a, T + 1)
                pe.wait_ge(tr_taken, 1 + T)
                for i in range(4):
                    for g in range(2):
                        c0 = i * P + g * DH
                        mm = pe.matmul(ps[:, 4, c0:c0 + DH], pct[:, g, i * P:(i + 1) * P],
                                       vc_p[:, (2 * gp + g) * DH:(2 * gp + g + 1) * DH], start=True, stop=True)
                mm.then_inc(cv_done, 1)
                for n in range(8):
                    turned(n)
                    if n:
                        values(n - 1)
                    if n + 2 < 8:
                        scores(n + 2)
                values(7)
                pe.wait_ge(a_o, 1 + 8 * T + 8)
                pe.wait_ge(ot_ready, T + 1)
                for i in range(4):
                    mm = pe.transpose(ps[:, 4, i * P:(i + 1) * P], ot[:, i, :], ident)
                mm.then_inc(tr_done, 1)

            for gp in range(2):
                pe.wait_ge(k_lo, gp + 1)
                with pe.Fori(0, 2) as hh:
                    for s in range(2):
                        turn(gp, s, 4 * gp + 2 * hh + s)

        def att_act(act, ca):
            def turn(gp, s, T):
                def probs(n):
                    g, i = unit(n)
                    act.wait_ge(a_mx, 8 * T + n + 1)
                    act.wait_ge(a_t, 1 + 8 * T + max(n - 1, 0))
                    w = P * (i + 1)
                    for j in range(2):
                        ins = act.activation(pr[:, n % 2, 512 * j:512 * j + w], ps[:, 2 * (n % 2) + j, 0:w],
                                             ACT.Exp, bias=stat[:, n % 2, 1, j:j + 1], scale=SCALE,
                                             accum_out=sums[:, n % 4, j:j + 1])
                    ins.then_inc(a_exp, 1)

                act.wait_ge(cx_ready, T + 1)
                act.activation(pc[:, :, :], pc[:, :, :], ACT.Exp, scale=SCALE).then_inc(cx_exp, 1)
                probs(0)
                probs(1)
                act.wait_ge(ct_done, T + 1)
                act.activation(pct[:, 1, :], ps[0:NC_P, 6, :], ACT.Copy).then_inc(ct_a, 1)
                for n in range(8):
                    g, i = unit(n)
                    act.wait_ge(a_t, 1 + 8 * T + n + 1)
                    act.wait_ge(a_v, 1 + 8 * T + max(n - 1, 0))
                    w = P * (i + 1)
                    act.activation(prt[:, n % 2, 512:512 + w], ps[:, 6, 0:w], ACT.Copy).then_inc(a_pta, 1)
                    if n + 2 < 8:
                        probs(n + 2)

            for gp in range(2):
                if gp:
                    act.wait_ge(tr_done, 1 + 4 * gp)
                act.activation(kh[:, :, :], k_t[:, gp:4:2, 0:PT], ACT.Copy).then_inc(k_hi, 1)
                with act.Fori(0, 2) as hh:
                    for s in range(2):
                        turn(gp, s, 4 * gp + 2 * hh + s)

        def att_dve(dve, cv):
            def turn(gp, s, T):
                def maxima(n):
                    g, i = unit(n)
                    dve.wait_ge(a_s, 1 + 8 * T + n + 1)
                    two = ps[:, 2 * (n % 2):2 * (n % 2) + 2, :]
                    cv.link(dve.tensor_tensor(two[:, :, i * P:(i + 1) * P], two[:, :, i * P:(i + 1) * P],
                                              causal[:, :].unsqueeze(1).to_broadcast([P, 2, P]), ALU.add))
                    cv.link(dve.tensor_reduce(stat[:, n % 2, 0, :], two[:, :, 0:P * (i + 1)], AX_X, ALU.max))
                    dve.tensor_scalar(stat[:, n % 2, 1, :], stat[:, n % 2, 0, :], -SCALE, None, ALU.mult
                                      ).then_inc(a_mx, 1)

                def gate(r0, n):
                    return gt[:, n // 2, ds(6 * T + 3 * (n % 2) + r0, 2)]

                def add(n):
                    g, i = unit(n)
                    dve.wait_ge(a_exp, 1 + 8 * T + n + 1)
                    cv.link(dve.reciprocal(ls[:, n % 2, :], sums[:, n % 4, :]))
                    cv.link(dve.tensor_tensor(ls[:, n % 2, :], ls[:, n % 2, :], gate(1, n), ALU.mult))
                    dve.wait_ge(a_v, 1 + 8 * T + n + 1)
                    to = ot[:, i, g * DH:(g + 1) * DH]
                    cv.link(dve.scalar_tensor_tensor(to, ps[:, 7, 0:DH], ls[:, n % 2, 0:1], to,
                                                     ALU.mult, ALU.add))
                    dve.scalar_tensor_tensor(to, ps[:, 7, DH:2 * DH], ls[:, n % 2, 1:2], to,
                                             ALU.mult, ALU.add).then_inc(a_o, 1)

                def eight(t):
                    return t.rearrange("p (g i) c -> p g i c", g=2)

                def over(t, k):
                    return t[:, k].unsqueeze(1).to_broadcast([P, 2, 4, NC_P])

                dve.wait_ge(cs_done, T + 1)
                cv.link(dve.tensor_tensor(
                    eight(pc[:, :, :]), ps[:, 5:7, 0:4 * NC_P].rearrange("p g (i c) -> p g i c", i=4),
                    over(cmask, 0), ALU.add))
                cv.link(dve.tensor_reduce(c8[:, 0, :], pc[:, :, :], AX_X, ALU.max))
                dve.tensor_tensor(pc[:, :, :], pc[:, :, :], c8[:, 0, :].unsqueeze(2).to_broadcast([P, 8, NC_P]),
                                  ALU.subtract).then_inc(cx_ready, 1)
                maxima(0)
                maxima(1)
                dve.wait_ge(cx_exp, T + 1)
                cv.link(dve.tensor_reduce(c8[:, 0, :], pc[:, :, :], AX_X, ALU.add))
                cv.link(dve.reciprocal(c8[:, 1, :], c8[:, 0, :]))
                cv.step(dve.tensor_tensor(
                    c8[:, 2, :].rearrange("p (g i) -> p g i", g=2),
                    c8[:, 1, :].rearrange("p (g i) -> p g i", g=2),
                    gt[:, 0:4, ds(6 * T, 6)].rearrange("p i (g r) -> p g i r", g=2)[:, :, :, 0], ALU.mult))
                cv.link(dve.tensor_tensor(eight(pc[:, :, :]), eight(pc[:, :, :]), over(cmask, 1), ALU.mult))
                dve.tensor_tensor(pc[:, :, :], pc[:, :, :], c8[:, 2, :].unsqueeze(2).to_broadcast([P, 8, NC_P]),
                                  ALU.mult).then_inc(cp_ready, 1)
                dve.wait_ge(ct_done, T + 1)
                dve.tensor_copy(pct[:, 0, :], ps[0:NC_P, 5, :]).then_inc(ct_v, 1)
                dve.wait_ge(cv_done, T + 1)
                dve.wait_ge(tr_done, 1 + T)
                dve.tensor_copy(ot[:, :, :], ps[:, 4, :].rearrange("p (i c) -> p i c", i=4)).then_inc(ot_ready, 1)
                dve.wait_ge(ot_ready, T + 1)
                for n in range(8):
                    g, i = unit(n)
                    dve.wait_ge(a_t, 1 + 8 * T + n + 1)
                    dve.wait_ge(a_v, 1 + 8 * T + max(n - 1, 0))
                    dve.tensor_copy(prt[:, n % 2, 0:P * (i + 1)], ps[:, 5, 0:P * (i + 1)]).then_inc(a_ptv, 1)
                    if n:
                        add(n - 1)
                    if n + 2 < 8:
                        maxima(n + 2)
                add(7)
                dve.wait_ge(tr_done, 1 + T + 1)
                row = ah[:, ds(T, 1), 0:PT].rearrange("p o c -> p (o c)")
                dve.tensor_copy(row, ps[:, 4, :]).then_inc(tr_mid, 1)
                dve.wait_ge(tr_mid, T + 1)
                dve.tensor_tensor(al[:, ds(T, 1), 0:PT].rearrange("p o c -> p (o c)"), ps[:, 4, :],
                                  row.bitcast(F32), ALU.subtract).then_inc(tr_taken, 1)

            for gp in range(2):
                dve.wait_ge(k_hi, gp + 1)
                dve.tensor_tensor(kl[:, :, :], k_t[:, gp:4:2, 0:PT], kh[:, :, :].bitcast(F32), ALU.subtract
                                  ).then_inc(k_lo, 1)

                def two(hh):
                    for s in range(2):
                        turn(gp, s, 4 * gp + 2 * hh + s)
                cv.loop(2, 2 * (2 + 4 + 8 * 2 + 8 * 3), two)

        def att_pool(pool, cg):
            for gp in range(2):
                def two(hh, gp=gp):
                    for s in range(2):
                        T = 4 * gp + 2 * hh + s
                        pool.wait_ge(a_s, 1 + 8 * T)
                        pool.nop(nofuse=True)
                        row = flat(q[:, ds(T, 1), 0:PT])
                        pool.tensor_copy(qst[:, s, :], row).then_inc(qs_ready, 1)
                        cg.link(pool.tensor_copy(qh[:, s, :], row))
                        pool.nop(nofuse=True)
                        pool.tensor_tensor(ql[:, s, :], row, qh[:, s, :].bitcast(F32), ALU.subtract
                                           ).then_inc(ql_ready, 1)
                cg.loop(2, 2, two)

        kin, vin, win_in, smp_tabs = (sem(n) for n in ("k_pages_in", "v_pages_in", "window_in", "sample_tables_in"))
        wv_in, win_sent, qa_ready, qb_ready = (sem(n) for n in (
            "window_values_in", "window_sent", "block_diagonal_ready", "batch_q_ready"))
        (c_s, c_x, c_e, c_p, c_t, c_ti, c_tp, c_imp, c_v, c_o) = (sem(f"past_cmp_{n}") for n in (
            "scores", "shifted", "exp", "probs", "turned", "importance_taken", "probs_taken", "importance",
            "values", "o_ready"))
        (b_s, b_mx, b_exp, b_t1, b_t1v, b_t1a, b_v1, b_t2, b_t2v, b_t2a, b_v2, b_o, b_ot) = (
            sem(f"sample_{n}") for n in (
                "scores", "max", "exp", "turned1", "taken1_v", "taken1_a", "values1", "turned2", "taken2_v",
                "taken2_a", "values2", "o_ready", "o_turned"))

        def smp_pe(pe):
            pe.wait_ge(smp_tabs, 16 * 4)
            pe.wait_ge(qa_ready, 4)
            for b in range(SB):
                for g in range(2):
                    mm = pe.matmul(ps[64 * g:64 * g + 64, 5, NC_S * b:NC_S * (b + 1)], qbd[:, b, g, :],
                                   kc_s[:, b, g, :], start=True, stop=True)
            mm.then_inc(c_s, 1)
            pe.wait_ge(c_p, 1)
            for b in range(SB):
                mm = pe.matmul(ps[0:NC_S, b // 4, b % 4 * P:(b % 4 + 1) * P], pcs[:, b, :], same,
                               start=True, stop=True)
            mm.then_inc(c_t, 1)
            for b in range(SB):
                mm = pe.transpose(ps[0:NC_S, 2 + b // 4, b % 4 * P:(b % 4 + 1) * P], pcs[:, b, :], ident)
            mm.then_inc(c_t, 1)
            pe.wait_ge(c_ti, 1)
            for b in range(SB):
                mm = pe.matmul(ps[:, 4, 14 * b:14 * b + 14], imp_t[:, b, :], ovl[:, :], start=True, stop=True)
            mm.then_inc(c_imp, 1)
            pe.wait_ge(c_tp, 1)
            for b in range(SB):
                mm = pe.matmul(ps[:, b // 2, b % 2 * 256:(b % 2 + 1) * 256], prob_t[:, b, :], vc_s[:, b, :],
                               start=True, stop=True)
            mm.then_inc(c_v, 1)
            pe.wait_ge(c_o, 1)

            def scores(b, s):
                pe.wait_ge(qb_ready, b + 1)
                pe.wait_ge(kin, 16 * NPG * (b + 1))
                pe.nop(nofuse=True)
                for g in range(2):
                    for h in range(2):
                        pe.matmul(ps[64 * g:64 * g + 64, h, :], qb[:, s, g, :], kp[:, 4 * h:4 * h + 4, g, :],
                                  start=True, stop=True)
                    pe.matmul(ps[64 * g:64 * g + 64, 2, 0:ST], qb[:, s, g, :], k_t[:, g, PT:NT],
                              start=True, stop=True)
                pe.wait_ge(win_in, 16 * (b + 1))
                pe.nop(nofuse=True)
                for g in range(2):
                    pe.matmul(ps[64 * g:64 * g + 64, 3, :], qb[:, s, g, :], kw[:, g, :], start=True, stop=True)
                    mm = pe.matmul(ps[64 * g:64 * g + 64, 4, 0:ST], qb[:, s, g, :], k_t[:, 2 + g, PT:NT],
                                   start=True, stop=True)
                mm.then_inc(b_s, 1)

            def batch(b, s, more=True):
                pe.wait_ge(b_exp, b + 1)
                pe.wait_ge(b_t2v, 1 + 2 * b)
                pe.wait_ge(b_t2a, 1 + b)
                for k in range(8):
                    mm = pe.transpose(ps[:, 6 + k // 4, k % 4 * P:(k % 4 + 1) * P], ps_[:, k * P:(k + 1) * P],
                                      ident)
                mm.then_inc(b_t1, 1)
                if more:
                    scores(b + 1, 1 - s)
                pe.wait_ge(vin, 16 * NPG * (b + 1))
                pe.wait_ge(b_t1v, b + 1)
                pe.wait_ge(b_t1a, b + 1)
                pe.wait_ge(b_o, 1 + b)
                for k in range(8):
                    mm = pe.matmul(ps[:, 5, 0:256], pst[:, k, :], vp[:, k, :], start=(k == 0), stop=False,
                                   skip_group_check=True)
                mm.then_inc(b_v1, 1)
                for k in range(4):
                    pe.transpose(ps[:, 6, k * P:(k + 1) * P], ps_[:, 1088 + k * P:1088 + (k + 1) * P], ident)
                pe.transpose(ps[0:ST, 7, 0:P], ps_[:, 1024:1088], ident)
                pe.transpose(ps[0:ST, 7, P:2 * P], ps_[:, 1600:1664], ident).then_inc(b_t2, 1)
                pe.wait_ge(b_t2v, 1 + 2 * b + 2)
                pe.wait_ge(b_t2a, 1 + b + 1)
                pe.matmul(ps[:, 5, 0:256], new_t[:, 0, :], v_tok[0:ST, 4, 0:256], start=False, stop=True,
                          skip_group_check=True)
                pe.wait_ge(wv_in, 16 * (b + 1))
                for k in range(4):
                    pe.matmul(ps[:, 5, 256:512], pst[:, k, :], vw[:, k, :], start=(k == 0), stop=False,
                              skip_group_check=True)
                pe.matmul(ps[:, 5, 256:512], new_t[:, 1, :], v_tok[0:ST, 4, 256:512], start=False, stop=True,
                          skip_group_check=True).then_inc(b_v2, 1)

            scores(0, 0)
            with pe.Fori(0, SB // 2 - 1) as bp:
                for s in range(2):
                    batch(2 * bp + s, s)
            batch(SB - 2, 0)
            batch(SB - 1, 1, False)
            pe.wait_ge(b_o, 1 + SB)
            for b in range(SB):
                mm = pe.transpose(ps[0:DH, b // 4, b % 4 * P:(b % 4 + 1) * P], oa[:, b, :], ident)
            mm.then_inc(b_ot, 1)

        def smp_act(act):
            act.wait_ge(c_x, 1)
            act.activation(pcs[:, :, :], pcs[:, :, :], ACT.Exp, scale=SCALE).then_inc(c_e, 1)
            act.wait_ge(c_t, 2)
            act.activation(prob_t, ps[0:NC_S, 2:4, :].rearrange("p k (b r) -> p (k b) r", b=4), ACT.Copy
                           ).then_inc(c_tp, 1)

            def batch(b):
                act.wait_ge(b_mx, b + 1)
                act.wait_ge(b_t2, 1 + b)
                act.activation(ps_[:, 0:1088], ps[:, 0:3, :].rearrange("p b c -> p (b c)")[:, 0:1088], ACT.Exp,
                               bias=sst2[:, 6:7], scale=SCALE, accum_out=sst2[:, 8:9])
                act.activation(ps_[:, 1088:1664], ps[:, 3:5, :].rearrange("p b c -> p (b c)")[:, 0:576], ACT.Exp,
                               bias=sst2[:, 7:8], scale=SCALE, accum_out=sst2[:, 9:10]).then_inc(b_exp, 1)
                act.wait_ge(b_t1, b + 1)
                act.activation(pst[:, 4:8, :], ps[:, 7, :].rearrange("p (k c) -> p k c", k=4), ACT.Copy
                               ).then_inc(b_t1a, 1)
                act.wait_ge(b_t2, 1 + b + 1)
                act.activation(new_t[:, :, :], ps[0:ST, 7, 0:2 * P].rearrange("p (k c) -> p k c", k=2), ACT.Copy
                               ).then_inc(b_t2a, 1)

            with act.Fori(0, SB) as b:
                batch(b)

        def smp_dve(dve, cv):
            dve.memset(drop[:, :, :], 0.0).then_inc(drop_set, 1)
            dve.wait_ge(drop_set, 1)
            dve.wait_ge(smp_tabs, 16 * 4)

            def over(t, n):
                return t.unsqueeze(2).to_broadcast([P, SB, n])

            dve.wait_ge(c_s, 1)
            first = ps[:, 5, 0:SB * NC_S].rearrange("p (b c) -> p b c", b=SB)
            cv.link(dve.tensor_reduce(cst[:, 0, :], first, AX_X, ALU.max))
            dve.tensor_tensor(pcs[:, :, :], first, over(cst[:, 0, :], NC_S), ALU.subtract).then_inc(c_x, 1)
            dve.wait_ge(c_e, 1)
            cv.link(dve.tensor_reduce(cst[:, 1, :], pcs[:, :, :], AX_X, ALU.add))
            cv.link(dve.reciprocal(cst[:, 2, :], cst[:, 1, :]))
            dve.tensor_tensor(pcs[:, :, :], pcs[:, :, :], over(cst[:, 2, :], NC_S), ALU.mult).then_inc(c_p, 1)
            dve.wait_ge(c_t, 1)
            dve.tensor_copy(imp_t, ps[0:NC_S, 0:2, :].rearrange("p k (b r) -> p (k b) r", b=4)).then_inc(c_ti, 1)
            dve.wait_ge(c_imp, 1)
            imp = ps[:, 4, 0:SB * 14].rearrange("p (b s) -> p b s", b=SB)
            numbers = iot[:, :].unsqueeze(1).to_broadcast([P, SB, 14])
            cv.link(dve.tensor_reduce(cst[:, 0, :], imp, AX_X, ALU.min))
            cv.link(dve.tensor_tensor(dtmp[:, 0], imp, over(cst[:, 0, :], 14), ALU.is_equal))
            cv.link(dve.tensor_tensor(dtmp[:, 1], dtmp[:, 0], numbers, ALU.mult))
            cv.link(dve.tensor_reduce(cst[:, 1, :], dtmp[:, 1], AX_X, ALU.max))
            cv.link(dve.tensor_tensor(dtmp[:, 0], numbers, over(cst[:, 1, :], 14), ALU.is_equal))
            cv.link(dve.tensor_scalar(drop[:, :, 1:15], dtmp[:, 0], NEG, None, ALU.mult))
            dve.wait_ge(c_v, 1)
            for g in range(G):
                rows = slice(32 * g, 32 * g + 32)
                src = ps[rows, 0:4, :].rearrange("p k (b c) -> p (k b) c", b=2)[:, :, g * DH:(g + 1) * DH]
                cv.link(dve.tensor_tensor(oa[rows, :, :], src, gs[rows, :, 0].unsqueeze(2).to_broadcast([32, SB, DH]),
                                          ALU.mult))
            dve.drain().then_inc(c_o, 1)
            slc = ps[:, 0:3, :].rearrange("p b c -> p (b c)")
            win = ps[:, 3:5, :].rearrange("p b c -> p (b c)")

            def maxima(b):
                dve.wait_ge(b_s, 1 + b + 1)
                new = flat(smask[:, ds(b, 1), :])
                past = slc[:, 0:PAST].rearrange("p (s t) -> p s t", s=NSEL)
                cv.step(dve.tensor_tensor(
                    past, past, flat(drop[:, ds(b, 1), :]).unsqueeze(2).to_broadcast([P, NSEL, SEL]), ALU.add))
                cv.step(dve.tensor_tensor(slc[:, 1024:1088], slc[:, 1024:1088], new, ALU.add))
                cv.step(dve.tensor_tensor(win[:, 512:576], win[:, 512:576], new, ALU.add))
                cv.link(dve.tensor_tensor(win[:, 0:SQ], win[:, 0:SQ], wmask[:, :], ALU.add))
                cv.step(dve.tensor_reduce(sst2[:, 5:6], win[:, 0:576], AX_X, ALU.max))
                cv.link(dve.tensor_reduce(sst2[:, 4:5], slc[:, 0:1088], AX_X, ALU.max))
                dve.tensor_scalar(sst2[:, 6:8], sst2[:, 4:6], -SCALE, None, ALU.mult).then_inc(b_mx, 1)

            def batch(b, more=True):
                dve.wait_ge(b_exp, b + 1)
                cv.link(dve.reciprocal(sst2[:, 12:14], sst2[:, 8:10]))
                cv.link(dve.tensor_tensor(sst2[:, 14:16], sst2[:, 12:14], flat(gs[:, ds(b, 1), 1:3]), ALU.mult))
                dve.wait_ge(b_t1, b + 1)
                dve.tensor_copy(pst[:, 0:4, :], ps[:, 6, :].rearrange("p (k c) -> p k c", k=4)).then_inc(b_t1v, 1)
                if more:
                    maxima(b + 1)
                dve.wait_ge(b_t2, 1 + b + 1)
                for k in range(2):
                    dve.tensor_copy(pst[:, 2 * k:2 * k + 2, :],
                                    ps[:, 6, 256 * k:256 * k + 256].rearrange("p (k c) -> p k c", k=2)
                                    ).then_inc(b_t2v, 1)
                dve.wait_ge(b_v2, 1 + b + 1)
                for n in range(2):
                    for g in range(G):
                        rows = slice(32 * g, 32 * g + 32)
                        to = flat(oa[rows, ds(b, 1), :])
                        ins = dve.scalar_tensor_tensor(to, ps[rows, 5, 256 * n + g * DH:256 * n + (g + 1) * DH],
                                                       sst2[rows, 14 + n:15 + n], to, ALU.mult, ALU.add)
                        if n == 1 and g == G - 1:
                            ins.then_inc(b_o, 1)
                        else:
                            cv.step(ins)
                    if n == 0:
                        cv.wait()

            maxima(0)
            cv.loop(SB - 1, 2 + 6 + 7, batch)
            batch(SB - 1, False)
            dve.wait_ge(b_ot, 1)
            for g in range(2):
                cv.step(dve.tensor_copy(
                    os_[g * DH:(g + 1) * DH].rearrange("d (p h) (b q) -> d p h b q", p=2, b=SB),
                    ps[0:DH, 0:2, :].rearrange("d k (b p g h q) -> d p g h (k b) q", b=4, p=2, g=2, h=HG)[:, :, g]))
            cv.wait()
            cv.link(dve.tensor_copy(ah[:, :, PT:NT], os_))
            cv.step(dve.tensor_tensor(al[:, :, PT:NT], os_, ah[:, :, PT:NT].bitcast(F32), ALU.subtract))

        def diagonal_pool(pool, cg):
            cg.link(pool.memset(qbd, 0.0))
            for g in range(2):
                rows = slice(g * DH, (g + 1) * DH)
                for t in range(2):
                    ins = pool.tensor_copy(
                        qbd[rows, :, t, 32 * g:32 * g + 32].rearrange("p b (h q) -> p h b q", h=HG),
                        q[rows, t * HG:(t + 1) * HG, PT:NT].rearrange("p h (b q) -> p h b q", b=SB))
                    ins.then_inc(qa_ready, 1)
                pool.wait_ge(qa_ready, 2 * g + 2)

        def values_pool(pool, b):
            for j in range(NPG):
                page = pool.value_load(pgt[0:1, ds(b * NPG + j, 1)], min_val=0, max_val=NPHYS - 1)
                pool.dma_start(vp[:, j, :], a["pages_v"][ds(page, 1)].rearrange("o p c -> p (o c)")
                               ).then_inc(vin, 16)

        def smp_pool(pool):
            for t, name in ((smask, "smask"), (wmask, "wmask"), (iot, "iot"), (ovl, "ovl")):
                pool.dma_start(t[:], a[name]).then_inc(smp_tabs, 16)

            def diagonal(b, s):
                pool.tensor_copy(qb[:, s, :, :].rearrange("p t r -> p (t r)"),
                                 qbd[:, ds(b, 1)].rearrange("p o t r -> p (o t r)")).then_inc(qb_ready, 1)

            diagonal(0, 0)
            diagonal(1, 1)
            values_pool(pool, 0)
            pool.dma_start(vw[:, :, :], a["win_v"][0]).then_inc(wv_in, 16)

            def batch(b, s, more=True):
                if more:
                    pool.wait_ge(b_s, 1 + b + 1)
                    pool.nop(nofuse=True)
                    diagonal(b + 2, s)
                pool.wait_ge(b_v1, b + 1)
                pool.nop(nofuse=True)
                values_pool(pool, b + 1)
                pool.wait_ge(b_v2, 1 + b + 1)
                pool.nop(nofuse=True)
                pool.dma_start(vw[:, :, :], a["win_v"][ds(b + 1, 1)].rearrange("o p g c -> p (o g) c")
                               ).then_inc(wv_in, 16)

            with pool.Fori(0, SB // 2 - 1) as bp:
                for s in range(2):
                    batch(2 * bp + s, s)
            batch(SB - 2, 0, False)

        def smp_sp(sp):
            def pages(b):
                for j in range(NPG):
                    page = sp.value_load(pgt[0:1, ds(b * NPG + j, 1)], min_val=0, max_val=NPHYS - 1)
                    sp.dma_start(kp_flat[:, j], a["pages_k"][ds(page, 1)].rearrange("o p c -> p (o c)")
                                 ).then_inc(kin, 16)

            sp.wait_ge(phase, 4 * ATT_BARRIER)
            pages(0)
            sp.wait_ge(phase, 4 * (ATT_BARRIER + 1))
            sp.dma_start(kw[:, :, :], a["win_k"][0]).then_inc(win_in, 16)
            with sp.Fori(1, SB) as b:
                sp.wait_ge(b_s, 1 + b)
                sp.nop(nofuse=True)
                pages(b)
                sp.dma_start(kw[:, :, :], a["win_k"][ds(b, 1)].rearrange("o p g c -> p (o g) c")
                             ).then_inc(win_in, 16)

        drop_set = sem("drop_cleared")

        def nsa_pe(pe):
            q_pe(pe)
            barrier(pe, ATT_BARRIER)
            pe.wait_ge(att_in, 16)
            att_pe(pe)
            barrier(pe, ATT_BARRIER + 1)
            smp_pe(pe)
            barrier(pe, ATT_BARRIER + 2)
            for i in range(8):
                unit_pe(pe, UN + 10 + i, i % 2, (F0, F1)[i % 2]["nsa"] + 4 + i // 2, KT, ah, al)

        def nsa_act(act, ca):
            q_act(act, ca)
            barrier(act, ATT_BARRIER)
            att_act(act, ca)
            barrier(act, ATT_BARRIER + 1)
            smp_act(act)
            barrier(act, ATT_BARRIER + 2)
            for i in range(8):
                split_high(act, UN + 12 + i, i % 2, UA)

        def nsa_dve(dve, cv):
            q_dve(dve, cv)
            barrier(dve, ATT_BARRIER)
            dve.wait_ge(att_in, 16)
            att_dve(dve, cv)
            barrier(dve, ATT_BARRIER + 1)
            smp_dve(dve, cv)
            barrier(dve, ATT_BARRIER + 2)
            for i in range(8):
                dve.wait_ge(w_used, UN + 11 + i)
                t = wide(x[:, i, :])
                dve.tensor_tensor(t, t, bank2(2 * (i % 2)), ALU.add).then_inc(free[i % 2], 1)
                split_low(dve, UN + 12 + i, i % 2, UA)

        def nsa_pool(pool, cg):
            pool.wait_ge(free[0], F0["nsa"])
            pool.wait_ge(free[1], F1["nsa"])
            pool.dma_start(sel_e[:], a["sel_e"]).then_inc(gate_tabs, 16)
            pool.dma_start(sel_m[:], a["sel_m"]).then_inc(gate_tabs, 16)
            for n in ("win_k", "win_v"):
                pool.dma_start(o[n], a[n]).then_inc(win_sent, 16)
            barrier(pool, ATT_BARRIER)
            pool.dma_start(cmask[:], a["cmask"]).then_inc(att_in, 16)
            att_pool(pool, cg)
            diagonal_pool(pool, cg)
            barrier(pool, ATT_BARRIER + 1)
            smp_pool(pool)
            barrier(pool, ATT_BARRIER + 2)

        ROOTS = {"ffn0": 0, "ret": 1, "ffn1": 6, "kv": 7, "ffn2": None, "nsa": 8, "ffn3": 9}
        NORMS = {s: i for i, s in enumerate(STAGES)}

        @block.sync
        def _(sp):
            for t, name in consts:
                sp.dma_start(t[:], a[name]).then_inc(consts_in, 16)

            def load(u, slot, src, size):
                if not (isinstance(u, int) and u < 2):
                    sp.wait_ge(lo_ready, u - 1)
                sp.dma_start(wf[:, slot, 0:size], src).then_inc(landed[slot], 16)

            def load_run(u0, first, count, src, size):
                def two(i, j):
                    for k in range(2):
                        load(u0 + 2 * i + k, k, src[ds(first + 2 * i + k, 1)].rearrange("o p c -> p (o c)"),
                             size)
                start = 0
                if u0 == 0:
                    two(0, 0)
                    start = 1
                with sp.Fori(start, count // 2) as i:
                    two(i, 0)

            ia = ib = 0
            for s in STAGES:
                if s.startswith("ffn"):
                    for h in range(2):
                        load_run(U0[s] + 30 * h, ia, 2 * FH, a["wa"], UA)
                        load_run(U0[s] + 30 * h + 2 * FH, ib, KT, a["wb"], UB)
                        ia, ib = ia + 2 * FH, ib + KT
                elif s == "nsa":
                    load_run(U0[s], ia, 14, a["wa"], UA)
                    smp_sp(sp)
                    load_run(U0[s] + 14, ia + 14, 4, a["wa"], UA)
                    ia += UNITS[s]
                else:
                    load_run(U0[s], ia, UNITS[s], a["wa"], UA)
                    ia += UNITS[s]
            sp.wait_ge(free[0], F0_END)
            sp.wait_ge(free[1], F1_END)
            sp.dma_start(o["y"], x[:, :, :]).then_inc(out_done, 16)
            sp.wait_ge(out_done, 16)

        @block.tensor
        def _(pe):
            pe.wait_ge(consts_in, 16 * N_CONST)
            for s in STAGES:
                if s.startswith("ffn"):
                    ffn_pe(pe, int(s[3]), s, ROOTS[s], NORMS[s])
                if s == "ret":
                    ret_pe(pe)
                if s == "kv":
                    kv_pe(pe)
                if s == "nsa":
                    nsa_pe(pe)

        @block.scalar
        def _(act):
            ca = Chain(act, chain_a)
            split_high(act, 0, 0, UA, False)
            split_high(act, 1, 1, UA, False)
            for s in STAGES:
                if s.startswith("ffn"):
                    ffn_act(act, ca, int(s[3]), s, ROOTS[s], NORMS[s], s == STAGES[-1])
                if s == "ret":
                    ret_act(act, ca)
                if s == "kv":
                    kv_act(act, ca)
                if s == "nsa":
                    nsa_act(act, ca)

        @block.vector
        def _(dve):
            cv = Chain(dve, chain_v)
            dve.memset(st[:, :, :, :], 1.0).then_inc(st_set, 1)
            dve.wait_ge(st_set, 1)
            dve.wait_ge(consts_in, 16 * N_CONST)
            split_low(dve, 0, 0, UA)
            split_low(dve, 1, 1, UA)
            for s in STAGES:
                if s.startswith("ffn"):
                    ffn_dve(dve, cv, int(s[3]), s, ROOTS[s], NORMS[s], s == STAGES[-1])
                if s == "ret":
                    ret_dve(dve, cv)
                if s == "kv":
                    kv_dve(dve, cv)
                if s == "nsa":
                    nsa_dve(dve, cv)

        @block.gpsimd
        def _(pool):
            cg = Chain(pool, chain_g)
            for counted in (h_ready, o_taken, og_ready, smp_new, st_done, a_s, a_t, a_exp, a_ptv,
                            a_pta, a_v, a_o, tr_done, tr_taken, b_s, b_o, b_v2, b_t2, b_t2v, b_t2a):
                pool.nop(nofuse=True).then_inc(counted, 1)
            for s in STAGES:
                if s == "ret":
                    ret_pool(pool, cg)
                if s == "kv":
                    kv_pool(pool, cg)
                if s == "nsa":
                    nsa_pool(pool, cg)
            pool.wait_ge(win_sent, 32)
            pool.wait_ge(st_sent, 16 * RH)
            for i in range(4):
                pool.wait_ge(sout[i], 32 * RH)



def constants():
    f = np.float32
    c = {}
    eye = np.eye(P, dtype=f)
    rot = np.zeros((P, P), f)
    for b in range(0, P, DH):
        for i in range(DH // 2):
            rot[b + DH // 2 + i, b + i] = -1.0
            rot[b + i, b + DH // 2 + i] = 1.0
    row = np.arange(P)
    same = ((row[:, None] // 32 == row[None] // 32) & (row[:, None] % SQ == row[None] % SQ)).astype(f)
    c["mats"] = np.stack([np.full((P, P), 1 / DV, f), rot, eye, same], 1)
    mcol = np.zeros((P, 4), f)
    mcol[:, 0], mcol[:, 1] = 1 / D, 1 / DV
    mcol[:DH, 2] = mcol[DH:, 3] = 1 / DH
    c["mcol"] = mcol
    c["causal"] = np.where(row[None] <= row[:, None], 0, NEG).astype(f)
    pos = np.concatenate([np.arange(PT), np.tile(PAST + np.arange(SQ), SB)]).astype(f)

    def angles(width, at):
        inv = f(10000.0) ** (-np.arange(width // 2, dtype=f) / f(width // 2))
        ang = at[None, :].astype(f) * inv.astype(f)[:, None]
        return np.cos(ang).astype(f), np.sin(ang).astype(f)

    cos, sin = angles(DK, pos)
    c["rtab"] = np.stack([cos, sin], 1)
    cos, sin = angles(DH, pos)
    c["atab"] = np.stack([np.tile(cos, (4, 1)), np.tile(sin, (4, 1))], 1)
    cos, sin = angles(DH, (np.arange(NC_S) * 16 + 31).astype(f))
    c["ctab"] = np.stack([np.tile(cos, (4, 1)), np.tile(sin, (4, 1))], 1)
    lg = np.log(f(1.0) - f(2.0) ** (f(-5.0) - np.arange(RH, dtype=f))).astype(f)
    rel = (row[None, :] - row[:, None]).astype(f)
    dec = np.where(rel >= 0, np.exp(np.maximum(rel, 0)[None] * lg[:, None, None]), 0).astype(f)
    ks = f(DK ** -0.5)
    c["rdec"] = (dec * ks).transpose(1, 0, 2)
    c["rqdec"] = np.tile(np.exp((row + 1.0)[None, :].astype(f) * lg[:, None]).astype(f)[None], (P, 1, 1))
    tok = np.arange(ST)
    blk = (tok[:, None] // SQ == tok[None] // SQ)
    c["rsdec"] = np.where(blk[None], dec[:, tok % SQ][:, :, tok % SQ] * ks, 0).transpose(1, 0, 2)
    rcol = np.zeros((P, 4, RH), f)
    rcol[:, 0] = np.exp((CH - 1.0 - row)[:, None].astype(f) * lg[None]) * ks
    rcol[:, 1] = np.exp((SQ - 1.0 - row % SQ)[:, None].astype(f) * lg[None]) * ks
    rcol[:, 2], rcol[:, 3] = np.exp(f(CH) * lg), np.exp(f(SQ) * lg)
    c["rcol"] = rcol
    c["rbm"] = (tok[:, None] // SQ == np.arange(SB)[None])
    qpos = np.arange(PT).reshape(4, P).T
    valid = (np.arange(NC_P) * 16 + 31)[None, None, :] <= qpos[:, :, None]
    c["cmask"] = np.stack([np.where(valid, 0, NEG), valid], 1)
    sel_e = np.zeros((ST, SB, P), f)
    for b in range(SB):
        sel_e[b * SQ + row % SQ, b, row] = 1
    c["sel_e"] = sel_e
    sel_m = np.zeros((P, 16, 3), f)
    for i in row:
        g, hh = i // 32, i // SQ % HG
        sel_m[i, 2 * ((g // 2) * HG + hh) + g % 2] = 1
    c["sel_m"] = sel_m.reshape(P, 48)
    c["smask"] = np.where((tok[None, None] // SQ == np.arange(SB)[None, :, None])
                          & (tok[None, None] % SQ <= (row % SQ)[:, None, None]), 0, NEG)
    c["wmask"] = np.where(np.arange(SQ)[None] > (row % SQ)[:, None], 0, NEG)
    c["iot"] = np.tile(np.arange(1, 15), (P, 1))
    ci, sj = np.arange(NC_S)[:, None], np.arange(1, 15)[None]
    c["ovl"] = (ci * 16 < (sj + 1) * SEL) & (ci * 16 + 32 > sj * SEL)
    return {k: np.ascontiguousarray(v, f) for k, v in c.items()}


def by_tile(v):
    return v.reshape(v.shape[:-1] + (-1, P)).swapaxes(-1, -2)


def blocks(w, nk=None):
    k, n = w.shape[0] // P, w.shape[1] // P
    return w.reshape(k, P, n, P).transpose(2, 1, 0, 3).reshape(n, P, k * P)


def by_rows(w, nk):
    k = w.shape[0] // P
    return w.reshape(k // nk, nk, P, -1).transpose(0, 2, 1, 3).reshape(k // nk, P, -1)


def layouts(v):
    d = {}
    xt = np.concatenate([v["x_prompt"].reshape(PT, D), v["x_sample"].reshape(ST, D)]).T
    d["x"] = xt.reshape(KT, P, NT).transpose(1, 0, 2)
    wi, wo = v["ffn_w_in"], v["ffn_w_out"]

    def ffn_in(f):
        w = wi.reshape(4, D, 2 * FF)[f]
        ab = np.stack([blocks(w[:, :FF]), blocks(w[:, FF:])], 1)
        return [ab.reshape(2 * FT, P, UA)]

    heads = [[(2 * gp + g) * HG + h for g in range(2)] for gp in range(2) for h in range(HG)]
    heads = np.array(heads).reshape(-1)
    qcol = (heads[:, None] * DH + np.arange(DH)).reshape(-1)
    gcol = D + (heads[:, None] * 3 + np.arange(3)).reshape(-1)
    rw, nw = v["ret_w_in"][0], v["nsa_w_in"][0]
    ret = []
    for h in range(RH):
        ret += [blocks(rw[:, h * DK:(h + 1) * DK]), blocks(rw[:, D + h * DK:D + (h + 1) * DK])]
        ret += [by_rows(rw[:, 2 * D + h * DV:2 * D + (h + 1) * DV], 2)]
        ret += [blocks(rw[:, 4 * D + h * DV:4 * D + (h + 1) * DV])]
        out = blocks(v["ret_w_out"][0][h * DV:(h + 1) * DV])
        ret += [out.reshape(4, 2, P, 4 * P).transpose(0, 2, 1, 3).reshape(4, P, UA)]
    kw = v["kv_w"].reshape(D, 6, 256)
    kv = [blocks(np.concatenate([kw[:, i] for i in (0, 1, 2, 4)], 1)),
          by_rows(np.concatenate([kw[:, 3], kw[:, 5]], 1), 2)]
    gates = np.zeros((2, P, UA), np.float32)
    gates[:, :, :4 * 48] = by_rows(nw[:, gcol], 4)
    nsa = [blocks(nw[:, qcol]), gates, blocks(v["nsa_w_out"][0][qcol])]
    d["wa"] = np.concatenate(ffn_in(0) + ret + ffn_in(1) + kv + ffn_in(2) + nsa + ffn_in(3))
    d["wb"] = np.concatenate([blocks(wo.reshape(4, FF, D)[f, h * FH * P:(h + 1) * FH * P])
                              for f in range(4) for h in range(2)])
    two = [np.concatenate([n, n])[:, None] for n in (*v["k_norm"], v["q_norm"][0])]
    b1 = np.zeros((P, 2), np.float32)
    b1[:DH] = v["cmp_b1"].T
    d["gain"] = np.concatenate(
        [by_tile(v["ffn_norm"].reshape(4, D)).transpose(1, 0, 2).reshape(P, 32), by_tile(v["ret_norm"][0]),
         by_tile(v["kv_norm"]), by_tile(v["nsa_norm"][0]), *two, b1], 1)
    d["state"] = v["state_ret"][0].reshape(SB, RH, 2, P, DV).transpose(1, 0, 3, 2, 4)
    d["w1"] = v["cmp_w1"].reshape(2, 2, 8, 2, DH, DH).transpose(3, 4, 0, 2, 1, 5).reshape(P, 2, 8, P)
    d["w2"] = v["cmp_w2"].transpose(1, 0, 2)
    d["pe"] = v["cmp_pe"].reshape(2, 2, 8, 2, DH).transpose(3, 4, 0, 2, 1).reshape(P, 2, 8, 2)
    pg = v["cache_kv"].reshape(NPHYS, 8, 8, 2, 4, G, DH)
    d["pages_cmp"] = pg[:, :, :, :, :2].transpose(0, 3, 6, 4, 5, 2, 1).reshape(NPHYS, P, 512)
    pg = v["cache_kv"]
    d["pages_k"] = pg[:, :, 2].reshape(NPHYS, PAGE, 2, 2, DH).transpose(0, 3, 4, 2, 1).reshape(NPHYS, P, 256)
    d["pages_v"] = pg[:, :, 3].reshape(NPHYS, PAGE, 256)
    cw = v["cache_win"]
    d["win_k"] = cw[:, :, 0].reshape(SB, WIN, 2, 2, DH).transpose(0, 3, 4, 2, 1).reshape(SB, P, 2, WIN)
    d["win_v"] = cw[:, :, 1].reshape(SB, 4, P, 256).transpose(0, 2, 1, 3)
    d["pt"] = v["page_table"].reshape(1, SB * NPG)
    return {k: np.ascontiguousarray(t) for k, t in d.items()}


OUTPUTS = {"y": (P, KT, NT), "state_p": (RH, P, 2, DV), "state_s": (RH, SB, P, 2, DV),
           "kv_fm": (P, 8, NT), "kv_tok": (P, 5, 512), "win_k": (SB, P, 2, WIN), "win_v": (SB, P, 4, 256)}


def kernel(**inputs):
    import concourse.bacc as bacc
    from concourse.bass_utils import run_bass_kernel_spmd

    v = {k: np.asarray(t) for k, t in inputs.items()}
    arrays = {f"in_{k}": t for k, t in {**constants(), **layouts(v)}.items()}
    nc = bacc.Bacc("TRN2", target_bir_lowering=False, num_devices=1)
    a = {k[3:]: nc.dram_tensor(k, t.shape, mybir.dt.from_np(t.dtype), kind="ExternalInput").ap()
         for k, t in arrays.items()}
    o = {k: nc.dram_tensor(f"out_{k}", s, F32, kind="ExternalOutput").ap() for k, s in OUTPUTS.items()}
    trunk_program(nc, a, o)
    res = run_bass_kernel_spmd(nc, [arrays], core_ids=[0]).results[0]
    return assemble({k: np.asarray(res[f"out_{k}"]) for k in OUTPUTS})


def assemble(res):
    y = res["y"].transpose(2, 1, 0).reshape(NT, D)
    fm = res["kv_fm"].transpose(2, 1, 0).reshape(NT, 4, G, DH)
    tok = res["kv_tok"].transpose(1, 0, 2).reshape(5 * P, 2, G, DH)[:NT]
    rows = np.stack([fm[:, 0], fm[:, 1], fm[:, 2], tok[:, 0]], 1)
    win = np.stack([fm[:, 3], tok[:, 1]], 1)
    old_k = res["win_k"].reshape(SB, 2, DH, 2, WIN).transpose(0, 4, 3, 1, 2).reshape(SB, WIN, G, DH)
    old_v = res["win_v"].transpose(0, 2, 1, 3).reshape(SB, WIN, G, DH)
    win_s = np.concatenate([np.stack([old_k, old_v], 2)[:, SQ:], win[PT:].reshape(SB, SQ, 2, G, DH)], 1)
    return (y[None, :PT], y[PT:].reshape(SB, SQ, D),
            res["state_p"].transpose(0, 2, 1, 3).reshape(1, 1, RH, DK, DV),
            res["state_s"].transpose(1, 0, 3, 2, 4).reshape(1, SB, RH, DK, DV),
            rows[None, :PT], rows[PT:].reshape(SB, SQ, 4, G, DH), win[None, :PT], win_s)
```
